# Optimizing a Trainium2 kernel written in Bass

```python
import math
import jax, jax.numpy as jnp
from jax import lax
import numpy as np

D_MODEL = 1024
BATCH = 1
SEQ = 512
DEPTH = 1

POOL_WINDOWS = (2, 4, 8, 16)
POOL_GROUPS = 4
POOL_GROUP_DIM = 128
POOL_WIDTH = POOL_GROUPS * POOL_GROUP_DIM
ATTN_HEADS = 8
ATTN_HEAD_DIM = 128
ATTN_WIDTH = ATTN_HEADS * ATTN_HEAD_DIM
KV_DIM = ATTN_HEAD_DIM
IDX_HEADS = 4
IDX_DIM = 64
TOPK_MAX = 256
Q_BLOCK = 128
N_BUCKETS = 32
MAX_DISTANCE = 128
N_MEM = 256
MEM_HEADS = 4
MEM_HEAD_DIM = 128
MEM_WIDTH = MEM_HEADS * MEM_HEAD_DIM
D_FF = -(-8 * D_MODEL // (3 * 256)) * 256
EPS = 1e-6

IN_SPLITS = (POOL_WIDTH, ATTN_WIDTH, KV_DIM, KV_DIM, IDX_HEADS * IDX_DIM, IDX_DIM, IDX_HEADS, D_MODEL, D_MODEL)
IN_WIDTH = sum(IN_SPLITS)


def _rmsnorm(x, g):
    xf = x.astype(jnp.float32)
    y = xf * lax.rsqrt(jnp.mean(xf * xf, axis=-1, keepdims=True) + EPS)
    return (y * g.astype(jnp.float32)).astype(x.dtype)

def _t5_bucket(dist):
    n = jnp.maximum(dist, 0)
    max_exact = N_BUCKETS // 2
    nf = jnp.maximum(n, 1).astype(jnp.float32)
    large = max_exact + (jnp.log(nf / max_exact) / math.log(MAX_DISTANCE / max_exact)
                         * (N_BUCKETS - max_exact)).astype(jnp.int32)
    large = jnp.minimum(large, N_BUCKETS - 1)
    return jnp.where(n < max_exact, n, large)

def _pool_mixer(u, pool_w, pool_scale):
    B, S, _ = u.shape
    ug = u.reshape(B, S, POOL_GROUPS, POOL_GROUP_DIM).astype(jnp.float32)
    cs = jnp.concatenate([jnp.zeros((B, 1, POOL_GROUPS, POOL_GROUP_DIM), jnp.float32),
                          jnp.cumsum(ug, axis=1)], axis=1)
    win = jnp.array(POOL_WINDOWS, jnp.int32)
    t1 = jnp.arange(1, S + 1, dtype=jnp.int32)[:, None]
    lo = jnp.maximum(t1 - win[None, :], 0)
    cnt = jnp.minimum(t1, win[None, :]).astype(jnp.float32)
    g_idx = jnp.arange(POOL_GROUPS)[None, :]
    mean = (cs[:, 1:] - cs[:, lo, g_idx, :]) / cnt[None, :, :, None]
    pooled = (mean - ug).astype(u.dtype)
    mixed = jnp.einsum('bsgc,gcd->bsgd', pooled, pool_w)
    return mixed.reshape(B, S, POOL_WIDTH) * pool_scale

def _sparse_attention(q, k, v, q_idx, k_idx, w_idx, rel_bias_table):
    B, S = q.shape[:2]
    n_sel = min(TOPK_MAX, S // 4)
    nb = S // Q_BLOCK
    key_pos = jnp.arange(S, dtype=jnp.int32)
    idx_scale = IDX_DIM ** -0.5
    w_scale = IDX_HEADS ** -0.5
    attn_scale = ATTN_HEAD_DIM ** -0.5

    def blockify(a):
        return a.reshape((B, nb, Q_BLOCK) + a.shape[2:]).swapaxes(0, 1)

    def one_block(args):
        qb, qib, wb, start = args
        q_pos = start + jnp.arange(Q_BLOCK, dtype=jnp.int32)
        dots = jnp.einsum('bthd,bsd->bths', qib, k_idx).astype(jnp.float32) * idx_scale
        score = jnp.einsum('bths,bth->bts', jax.nn.relu(dots), wb.astype(jnp.float32) * w_scale)
        causal = key_pos[None, :] <= q_pos[:, None]
        score = jnp.where(causal[None], score, -jnp.inf)
        _, sel = lax.top_k(score, n_sel)
        valid = sel <= q_pos[None, :, None]
        kg = jax.vmap(lambda kb, ib: kb[ib])(k, sel)
        vg = jax.vmap(lambda vb, ib: vb[ib])(v, sel)
        logits = jnp.einsum('bthd,btkd->bhtk', qb, kg).astype(jnp.float32) * attn_scale
        bias = rel_bias_table[_t5_bucket(q_pos[None, :, None] - sel)]
        logits = logits + jnp.moveaxis(bias, -1, 1).astype(jnp.float32)
        logits = jnp.where(valid[:, None], logits, -jnp.inf)
        p = jax.nn.softmax(logits, axis=-1).astype(vg.dtype)
        return jnp.einsum('bhtk,btkd->bthd', p, vg)

    starts = jnp.arange(nb, dtype=jnp.int32) * Q_BLOCK
    out = lax.map(one_block, (blockify(q), blockify(q_idx), blockify(w_idx), starts))
    return out.swapaxes(0, 1).reshape(B, S, ATTN_HEADS * ATTN_HEAD_DIM)

def _mixer_sublayer(h, w_in, pool_w, pool_scale, w_proj_pool, w_proj_attn, rel_bias_table, w_out):
    B, S, _ = h.shape
    proj = h @ w_in
    offs = np.cumsum(IN_SPLITS)[:-1].tolist()
    u_pool, q, k, v, q_idx, k_idx, w_idx, g_pool, g_attn = jnp.split(proj, offs, axis=-1)
    a = _pool_mixer(u_pool, pool_w, pool_scale) @ w_proj_pool
    att = _sparse_attention(q.reshape(B, S, ATTN_HEADS, ATTN_HEAD_DIM), k, v,
                            q_idx.reshape(B, S, IDX_HEADS, IDX_DIM), k_idx, w_idx,
                            rel_bias_table)
    b = att @ w_proj_attn
    merged = jax.nn.sigmoid(g_pool) * a + jax.nn.sigmoid(g_attn) * b
    return merged @ w_out

def _memory_cross_attention(h, mem, norm_mem_kv, w_q_mem, w_kv_mem, w_o_mem):
    B, S, _ = h.shape
    q = (h @ w_q_mem).reshape(B, S, MEM_HEADS, MEM_HEAD_DIM)
    kv = _rmsnorm(mem, norm_mem_kv) @ w_kv_mem
    k, v = jnp.split(kv, 2, axis=-1)
    k = k.reshape(B, N_MEM, MEM_HEADS, MEM_HEAD_DIM)
    v = v.reshape(B, N_MEM, MEM_HEADS, MEM_HEAD_DIM)
    logits = jnp.einsum('bshd,bmhd->bhsm', q, k).astype(jnp.float32) * MEM_HEAD_DIM ** -0.5
    p = jax.nn.softmax(logits, axis=-1).astype(v.dtype)
    o = jnp.einsum('bhsm,bmhd->bshd', p, v).reshape(B, S, MEM_WIDTH)
    return o @ w_o_mem

def _swiglu(h, w_gate_up, w_down):
    g, u = jnp.split(h @ w_gate_up, 2, axis=-1)
    return (jax.nn.silu(g) * u) @ w_down

def first_inputs(seed: int = 0) -> dict:
    key = jax.random.key(seed)
    ks = jax.random.split(key, 24)
    f32 = jnp.float32

    def w(k, shape, fan_in):
        return jax.random.normal(k, shape, f32) * fan_in ** -0.5

    def gain(k, n):
        return 1.0 + 0.02 * jax.random.normal(k, (n,), f32)

    return {
        "x": jax.random.normal(ks[0], (BATCH, SEQ, D_MODEL), f32),
        "mem": jax.random.normal(ks[1], (BATCH, N_MEM, D_MODEL), f32),
        "norm_mix_pre": gain(ks[2], D_MODEL),
        "norm_mix_post": gain(ks[3], D_MODEL),
        "w_in": w(ks[4], (D_MODEL, IN_WIDTH), D_MODEL),
        "pool_w": w(ks[5], (POOL_GROUPS, POOL_GROUP_DIM, POOL_GROUP_DIM), POOL_GROUP_DIM),
        "pool_scale": gain(ks[6], POOL_WIDTH),
        "w_proj_pool": w(ks[7], (POOL_WIDTH, D_MODEL), POOL_WIDTH),
        "w_proj_attn": w(ks[8], (ATTN_WIDTH, D_MODEL), ATTN_WIDTH),
        "rel_bias_table": 0.5 * jax.random.normal(ks[9], (N_BUCKETS, ATTN_HEADS), f32),
        "w_out": w(ks[10], (D_MODEL, D_MODEL), D_MODEL),
        "norm_mem_pre": gain(ks[11], D_MODEL),
        "norm_mem_kv": gain(ks[12], D_MODEL),
        "norm_mem_post": gain(ks[13], D_MODEL),
        "w_q_mem": w(ks[14], (D_MODEL, MEM_WIDTH), D_MODEL),
        "w_kv_mem": w(ks[15], (D_MODEL, 2 * MEM_WIDTH), D_MODEL),
        "w_o_mem": w(ks[16], (MEM_WIDTH, D_MODEL), MEM_WIDTH),
        "norm_ffn_pre": gain(ks[17], D_MODEL),
        "norm_ffn_post": gain(ks[18], D_MODEL),
        "w_gate_up": w(ks[19], (D_MODEL, 2 * D_FF), D_MODEL),
        "w_down": w(ks[20], (D_FF, D_MODEL), D_FF),
    }

def first_block(x, mem, norm_mix_pre, norm_mix_post, w_in, pool_w, pool_scale, w_proj_pool,
              w_proj_attn, rel_bias_table, w_out, norm_mem_pre, norm_mem_kv, norm_mem_post,
              w_q_mem, w_kv_mem, w_o_mem, norm_ffn_pre, norm_ffn_post, w_gate_up, w_down):
    for _ in range(DEPTH):
        h = _rmsnorm(x, norm_mix_pre)
        x = x + _rmsnorm(_mixer_sublayer(h, w_in, pool_w, pool_scale, w_proj_pool,
                                         w_proj_attn, rel_bias_table, w_out), norm_mix_post)
        h = _rmsnorm(x, norm_mem_pre)
        x = x + _rmsnorm(_memory_cross_attention(h, mem, norm_mem_kv, w_q_mem, w_kv_mem, w_o_mem),
                         norm_mem_post)
        h = _rmsnorm(x, norm_ffn_pre)
        x = x + _rmsnorm(_swiglu(h, w_gate_up, w_down), norm_ffn_post)
    return x


DEPTH_2 = 2

HEAD_DIM = 64
ATTN_WIDTH_2 = D_MODEL
N_Q_HEADS = ATTN_WIDTH_2 // HEAD_DIM
N_KV_HEADS = N_Q_HEADS // 4
Q_PER_KV = N_Q_HEADS // N_KV_HEADS
KV_WIDTH = N_KV_HEADS * HEAD_DIM
WINDOW = 128
ATTN_BLOCK = 128

D_INNER = D_MODEL
SSM_HEAD_DIM = 64
N_SSM_HEADS = D_INNER // SSM_HEAD_DIM
N_SSM_GROUPS = 2
SSM_HEADS_PER_GROUP = N_SSM_HEADS // N_SSM_GROUPS
D_STATE = 128
CONV_WIDTH = 4
CHUNK = 128
CONV_CH = D_INNER + 2 * N_SSM_GROUPS * D_STATE

MIX_WIDTH = ATTN_WIDTH_2 + D_INNER
IN_SPLITS_2 = tuple(int(s) for s in np.cumsum([ATTN_WIDTH_2, KV_WIDTH, KV_WIDTH, ATTN_WIDTH_2, D_INNER, CONV_CH]))
IN_WIDTH_2 = IN_SPLITS_2[-1] + N_SSM_HEADS

DEEPNORM_ALPHA = (2.0 * DEPTH_2) ** 0.25
DEEPNORM_BETA = (8.0 * DEPTH_2) ** -0.25
LN_EPS = 1e-5
RMS_EPS = 1e-5


def alibi_slopes():
    h = jnp.arange(1, N_Q_HEADS + 1, dtype=jnp.float32)
    return jnp.exp2(-8.0 * h / N_Q_HEADS)

def sliding_window_attention(q, k, v, sinks):
    b, l, _ = q.shape
    nb = l // ATTN_BLOCK
    q = q.reshape(b, nb, ATTN_BLOCK, N_KV_HEADS, Q_PER_KV, HEAD_DIM)

    def band(t):
        t = t.reshape(b, l, N_KV_HEADS, HEAD_DIM)
        t = jnp.pad(t, ((0, 0), (ATTN_BLOCK, 0), (0, 0), (0, 0)))
        t = t.reshape(b, nb + 1, ATTN_BLOCK, N_KV_HEADS, HEAD_DIM)
        return jnp.concatenate([t[:, :-1], t[:, 1:]], axis=2)

    kb, vb = band(k), band(v)
    scores = jnp.einsum("bnqkgd,bnskd->bnkgqs", q, kb).astype(jnp.float32) * (HEAD_DIM ** -0.5)
    qi = jnp.arange(ATTN_BLOCK)[:, None]
    sj = jnp.arange(2 * ATTN_BLOCK)[None, :]
    dist = qi - sj + ATTN_BLOCK
    blk = jnp.arange(nb)[:, None, None]
    valid = (dist >= 0) & (dist < WINDOW) & (blk * ATTN_BLOCK + sj - ATTN_BLOCK >= 0)
    slopes = alibi_slopes().reshape(N_KV_HEADS, Q_PER_KV)[:, :, None, None]
    scores = scores - slopes * dist.astype(jnp.float32)
    scores = jnp.where(valid[None, :, None, None], scores, -jnp.inf)
    sink = sinks.astype(jnp.float32).reshape(N_KV_HEADS, Q_PER_KV)[:, :, None, None]
    m = jnp.maximum(scores.max(axis=-1, keepdims=True), sink)
    p = jnp.exp(scores - m)
    probs = (p / (p.sum(axis=-1, keepdims=True) + jnp.exp(sink - m))).astype(v.dtype)
    out = jnp.einsum("bnkgqs,bnskd->bnqkgd", probs, vb)
    return out.reshape(b, l, ATTN_WIDTH_2)

def causal_depthwise_conv(u, w, bias):
    out = lax.conv_general_dilated(u, w[:, None, :], window_strides=(1,),
                                   padding=[(CONV_WIDTH - 1, 0)],
                                   dimension_numbers=("NWC", "WIO", "NWC"),
                                   feature_group_count=u.shape[-1])
    return out + bias

def exp_segsum(a_cs):
    n = a_cs.shape[-1]
    diff = a_cs[..., :, None] - a_cs[..., None, :]
    mask = jnp.tril(jnp.ones((n, n), dtype=bool))
    return jnp.exp(jnp.where(mask, diff, -jnp.inf))

def ssd_chunked(xs, dt, a, bm, cm):
    b, l, _ = xs.shape
    nc = l // CHUNK
    G, HG, P, N = N_SSM_GROUPS, SSM_HEADS_PER_GROUP, SSM_HEAD_DIM, D_STATE
    xc = xs.reshape(b, nc, CHUNK, G, HG, P)
    dtc = dt.reshape(b, nc, CHUNK, G, HG)
    bc = bm.reshape(b, nc, CHUNK, G, N)
    cc = cm.reshape(b, nc, CHUNK, G, N)
    a_cs = jnp.moveaxis(jnp.cumsum(dtc * a.reshape(G, HG), axis=2), 2, -1)
    xdt = xc * dtc[..., None]
    cb = jnp.einsum("bclgn,bcsgn->bcgls", cc, bc)
    y_diag = jnp.einsum("bcgls,bcghls,bcsghp->bclghp", cb, exp_segsum(a_cs), xdt)
    decay_to_end = jnp.exp(a_cs[..., -1:] - a_cs)
    states = jnp.einsum("bclgn,bcghl,bclghp->bcghpn", bc, decay_to_end, xdt)
    chunk_decay = jnp.exp(a_cs[..., -1])

    def step(carry, inp):
        st, dec = inp
        return carry * dec[..., None, None] + st, carry

    init = jnp.zeros(states.shape[:1] + states.shape[2:], states.dtype)
    _, prev = lax.scan(step, init, (jnp.moveaxis(states, 1, 0), jnp.moveaxis(chunk_decay, 1, 0)))
    prev = jnp.moveaxis(prev, 0, 1)
    y_off = jnp.einsum("bclgn,bcghpn,bcghl->bclghp", cc, prev, jnp.exp(a_cs))
    return (y_diag + y_off).astype(xs.dtype).reshape(b, l, D_INNER)

def gated_rmsnorm(y, z, w):
    b, l, _ = y.shape
    g = (y * jax.nn.silu(z)).astype(jnp.float32).reshape(b, l, N_SSM_GROUPS, D_INNER // N_SSM_GROUPS)
    g = g * lax.rsqrt(jnp.mean(g * g, axis=-1, keepdims=True) + RMS_EPS)
    return (g.reshape(b, l, D_INNER) * w.astype(jnp.float32)).astype(y.dtype)

def layer_norm(x, g, bias):
    xf = x.astype(jnp.float32)
    mu = jnp.mean(xf, axis=-1, keepdims=True)
    var = jnp.mean(jnp.square(xf - mu), axis=-1, keepdims=True)
    return ((xf - mu) * lax.rsqrt(var + LN_EPS) * g + bias).astype(x.dtype)

def hybrid_layer(x, w_in, conv_w, conv_b, dt_bias, a_log, d_skip, ssm_norm_w, sinks, w_out, ln_g, ln_b):
    b, l, _ = x.shape
    proj = jnp.einsum("bld,de->ble", x, w_in)
    q, k, v, z_attn, z_ssm, xbc, dt_raw = jnp.split(proj, IN_SPLITS_2, axis=-1)
    attn = sliding_window_attention(q, k, v, sinks) * jax.nn.silu(z_attn)
    xbc = jax.nn.silu(causal_depthwise_conv(xbc, conv_w, conv_b))
    xs, bm, cm = jnp.split(xbc, [D_INNER, D_INNER + N_SSM_GROUPS * D_STATE], axis=-1)
    dt = jax.nn.softplus(dt_raw.astype(jnp.float32) + dt_bias.astype(jnp.float32))
    a = -jnp.exp(a_log.astype(jnp.float32))
    y = ssd_chunked(xs, dt, a, bm, cm)
    y = y + (xs.reshape(b, l, N_SSM_HEADS, SSM_HEAD_DIM) * d_skip[:, None]).reshape(b, l, D_INNER)
    ssm = gated_rmsnorm(y, z_ssm, ssm_norm_w)
    out = jnp.einsum("ble,ed->bld", jnp.concatenate([attn, ssm], axis=-1), w_out)
    return layer_norm(DEEPNORM_ALPHA * x + out, ln_g, ln_b)

def second_inputs(seed: int = 0) -> dict:
    key = jax.random.key(seed)
    ks = jax.random.split(key, 12)
    f32 = jnp.float32
    x = jax.random.normal(ks[0], (BATCH, SEQ, D_MODEL), f32)
    w_in = jax.random.normal(ks[1], (DEPTH_2, D_MODEL, IN_WIDTH_2), f32) * D_MODEL ** -0.5
    conv_w = jax.random.normal(ks[2], (DEPTH_2, CONV_WIDTH, CONV_CH), f32) * CONV_WIDTH ** -0.5
    conv_b = jax.random.normal(ks[3], (DEPTH_2, CONV_CH), f32) * 0.02
    dt0 = jnp.exp(jax.random.uniform(ks[4], (DEPTH_2, N_SSM_HEADS), f32) * (jnp.log(0.1) - jnp.log(0.001)) + jnp.log(0.001))
    dt_bias = dt0 + jnp.log(-jnp.expm1(-dt0))
    a_log = jnp.log(jax.random.uniform(ks[5], (DEPTH_2, N_SSM_HEADS), f32, 1.0, 16.0))
    d_skip = 1.0 + 0.1 * jax.random.normal(ks[6], (DEPTH_2, N_SSM_HEADS), f32)
    ssm_norm_w = 1.0 + 0.02 * jax.random.normal(ks[7], (DEPTH_2, D_INNER), f32)
    sinks = jax.random.normal(ks[8], (DEPTH_2, N_Q_HEADS), f32)
    w_out = jax.random.normal(ks[9], (DEPTH_2, MIX_WIDTH, D_MODEL), f32) * (MIX_WIDTH ** -0.5 * DEEPNORM_BETA)
    ln_g = 1.0 + 0.02 * jax.random.normal(ks[10], (DEPTH_2, D_MODEL), f32)
    ln_b = 0.02 * jax.random.normal(ks[11], (DEPTH_2, D_MODEL), f32)
    return {"x": x, "w_in": w_in, "conv_w": conv_w, "conv_b": conv_b, "dt_bias": dt_bias,
            "a_log": a_log, "d_skip": d_skip, "ssm_norm_w": ssm_norm_w, "sinks": sinks,
            "w_out": w_out, "ln_g": ln_g, "ln_b": ln_b}

def second_block(x, w_in, conv_w, conv_b, dt_bias, a_log, d_skip, ssm_norm_w, sinks, w_out, ln_g, ln_b):
    h = x
    for i in range(DEPTH_2):
        h = hybrid_layer(h, w_in[i], conv_w[i], conv_b[i], dt_bias[i], a_log[i], d_skip[i],
                         ssm_norm_w[i], sinks[i], w_out[i], ln_g[i], ln_b[i])
    return h


def setup_inputs(seed=0):
    out = dict(first_inputs(seed))
    for name, value in second_inputs(seed + 1).items():
        if name != "x":
            out[name + "_2"] = value
    return out


def reference(
    x, mem, norm_mix_pre, norm_mix_post, w_in, pool_w, pool_scale, w_proj_pool, w_proj_attn,
    rel_bias_table, w_out, norm_mem_pre, norm_mem_kv, norm_mem_post, w_q_mem, w_kv_mem, w_o_mem,
    norm_ffn_pre, norm_ffn_post, w_gate_up, w_down, w_in_2, conv_w_2, conv_b_2, dt_bias_2,
    a_log_2, d_skip_2, ssm_norm_w_2, sinks_2, w_out_2, ln_g_2, ln_b_2,
):
    x = first_block(
        x, mem, norm_mix_pre, norm_mix_post, w_in, pool_w, pool_scale, w_proj_pool, w_proj_attn,
        rel_bias_table, w_out, norm_mem_pre, norm_mem_kv, norm_mem_post, w_q_mem, w_kv_mem,
        w_o_mem, norm_ffn_pre, norm_ffn_post, w_gate_up, w_down,
    )
    return second_block(
        x, w_in_2, conv_w_2, conv_b_2, dt_bias_2, a_log_2, d_skip_2, ssm_norm_w_2, sinks_2,
        w_out_2, ln_g_2, ln_b_2,
    )


_drawn_inputs = setup_inputs


def setup_inputs(seed=0):
    import zlib

    import numpy as np

    out = dict(_drawn_inputs(seed))
    spreads = {}
    factors = {'norm_mix_post': 3.158,
     'pool_scale': 2.955,
     'norm_mem_pre': 3.69,
     'norm_mem_post': 3.562,
     'norm_ffn_pre': 3.335,
     'norm_ffn_post': 4.828,
     'conv_b_2': 7.653,
     'd_skip_2': 3.964,
     'ssm_norm_w_2': 24.552,
     'sinks_2': 4.912}
    for name, (base, spread) in spreads.items():
        noise = np.random.default_rng([zlib.crc32(name.encode()), seed]).standard_normal(out[name].shape)
        drawn = base * np.exp(spread * noise) if base else spread * noise
        out[name] = __import__('jax').numpy.asarray(drawn.astype(out[name].dtype))
    for name, factor in factors.items():
        out[name] = (out[name] * factor).astype(out[name].dtype)
    return out
```

```python
from contextlib import ExitStack

import numpy as np

import concourse.bass as bass
from concourse import mybir

F32 = mybir.dt.float32
F32R = mybir.dt.float32r
I32 = mybir.dt.int32
ALU = mybir.AluOpType
ACT = mybir.ActivationFunctionType
AX = mybir.AxisListType.X
ENG = mybir.EngineType

P = 128
T = 512
NT = T // P
D = 1024
KD = D // P
BLOCKS = 8
RING = 4
KB = 1024
EPS1 = 1e-6
EPS2 = 1e-5
NEG = -1e30
TAKEN = -3e38
TOPK = 128
ALPHA = 4.0 ** 0.25
POOL_WINDOWS = (2, 4, 8, 16)
D_FF = 2816
KF = D_FF // P

C_ID, C_ONE, C_CAUS, C_TRIL, C_DIST, C_HOT, C_INV, C_SLOPE = 0, 128, 256, 384, 512, 768, 1152, 1216
C_N = 1232
(Q_MIXPRE, Q_MIXPOST, Q_MEMPRE, Q_MEMKV, Q_MEMPOST, Q_FFNPRE, Q_FFNPOST, Q_PSCALE, Q_TAB) = \
    (0, 8, 16, 24, 32, 40, 48, 56, 60)
Q_N = 68
L_CW, L_CB, L_SKIP, L_NORM, L_LNG, L_LNB, L_SINK, L_DTB, L_ALOG, L_N = 0, 48, 60, 68, 76, 84, 92, 108, 109, 110


class Mark:

    def __init__(self, sem, value, steps=()):
        self.sem, self.value, self.steps = sem, value, steps


class Counter:
    def __init__(self, sem, value):
        self.sem, self.value = sem, value


class Program:

    def __init__(self, nc):
        self.nc = nc
        self.dry = False
        self.loops = []
        self.counters = {}
        self.users = {}
        self.fixed = {"blocks": 0, "tiles": 0}

    def counter(self, name, sem, value):
        self.counters[name] = Counter(sem, value)
        return self.counters[name]

    def mark(self, c):
        return Mark(c.sem, c.value, tuple((l, l.steps[c.sem.name]) for l in self.loops))

    def row(self, t, j):
        return t[:, bass.ds(j, 1), :].rearrange("p a t -> p (a t)")

    def loop(self, n, body):
        first = {k: c.value for k, c in self.counters.items()}
        held = {k: list(v) for k, v in self.users.items()}
        was = self.dry
        self.dry = True
        fixed = dict(self.fixed)
        body(0)
        self.dry = was
        loop = Loop(n)
        for k, c in self.counters.items():
            loop.steps[c.sem.name] = c.value - first[k]
        start = {c.sem.name: first[k] for k, c in self.counters.items()}
        last = self.users
        if not self.dry:
            for k, c in self.counters.items():
                c.value = first[k]
            self.users = {}
            for k, marks in last.items():
                back = [Mark(m.sem, m.value - loop.steps[m.sem.name],
                             m.steps + ((loop, loop.steps[m.sem.name]),))
                        for m in marks if m.value > start[m.sem.name]]
                self.users[k] = held.get(k, []) + back
            with self.nc.Fori(0, n, engines=(ENG.PE, ENG.Activation, ENG.DVE)) as i:
                loop.i = i
                self.loops.append(loop)
                self.fixed = fixed
                body(i)
                self.loops.pop()
        for k, marks in self.users.items():
            self.users[k] = [self.ended(m, loop, start, n) for m in marks]
        for k, c in self.counters.items():
            c.value = first[k] + n * loop.steps[c.sem.name]

    def ended(self, m, loop, start, n):
        steps = tuple(s for s in m.steps if s[0] is not loop)
        if m.value <= start[m.sem.name] and len(steps) == len(m.steps):
            return m
        return Mark(m.sem, m.value + (n - 1) * loop.steps[m.sem.name], steps)


class Loop:
    def __init__(self, n):
        self.n, self.i, self.steps = n, None, {}


class Queue:

    def __init__(self, prog, engine, counter, gate):
        self.p, self.e, self.c, self.gate_sem = prog, engine, counter, gate

    def wait(self, *marks):
        if self.p.dry:
            return
        for m in marks:
            value = m.value
            for loop, step in m.steps:
                if step:
                    value = loop.i * step + value
            self.e.wait_ge(m.sem, value)

    def gate(self):
        if not self.p.dry and self.p.loops:
            self.e.sem_inc(self.gate_sem, 1)

    def run(self, f, *args, after=(), count=None, quiet=False, gate=False, **kw):
        self.wait(*after)
        if gate and after:
            self.gate()
        c = count or self.c
        if not quiet:
            c.value += 1
        if self.p.dry:
            return self.p.mark(c)
        ins = f(*args, **kw)
        if not quiet:
            ins.then_inc(c.sem, 1)
            return self.p.mark(c)
        return None

    def done(self):
        return self.p.mark(self.c)


def build(nc, ins, out, n_units, stop=None):
    ctx = ExitStack()
    with ctx:
        sem = lambda n: ctx.enter_context(nc.semaphore(n))
        prog = Program(nc)
        users = lambda name: prog.users.get(name, [])

        base = (nc.sbuf_base + 63) // 64 * 64

        def at(name, kb, shape, dt=F32):
            size = 4 * int(np.prod(shape[1:]))
            assert base + kb * KB + size <= nc.sbuf_top, (name, kb, size)
            return nc.alloc_sbuf_tensor_at(name, shape, dt, offset=base + int(kb * KB))

        X = at("X", 0, [P, KD, T])
        RAW = at("RAW", 16, [P, RING, BLOCKS * P])
        WH = at("WH", 32, [P, RING, BLOCKS * P], F32R)
        WL = at("WL", 48, [P, RING, BLOCKS * P], F32R)
        AH = at("AH", 64, [P, KD, T], F32R)
        AL = at("AL", 80, [P, KD, T], F32R)
        SQ = at("SQ", 96, [P, 2, T])
        RSTD = at("RSTD", 100, [P, 2, T])
        CON = at("CON", 104, [P, C_N])
        PAR = at("PAR", 109, [P, Q_N])
        LPARS = at("LPARS", 109.5, [P, 2, L_N])
        LP = at("LP", 110.5, [P, L_N])
        ST = at("ST", 111, [P, 64])
        ONES = at("ONES", 111.25, [P, 8])
        Z = 111.5
        con = lambda c, n: CON[:, c:c + n]
        IDENT = con(C_ID, P)

        psum = [ctx.enter_context(nc.psum_tensor(f"bank{b}", [P, T], F32)) for b in range(8)]

        PEC = prog.counter("pe", sem("s_pe"), 64)
        ACC = prog.counter("act", sem("s_act"), 64)
        DVC = prog.counter("dve", sem("s_dve"), 64)
        UNC = prog.counter("unit", sem("s_unit_read"), RING)
        s_split = sem("s_unit_split")
        s_hi = sem("s_unit_hi")
        s_raw = [sem(f"s_unit_loaded{j}") for j in range(RING)]
        s_ones = sem("s_ones")
        s_in = {n: sem(f"s_in_{n}") for n in ("x", "con", "par", "lp", "mem", "row0", "row1", "strip")}
        s_out = sem("s_out")
        pe = Queue(prog, nc.tensor, PEC, sem("s_pe_gate"))
        act = Queue(prog, nc.scalar, ACC, sem("s_act_gate"))
        dve = Queue(prog, nc.vector, DVC, sem("s_dve_gate"))
        for q in (pe, act, dve):
            q.e.sem_inc(q.c.sem, 64)
        pe.e.sem_inc(UNC.sem, RING)
        loaded = lambda n, v=16: Mark(s_in[n], v)

        nc.scalar.dma_start(X[:, :, :], ins["x"]).then_inc(s_in["x"], 16)
        nc.scalar.dma_start(CON[:, :], ins["con"]).then_inc(s_in["con"], 16)
        nc.scalar.dma_start(PAR[:, :], ins["par"]).then_inc(s_in["par"], 16)
        nc.scalar.dma_start(LPARS[:, :, :], ins["lpar"]).then_inc(s_in["lp"], 16)
        for q in (pe, act, dve):
            q.wait(loaded("x"), loaded("con"), loaded("par"), loaded("lp"))

        WS = ins["ws"]
        nc.gpsimd.memset(ONES[:, :], 1.0).then_inc(s_ones, 1)
        nc.gpsimd.wait_ge(s_ones, 1)
        nc.gpsimd.sem_inc(s_split, RING)
        with nc.sync.Fori(0, n_units // RING) as i:
            for j in range(RING):
                nc.sync.wait_ge(s_split, i * RING + (j + 1))
                nc.sync.dma_start(RAW[:, j, :], WS[i * RING + j]).then_inc(s_raw[j], 16)
        with nc.gpsimd.Fori(0, n_units // RING) as i:
            for j in range(RING):
                nc.gpsimd.wait_ge(s_raw[j], i * 16 + 16)
                nc.gpsimd.wait_ge(UNC.sem, i * RING + (j + 1))
                nc.gpsimd.tensor_tensor(WH[:, j, :], RAW[:, j, :], ONES[:, 0:1].to_broadcast([P, BLOCKS * P]),
                                        ALU.mult).then_inc(s_hi, 1)
                nc.gpsimd.wait_ge(s_hi, i * RING + (j + 1))
                nc.gpsimd.tensor_tensor(WL[:, j, :], RAW[:, j, :], WH[:, j, :].bitcast(F32),
                                        ALU.subtract).then_inc(s_split, 1)

        V, S, PE = nc.vector, nc.scalar, nc.tensor
        row = prog.row

        def tt(o, a, b, op, after=(), **k):
            return dve.run(V.tensor_tensor, o, a, b, op, after=after, **k)

        def ts(o, a, s1, op0, s2=None, op1=ALU.bypass, after=(), **k):
            return dve.run(V.tensor_scalar, o, a, s1, s2, op0, op1, after=after, **k)

        def stt(o, a, s, b, op0, op1, after=(), **k):
            return dve.run(V.scalar_tensor_tensor, after=after, out=o, in0=a, scalar=s, in1=b, op0=op0, op1=op1, **k)

        def vcopy(o, a, after=(), **k):
            return dve.run(V.tensor_copy, o, a, after=after, **k)

        def actf(o, a, f=ACT.Copy, after=(), **k):
            return act.run(S.activation, o, a, f, after=after, **k)

        def mm(o, l, r, start, stop, last=False, after=(), count=None):
            return pe.run(PE.matmul, o, l, r, start=start, stop=stop, after=after, quiet=not last, count=count,
                          skip_group_check=True)

        def transpose(o, a, after=(), last=False):
            k = a.shape[0]
            return pe.run(PE.transpose, o, a, IDENT[0:k, 0:k], after=after, quiet=not last, gate=k < P)

        def split(hi, lo, src, scale, after):
            h = actf(hi, src, ACT.Copy, scale=scale, after=after)
            return stt(lo, src, scale, hi.bitcast(F32), ALU.mult, ALU.subtract, after=[h, *after])

        def fence():
            marks = [*(q.done() for q in (pe, act, dve)), prog.mark(UNC)]
            for q in (pe, act, dve):
                q.wait(*marks)
                q.gate()
            prog.users.clear()

        def product(o, hi, lo, nk, need=(), cols=P, more=False, marks=None):
            pe.wait(*need)
            mark = None
            for k in range(nk):
                pos = prog.fixed["blocks"]
                slot, b = pos // BLOCKS % RING, pos % BLOCKS
                if b == 0:
                    now = prog.mark(UNC)
                    pe.wait(Mark(s_split, now.value + 1, now.steps))
                if marks is not None:
                    pe.wait(*marks[k])
                w = slice(b * P, b * P + cols)
                end = b == BLOCKS - 1 or (k == nk - 1 and not more)
                mm(o, WH[:, slot, w], hi(k), k == 0, False)
                mm(o, WH[:, slot, w], lo(k), False, False)
                mark = mm(o, WL[:, slot, w], hi(k), False, k == nk - 1, last=end or k == nk - 1,
                          count=UNC if end else None)
                prog.fixed["blocks"] = (pos // BLOCKS + 1) * BLOCKS if end else pos + 1
            return mark

        def gbank():
            prog.fixed["tiles"] += 1
            return prog.fixed["tiles"] % 2

        def dense(hi, lo, nk, need=(), n=T, cols=P, more=False, marks=None):
            b = gbank()
            o = psum[b][0:cols, 0:n]
            m = product(o, hi, lo, nk, need=[*need, *users(b)], cols=cols, more=more, marks=marks)
            return b, o, m

        A_hi = lambda k: AH[:, k, :]
        A_lo = lambda k: AL[:, k, :]

        def square_sum(k, n, src, after, bank=7, nt=NT, first=None, div=D):
            s = k % 2
            w = nt * P
            m = actf(SQ[:, s, 0:w], src, ACT.Square, after=[*after, *users(f"sq{s}")])
            for q in range(nt):
                r = mm(psum[bank][:, q:q + 1], SQ[:, s, q * P:(q + 1) * P], ONEC, k == 0 and q == 0,
                       k == n - 1, last=q == nt - 1, after=[m, *(users(bank) if k == 0 else [])] if q == 0 else [])
            prog.users[f"sq{s}"] = [r]
            return r

        ONEC = CON[:, C_ONE:C_ONE + 1]

        def inverse_root(v, r, n, after):
            t = ST[:, 40:40 + n]
            m = ts(r.bitcast(I32), v.bitcast(I32), 1, ALU.logical_shift_right, after=after)
            m = ts(r.bitcast(I32), r.bitcast(I32), -1.0, ALU.mult, 1597463007.0, ALU.add, after=[m])
            for _ in range(4):
                m = tt(t, r, r, ALU.mult, after=[m])
                m = tt(t, t, v, ALU.mult, after=[m])
                m = ts(t, t, -0.5, ALU.mult, 1.5, ALU.add, after=[m])
                m = tt(r, r, t, ALU.mult, after=[m])
            return m

        def spread(slot, rs, after, nt=NT, bank=6):
            d = SQ[:, 1, 0:nt * P]
            for q in range(nt):
                m = ts(d[:, q * P:(q + 1) * P], IDENT, rs[:, q:q + 1], ALU.mult,
                       after=[*after, *users("sq1")] if q == 0 else [])
            w = mm(psum[bank][:, 0:nt * P], CON[:, C_ONE:C_ONE + P], d, True, True, last=True, after=[m, *users(bank)])
            prog.users["sq1"] = [w]
            r = actf(RSTD[:, slot, 0:nt * P], psum[bank][:, 0:nt * P], ACT.Copy, after=[w, *users(f"rstd{slot}")])
            prog.users[bank] = [r]
            return r

        def norm_scale(slot, after, eps, scale=1.0 / D, nt=NT, bank=7):
            v, r = ST[:, 32:32 + nt], ST[:, 36:36 + nt]
            m = ts(v, psum[bank][:, 0:nt], scale, ALU.mult, eps, ALU.add, after=after)
            prog.users[bank] = [m]
            m = inverse_root(v, r, nt, [m])
            return spread(slot, r, [m], nt)

        def store_out(after):
            nc.scalar.wait_ge(after.sem, after.value)
            nc.scalar.dma_start(out, X[:, :, :]).then_inc(s_out, 16)
            nc.scalar.wait_ge(s_out, 16)

        col = lambda base_, k: PAR[:, base_ + k:base_ + k + 1]
        kT = at("kT", Z + 0, [P, T])
        vTM = at("vTM", Z + 2, [P, NT, P])
        MSK = at("MSK", Z + 4, [P, 1280])
        STRIP = at("STRIP", Z + 9, [P, 8, 256])
        G = at("G", Z + 17, [P, KD, T])
        BH = at("BH", Z + 33, [P, KD, T], F32R)
        BL = at("BL", Z + 49, [P, KD, T], F32R)
        vF = at("vF", Z + 65, [P, T])
        qI = at("qI", Z + 67, [P, 2, T])
        kI = at("kI", Z + 71, [P, T])
        SC = at("SC", Z + 73, [P, T])
        RL = at("RL", Z + 75, [P, 2, T])
        wTM = at("wTM", Z + 79, [P, NT * 4])
        T8 = at("T8", Z + 79.25, [P, 8])
        UP = at("UP", Z + 80, [P, 3, T + 16])
        ROW = at("ROW", Z + 87, [P, 2, 384])
        qC = at("qC", Z + 65, [P, 2, T])
        PR = at("PR", Z + 69, [P, 2, 1280])
        PT = at("PT", Z + 79, [P, 2, 1280])
        mOFF = [0, 128, 384, 768]
        kOFF = [0, 512, 1024, 896]

        amark = []
        for k in range(KD):
            amark.append([split(A_hi(k), A_lo(k), X[:, k, :], col(Q_MIXPRE, k), [])])
        for k in range(KD):
            sq = square_sum(k, KD, X[:, k, :], [])
        rstd = norm_scale(0, [sq], EPS1)
        R0 = RSTD[:, 0, :]

        def scaled(dst, b, o, m, extra=()):
            r = tt(dst, o, R0[0:o.shape[0], :], ALU.mult, after=[m, rstd, *extra])
            prog.users[b] = [r]
            return r

        b, o, m = dense(A_hi, A_lo, KD, marks=amark)
        k_ready = scaled(kT[:, :], b, o, m)
        b, o, m = dense(A_hi, A_lo, KD)
        v_f = scaled(vF[:, :], b, o, m)
        b, o, m = dense(A_hi, A_lo, KD, cols=68)
        ki_w = scaled(kI[0:68, :], b, o, m)
        for q in range(NT):
            w = pe.run(PE.transpose, psum[2][:, q * 4:q * 4 + 4], kI[64:68, q * P:(q + 1) * P],
                       IDENT[64:68, 64:68], after=[ki_w], quiet=q < NT - 1)
        w_ready = ts(wTM[:, :], psum[2][:, 0:16], 1.0 / 16, ALU.mult, after=[w])
        ki_ready = vcopy(kI[64:128, :], kI[0:64, :], after=[w])
        prog.users[2] = [w_ready]
        for q in range(NT):
            w = transpose(psum[3][:, q * P:(q + 1) * P], vF[:, q * P:(q + 1) * P], after=[v_f], last=q == NT - 1)
        v_ready = actf(vTM[:, :, :].rearrange("p a b -> p (a b)"), psum[3][:, :], after=[w])
        prog.users[3] = [v_ready]
        for j in range(2):
            b, o, m = dense(A_hi, A_lo, KD)
            qi_ready = scaled(qI[:, j, :], b, o, m)

        table = PAR[0:32, Q_TAB:Q_TAB + 8]
        SCR = ins["scratch"]
        for h in range(8):
            s = h % 2
            w = mm(psum[4 + s][:, 0:384], table[:, h:h + 1].to_broadcast([32, P]), CON[0:32, C_HOT:C_HOT + 384],
                   True, True, last=True, after=users(4 + s))
            r = actf(ROW[:, s, :], psum[4 + s][:, 0:384], after=[w] + ([loaded(f"row{s}", 16 * (h // 2))] if h > 1 else []))
            prog.users[4 + s] = [r]
            act.wait(r)
            nc.scalar.dma_start(SCR[h], ROW[:, s, :]).then_inc(s_in[f"row{s}"], 16)
        act.wait(loaded("row0", 64), loaded("row1", 64))
        nc.scalar.dma_start(STRIP[:, :, :], SCR.rearrange("h p c -> h (p c)")[:, 127:127 + P * 383]
                            .rearrange("h (p c) -> p h c", c=383)[:, :, 0:256]).then_inc(s_in["strip"], 16)

        m0 = vcopy(MSK[:, 0:P], con(C_CAUS, P))

        def scores(q):
            keys = (q + 1) * P
            acc = None
            for h in range(4):
                half = slice(64 * (h % 2), 64 * (h % 2) + 64)
                bk = 2 + h % 2
                w = mm(psum[bk][:, 0:keys], qI[half, h // 2, q * P:(q + 1) * P], kI[half, 0:keys], True, True,
                       last=True, after=[qi_ready, ki_ready, *users(bk)])
                r = actf(RL[:, h % 2, 0:keys], psum[bk][:, 0:keys], ACT.Relu, after=[w, *users(f"rl{h % 2}")])
                prog.users[bk] = [r]
                wh = wTM[:, q * 4 + h:q * 4 + h + 1]
                if h == 0:
                    acc = ts(SC[:, 0:keys], RL[:, 0, 0:keys], wh, ALU.mult, after=[r, *users("sc")])
                else:
                    acc = stt(SC[:, 0:keys], RL[:, h % 2, 0:keys], wh, SC[:, 0:keys], ALU.mult, ALU.add, after=[r, acc])
                prog.users[f"rl{h % 2}"] = [acc]
            return tt(SC[:, keys - P:keys], SC[:, keys - P:keys], con(C_CAUS, P), ALU.add, after=[acc])

        def select(q, m):
            keys = (q + 1) * P
            first = dve.done()
            for _ in range(TOPK // 8):
                m = dve.run(V.max, T8[:, :], SC[:, 0:keys], after=[m])
                m = dve.run(V.match_replace, SC[:, 0:keys], T8[:, :], SC[:, 0:keys], TAKEN, after=[m])
            m = ts(MSK[:, mOFF[q]:mOFF[q] + keys], SC[:, 0:keys], -2e38, ALU.is_gt, NEG, ALU.mult, after=[m])
            prog.users["sc"] = [m]
            return m

        s1 = scores(1)
        um = dve.run(V.memset, UP[:, :, 0:16], 0.0)
        U, S0, S1 = (UP[:, j, :] for j in range(3))
        N0, N1 = 16, T + 16
        pooled = []
        for g, win in enumerate(POOL_WINDOWS):
            b, o, m = dense(A_hi, A_lo, KD)
            m = scaled(U[:, N0:N1], b, o, m, [um])
            src, dst, step = U, S0, 1
            while step < win:
                m = tt(dst[:, N0:N1], src[:, N0:N1], src[:, N0 - step:N1 - step], ALU.add, after=[m])
                src, dst, step = dst, (S1 if dst is S0 else S0), step * 2
            inv = CON[:, C_INV + 16 * g:C_INV + 16 * g + 16]
            m1 = tt(dst[:, N0:N0 + 16], src[:, N0:N0 + 16], inv, ALU.mult, after=[m])
            m = stt(src[:, N0:N1], src[:, N0:N1], 1.0 / win, U[:, N0:N1], ALU.mult, ALU.subtract, after=[m1])
            m = tt(src[:, N0:N0 + 16], dst[:, N0:N0 + 16], U[:, N0:N0 + 16], ALU.subtract, after=[m])
            um = split(BH[:, g, :], BL[:, g, :], src[:, N0:N1], 1.0, [m])
            pooled.append([um])
            if g == 0:
                sel = select(1, s1)
                s1 = scores(2)
            if g == 2:
                sel = select(2, s1)
                s1 = scores(3)
        mixed = []
        for g in range(4):
            b, o, m = dense(lambda k: BH[:, g, :], lambda k: BL[:, g, :], 1, need=pooled[g], more=g < 3)
            r = split(BH[:, 4 + g, :], BL[:, 4 + g, :], o, col(Q_PSCALE, g), [m])
            prog.users[b] = [r]
            mixed.append([r])
        sel = select(3, s1)
        for j in range(KD):
            b, o, m = dense(lambda k: BH[:, 4 + k, :], lambda k: BL[:, 4 + k, :], 4, marks=mixed,
                            more=j % 2 == 0)
            r = actf(G[:, j, :], o, after=[m])
            prog.users[b] = [r]
        for q in (pe, act, dve):
            q.wait(loaded("strip"))
        fence()

        SCALE = 128.0 ** -0.5

        def query_tile(s):
            b, o, m = dense(A_hi, A_lo, KD)
            return scaled(qC[:, s, :], b, o, m, users(f"q{s}"))

        def head_logits(h, s, q_ready):
            where = [(2, 0), (3, 0), (2, 128), (4, 0)]
            mx, den = ST[:, 4 * s:4 * s + 4], ST[:, 8 + 4 * s:12 + 4 * s]
            wrote = {}
            for q in (0, 2, 1, 3):
                bk, c = where[q]
                keys = (q + 1) * P
                wrote[bk] = mm(psum[bk][:, c:c + keys], qC[:, s, q * P:(q + 1) * P], kT[:, 0:keys], c == 0, True,
                               last=True, after=[q_ready, *users(bk)] if c == 0 else [])
            for q in (0, 2, 1, 3):
                bk, c = where[q]
                keys = (q + 1) * P
                pr = PR[:, s, mOFF[q]:mOFF[q] + keys]
                m = stt(pr, psum[bk][:, c:c + keys], SCALE, MSK[:, mOFF[q]:mOFF[q] + keys], ALU.mult, ALU.add,
                        after=[wrote[bk], *users(f"pr{s}")])
                if q != 0:
                    near = slice(mOFF[q] + keys - 256, mOFF[q] + keys)
                    m = tt(PR[:, s, near], PR[:, s, near], row(STRIP, h), ALU.add, after=[m])
                else:
                    m = tt(PR[:, s, 0:P], PR[:, s, 0:P], row(STRIP, h)[:, P:256], ALU.add, after=[m])
                m = dve.run(V.tensor_reduce, mx[:, q:q + 1], pr, AX, ALU.max, negate=True, after=[m])
                if q:
                    prog.users[bk] = [m]
                e = actf(pr, pr, ACT.Exp, bias=mx[:, q:q + 1], accum_out=den[:, q:q + 1], after=[m])
            m = dve.run(V.reciprocal, den, den, after=[e])
            for q in range(NT):
                pr = PR[:, s, mOFF[q]:mOFF[q] + (q + 1) * P]
                m = ts(pr, pr, den[:, q:q + 1], ALU.mult, after=[m])
            prog.users[f"q{s}"] = [wrote[4]]
            return m

        def head_turn(s, p_ready):
            copies = []
            for bk, tiles in ((5, (0,)), (6, (1, 3)), (7, (2,))):
                c = 0
                for b in tiles:
                    for q in range(b, NT):
                        w = transpose(psum[bk][:, c:c + P], PR[:, s, mOFF[q] + b * P:mOFF[q] + (b + 1) * P],
                                      after=[p_ready, *users(bk)] if c == 0 else [], last=b == tiles[-1] and q == NT - 1)
                        c += P
                at_ = kOFF[tiles[0]]
                copy = vcopy if bk == 6 else actf
                copies.append(copy(PT[:, s, at_:at_ + c], psum[bk][:, 0:c], after=[w, *users(f"pt{s}")]))
                prog.users[bk] = [copies[-1]]
            prog.users[f"pr{s}"] = [w]
            return copies

        def head_values(h, s, pt):
            for b in range(NT):
                w = mm(psum[3][:, b * P:T], vTM[:, b, :], PT[:, s, kOFF[b]:kOFF[b] + T - b * P], b == 0, b == NT - 1,
                       last=b == NT - 1, after=[*pt, *users(3)] if b == 0 else [])
            prog.users[f"pt{s}"] = [w]
            r = split(row(BH, h), row(BL, h), psum[3][:, :], 1.0, [w])
            prog.users[3] = [r]
            prog.users["att_r"] = [r]

        def pool_gate(j):
            s = 0
            b, o, m = dense(A_hi, A_lo, KD)
            m = tt(SQ[:, s, :], o, R0, ALU.mult, after=[m, *users("sq0")])
            prog.users[b] = [m]
            m = actf(SQ[:, s, :], SQ[:, s, :], ACT.Tanh, scale=0.5, after=[m])
            g = row(G, j)
            m = stt(g, SQ[:, s, :], 1.0, g, ALU.add, ALU.mult, after=[m])
            prog.users["sq0"] = [m]

        def two_heads(i):
            h0, h1 = i * 2, i * 2 + 1
            q0 = query_tile(0)
            p0 = head_logits(h0, 0, q0)
            q1 = query_tile(1)
            t0 = head_turn(0, p0)
            p1 = head_logits(h1, 1, q1)
            pool_gate(h0)
            head_values(h0, 0, t0)
            t1 = head_turn(1, p1)
            pool_gate(h1)
            head_values(h1, 1, t1)

        prog.loop(4, two_heads)
        att_ready = users("att_r")
        B_hi = lambda k: BH[:, k, :]
        B_lo = lambda k: BL[:, k, :]

        def merge(j, after):
            b, o, m = dense(A_hi, A_lo, KD)
            m = tt(SQ[:, 0, :], o, R0, ALU.mult, after=[m, *users("sq0")])
            prog.users[b] = [m]
            t_m = actf(SQ[:, 0, :], SQ[:, 0, :], ACT.Tanh, scale=0.5, after=[m])
            b, o, m = dense(B_hi, B_lo, KD, need=after)
            m = stt(SQ[:, 0, :], SQ[:, 0, :], 1.0, o, ALU.add, ALU.mult, after=[m, t_m])
            prog.users[b] = [m]
            g = row(G, j)
            m = tt(g, g, SQ[:, 0, :], ALU.add, after=[m])
            prog.users["sq0"] = [m]
            prog.users["g"] = [m]

        def merge_two(i):
            merge(i * 2, att_ready)
            merge(i * 2 + 1, att_ready)

        prog.loop(4, merge_two)
        g_ready = users("g") + [prog.mark(UNC)]


        def project(hi, lo, nk, marks, Y, need=()):
            for j in range(KD):
                b, o, m = dense(hi, lo, nk, marks=marks if j == 0 else None, need=need)
                r = actf(Y[:, j, :], o, after=[m])
                prog.users[b] = [r]
                s = square_sum(j, KD, Y[:, j, :], [r])
            return s

        def residual(Y, gain, next_gain, rs, a_free, nxt=True):
            marks = []
            xs = []
            for k in range(KD):
                m = stt(Y[:, k, :], Y[:, k, :], col(gain, k), RSTD[:, 1, :], ALU.mult, ALU.mult, after=[rs])
                m = tt(X[:, k, :], X[:, k, :], Y[:, k, :], ALU.add, after=[m])
                xs.append(m)
                if next_gain is not None:
                    marks.append([split(A_hi(k), A_lo(k), X[:, k, :], next_gain(k), [m, *a_free])])
            prog.users["rstd1"] = [xs[-1]]
            return marks, xs

        amark = [[split(A_hi(k), A_lo(k), G[:, k, :], 0.5, g_ready)] for k in range(KD)]
        memX = at("memX", Z + 65, [P, KD, 256])
        MH = at("MH", Z + 33, [P, KD, 256], F32R)
        ML = at("ML", Z + 41, [P, KD, 256], F32R)
        kM = at("kM", Z + 0, [P, 4, 256])
        vM = at("vM", Z + 4, [P, 2, T])
        qM = at("qM", Z + 8, [P, 2, T])
        PM = at("PM", Z + 57, [P, 2, 4 * 256])
        PMT = at("PMT", Z + 65, [P, 2, 2 * T])
        MAH = at("MAH", Z + 73, [P, 4, T], F32R)
        MAL = at("MAL", Z + 81, [P, 4, T], F32R)
        NM = 256
        act.wait(*att_ready, *users("pt0"), *users("pt1"))
        nc.scalar.dma_start(memX[:, :, :], ins["mem"]).then_inc(s_in["mem"], 16)
        act.wait(*g_ready)
        dve.wait(*g_ready)
        mm_marks = [[split(MH[:, k, :], ML[:, k, :], memX[:, k, :], col(Q_MEMKV, k), [loaded("mem")])] for k in range(KD)]
        for k in range(KD):
            sq = square_sum(k, KD, memX[:, k, :], [loaded("mem")], nt=2)
        v2, r2 = ST[:, 32:34], ST[:, 36:38]
        m = ts(v2, psum[7][:, 0:2], 1.0 / D, ALU.mult, EPS1, ALU.add, after=[sq])
        prog.users[7] = [m]
        mem_r = inverse_root(v2, ST[:, 48:50], 2, [m])
        mem_rstd = spread(0, ST[:, 48:50], [mem_r], nt=2)

        Y = G
        sq = project(A_hi, A_lo, KD, amark, Y, need=amark[-1])
        rs = norm_scale(1, [sq], EPS1)

        amark, xmark = residual(Y, Q_MIXPOST, lambda k: col(Q_MEMPRE, k), rs, [prog.mark(UNC)])
        for j in range(4):
            b, o, m = dense(lambda k: MH[:, k, :], lambda k: ML[:, k, :], KD, n=NM, marks=mm_marks)
            r = tt(kM[:, j, :], o, RSTD[:, 0, 0:NM], ALU.mult, after=[m, mem_rstd])
            prog.users[b] = [r]
        km_ready = r
        prog.users["rstd0"] = [r]
        vb = [2, 3]
        for u in range(4):
            pos = prog.fixed["blocks"]
            slot = pos // BLOCKS % RING
            now = prog.mark(UNC)
            pe.wait(Mark(s_split, now.value + 1, now.steps))
            for kk in range(2):
                k = 2 * u + kk
                for t in range(2):
                    o = psum[vb[t]][:, :]
                    tk = slice(t * P, (t + 1) * P)
                    wsl = slice(kk * T, (kk + 1) * T)
                    mm(o, MH[:, k, tk], WH[:, slot, wsl], k == 0, False)
                    mm(o, MH[:, k, tk], WL[:, slot, wsl], False, False)
                    last = kk == 1 and t == 1
                    m = mm(o, ML[:, k, tk], WH[:, slot, wsl], False, k == KD - 1, last=last, count=UNC if last else None)
            prog.fixed["blocks"] += BLOCKS
        for t in range(2):
            vm_ready = ts(vM[:, t, :], psum[vb[t]][:, :], ST[:, 48 + t:49 + t], ALU.mult, after=[m, mem_r])
            prog.users[vb[t]] = [vm_ready]
        for k in range(KD):
            sq = square_sum(k, KD, X[:, k, :], [xmark[k]])
        rstd = norm_scale(0, [sq], EPS1)

        MSCALE = 128.0 ** -0.5

        def mem_logits(h, s, q_ready):
            mx, den = ST[:, 4 * s:4 * s + 4], ST[:, 8 + 4 * s:12 + 4 * s]
            for q in range(NT):
                bk = 2 + q // 2
                w = mm(psum[bk][:, (q % 2) * NM:(q % 2 + 1) * NM], qM[:, s, q * P:(q + 1) * P], kM[:, h, :],
                       q % 2 == 0, True, last=True, after=[q_ready, km_ready, *users(bk)] if q % 2 == 0 else [])
                if q % 2:
                    m = dve.run(V.tensor_reduce, mx[:, q - 1:q + 1],
                                psum[bk][:, :].rearrange("p (a b) -> p a b", a=2), AX, ALU.max, negate=True, after=[w])
            prog.users[f"qm{s}"] = [w]
            m = ts(mx, mx, MSCALE, ALU.mult, after=[m])
            for q in range(NT):
                bk = 2 + q // 2
                e = actf(PM[:, s, q * NM:(q + 1) * NM], psum[bk][:, (q % 2) * NM:(q % 2 + 1) * NM], ACT.Exp, scale=MSCALE,
                         bias=mx[:, q:q + 1], accum_out=den[:, q:q + 1], after=[m, *users(f"pm{s}")])
            prog.users[2] = prog.users[3] = [e]
            m = dve.run(V.reciprocal, den, den, after=[e])
            for q in range(NT):
                pr = PM[:, s, q * NM:(q + 1) * NM]
                m = ts(pr, pr, den[:, q:q + 1], ALU.mult, after=[m])
            return m

        def mem_values(h, s, p_ready):
            done = []
            for b in range(2):
                for q in range(NT):
                    w = transpose(psum[4 + b][:, q * P:(q + 1) * P], PM[:, s, q * NM + b * P:q * NM + (b + 1) * P],
                                  after=[p_ready, *users(4 + b)] if q == 0 else [], last=q == NT - 1)
                c = (actf, vcopy)[b](PMT[:, s, b * T:(b + 1) * T], psum[4 + b][:, :], after=[w, *users(f"pmt{s}")])
                prog.users[4 + b] = [c]
                done.append(c)
            prog.users[f"pm{s}"] = [w]
            for b in range(2):
                w = mm(psum[6][:, :], vM[:, b, h * P:(h + 1) * P], PMT[:, s, b * T:(b + 1) * T], b == 0, b == 1,
                       last=b == 1, after=[*done, vm_ready, *users(6)] if b == 0 else [])
            prog.users[f"pmt{s}"] = [w]
            r = split(MAH[:, h, :], MAL[:, h, :], psum[6][:, :], 1.0, [w])
            prog.users[6] = [r]
            return r

        held = None
        mark4 = []
        for h in range(4):
            s = h % 2
            b, o, m = dense(A_hi, A_lo, KD, marks=amark if h == 0 else None)
            q_ready = scaled(qM[:, s, :], b, o, m, users(f"qm{s}"))
            if held is not None:
                mark4.append([mem_values(h - 1, 1 - s, held)])
            held = mem_logits(h, s, q_ready)
        prog.users["rstd0"] = [q_ready]
        mark4.append([mem_values(3, 1, held)])
        Y = G
        for j in range(KD):
            b, o, m = dense(lambda k: MAH[:, k, :], lambda k: MAL[:, k, :], 4, marks=mark4 if j == 0 else None,
                            more=j % 2 == 0)
            r = actf(Y[:, j, :], o, after=[m])
            prog.users[b] = [r]
            sq = square_sum(j, KD, Y[:, j, :], [r])
        rs = norm_scale(1, [sq], EPS1)
        amark, xmark = residual(Y, Q_MEMPOST, lambda k: col(Q_FFNPRE, k), rs, [])
        for k in range(KD):
            sq = square_sum(k, KD, X[:, k, :], [xmark[k]])
        rstd = norm_scale(0, [sq], EPS1)
        fence()

        DH = at("DH", Z + 0, [P, KF, T], F32R)
        DL = at("DL", Z + 44, [P, KF, T], F32R)
        HG = at("HG", Z + 88, [P, 2, T])
        HH = at("HH", Z + 92, [P, T])

        def gate_up(j, s):
            b, o, m = dense(A_hi, A_lo, KD)
            m = tt(HG[:, s, :], o, R0, ALU.mult, after=[m, *users(f"hg{s}")])
            prog.users[b] = [m]
            t_m = actf(SQ[:, s, :], HG[:, s, :], ACT.Tanh, scale=0.5, after=[m, *users(f"sq{s}")])
            m = stt(HG[:, s, :], SQ[:, s, :], 1.0, HG[:, s, :], ALU.add, ALU.mult, after=[t_m])
            prog.users[f"sq{s}"] = [m]
            m = tt(HG[:, s, :], HG[:, s, :], R0, ALU.mult, after=[m])
            b, o, m2 = dense(A_hi, A_lo, KD)
            m = tt(HH[:, :], o, HG[:, s, :], ALU.mult, after=[m, m2, *users("hh")])
            prog.users[b] = prog.users[f"hg{s}"] = [m]
            r = split(row(DH, j), row(DL, j), HH[:, :], 0.5, [m])
            prog.users["hh"] = prog.users["d"] = [r]

        def gate_up_two(i):
            gate_up(i * 2, 0)
            gate_up(i * 2 + 1, 1)

        prog.loop(KF // 2, gate_up_two)
        d_ready = users("d")
        YF = at("YF", 64, [P, KD, T])
        for j in range(KD):
            b, o, m = dense(lambda k: DH[:, k, :], lambda k: DL[:, k, :], KF, need=d_ready)
            r = actf(YF[:, j, :], o, after=[m])
            prog.users[b] = [r]
            sq = square_sum(j, KD, YF[:, j, :], [r])
        rs = norm_scale(1, [sq], EPS1)
        amark, xmark = residual(YF, Q_FFNPOST, lambda k: 1.0, rs, [])
        fence()
        if stop == 1:
            store_out(Mark(DVC.sem, DVC.value))
            return prog.fixed

        kW = at("kW", Z + 0, [P, 2, T])
        vW = at("vW", Z + 4, [P, NT, 256])
        ATT = at("ATT", Z + 8, [P, KD, T])
        XS = at("XS", Z + 24, [P, KD, T])
        OH = at("OH", 64, [P, 2 * KD, T], F32R)
        OL = at("OL", Z + 8, [P, 2 * KD, T], F32R)
        bF = at("bF", Z + 40, [P, 2, T])
        cF = at("cF", Z + 44, [P, 2, T])
        dtF = at("dtF", Z + 48, [P, T])
        acF = at("acF", Z + 50, [P, T])
        TM = at("TM", Z + 52, [P, 6, 64])
        dtT, acT, lastT, endT, chT = (TM[:, j, :] for j in range(5))
        PV = at("PV", Z + 53.5, [P, D])
        qW = at("qW", Z + 59.5, [P, 2, T])
        PW = at("PW", Z + 63.5, [P, 896])
        PWT = at("PWT", Z + 67, [P, 896])
        MX = at("MX", Z + 70.5, [P, 8, P])
        XDT = at("XDT", Z + 74.5, [P, D])
        XDD = at("XDD", Z + 78.5, [P, T])
        Y1 = at("Y1", Z + 80.5, [P, D])
        xC = at("xC", Z + 84.5, [P, KD, P])
        bC = at("bC", Z + 88.5, [P, 2, P])
        cC = at("cC", Z + 89.5, [P, 2, P])
        CBT = at("CBT", Z + 90.5, [P, 2, P])
        bT = at("bT", Z + 91.5, [P, 2, P])
        acC = at("acC", Z + 92.5, [P, P])
        ACV = at("ACV", Z + 57.5, [P, 2, T])
        TCV = at("TCV", Z + 61.5, [P, 2, T])
        vWF = at("vWF", Z + 65.5, [P, 2, T])
        lcol = lambda c, k=0: LP[:, c + k:c + k + 1]

        units_before = prog.fixed["blocks"] // BLOCKS

        def layer(L):
            fence()
            m = vcopy(LP[:, :], row(LPARS, L))
            m = ts(LP[:, L_CW:L_CW + 60], LP[:, L_CW:L_CW + 60], 0.5, ALU.mult, after=[m])
            lp_ready = m

            for j in range(12):
                s = j % 2
                b, o, m = dense(A_hi, A_lo, KD)
                acc = ACV[:, s, :]
                m = ts(acc, o, lcol(L_CW, 4 * j + 3), ALU.mult, lcol(L_CB, j), ALU.add,
                       after=[m, lp_ready, *users(f"acv{s}")])
                for tap in (2, 1, 0):
                    d = 3 - tap
                    m = stt(acc[:, d:T], o[:, 0:T - d], lcol(L_CW, 4 * j + tap), acc[:, d:T], ALU.mult, ALU.add, after=[m])
                prog.users[b] = [m]
                t_m = actf(TCV[:, s, :], acc, ACT.Tanh, after=[m, *users(f"acv{s}")])
                dst = XS[:, j, :] if j < 8 else (bF[:, j - 8, :] if j < 10 else cF[:, j - 10, :])
                m = stt(dst, TCV[:, s, :], 1.0, acc, ALU.add, ALU.mult, after=[t_m])
                prog.users[f"acv{s}"] = [m]
            xbc_ready = m
            b, o, m = dense(A_hi, A_lo, KD, cols=16)
            a16 = ST[0:16, 56:57]
            e = actf(a16, LP[0:16, L_ALOG:L_ALOG + 1], ACT.Exp, after=[lp_ready])
            an = ts(a16, a16, -1.0, ALU.mult, after=[e])
            v, e1, u, t1 = ACV[0:16, 0, :], ACV[0:16, 1, :], TCV[0:16, 0, :], TCV[0:16, 1, :]
            m = ts(v, o, LP[0:16, L_DTB:L_DTB + 1], ALU.add, after=[m, *users("acv0"), *users("acv1")])
            prog.users[b] = [m]
            m = stt(e1, v, -1.0, v, ALU.mult, ALU.max, after=[m])
            m = actf(e1, e1, ACT.Exp, scale=-1.0, after=[m])
            m = ts(u, e1, 1.0, ALU.add, after=[m])
            lg = actf(dtF[0:16, :], u, ACT.Ln, after=[m])
            m = ts(t1, u, -1.0, ALU.add, after=[m])
            m = tt(e1, e1, t1, ALU.subtract, after=[m])
            m = dve.run(V.reciprocal, u, u, after=[m, lg])
            m = tt(e1, e1, u, ALU.mult, after=[m])
            m = tt(e1, e1, dtF[0:16, :], ALU.add, after=[m])
            m = stt(dtF[0:16, :], v, 0.0, e1, ALU.max, ALU.add, after=[m])
            m = ts(ACV[0:16, 0, :], dtF[0:16, :], a16, ALU.mult, after=[m, an])
            for c in range(NT):
                cs = slice(c * P, (c + 1) * P)
                m = dve.run(V.tensor_tensor_scan, acF[0:16, cs], ONES[0:16, 0:1].to_broadcast([16, P]), ACV[0:16, 0, cs],
                            0.0, ALU.mult, ALU.add, after=[m])
            for c in range(NT):
                cs = slice(c * P, (c + 1) * P)
                c16 = slice(16 * c, 16 * c + 16)
                w = transpose(psum[2][:, c16], dtF[0:16, cs], after=[m, *users(2)] if c == 0 else [])
                w = transpose(psum[2][:, 64 + 16 * c:80 + 16 * c], acF[0:16, cs])
                w = mm(psum[2][:, 128 + 16 * c:144 + 16 * c], acF[0:16, (c + 1) * P - 1:(c + 1) * P].to_broadcast([16, P]),
                       IDENT[0:16, 0:16], True, True, last=c == 3)
            r = vcopy(TM[:, 0:3, :], psum[2][:, 0:192].rearrange("p (a b) -> p a b", a=3), after=[w])
            prog.users[2] = [r]
            m = tt(endT, lastT, acT, ALU.subtract, after=[r])
            m = actf(endT, endT, ACT.Exp, after=[m])
            tm_ready = actf(chT, lastT, ACT.Exp, after=[r])
            z0 = dve.run(V.memset, PV[:, :], 0.0)

            for j in range(2):
                b, o, m = dense(A_hi, A_lo, KD)
                kw = actf(kW[:, j, :], o, after=[m])
                prog.users[b] = [kw]
            for j in range(2):
                b, o, m = dense(A_hi, A_lo, KD)
                r = actf(vWF[:, j, :], o, after=[m])
                prog.users[b] = [r]
                for q in range(NT):
                    w = transpose(psum[3 + j][:, q * P:(q + 1) * P], vWF[:, j, q * P:(q + 1) * P],
                                  after=[r, *users(3 + j)] if q == 0 else [], last=q == NT - 1)
                vw = vcopy(vW[:, :, j * P:(j + 1) * P], psum[3 + j][:, :].rearrange("p (a b) -> p a b", a=NT), after=[w])
                prog.users[3 + j] = [vw]
            fence()

            oW = [512, 0, 256, 640]

            def window_head(c, s, hh, q_ready):
                half = slice(64 * hh, 64 * hh + 64)
                hc = (c * 2 + s) * 2 + hh
                kv = lambda c0, c1: kW[half, s, c0:c1]
                for q in (1, 2, 3, 0):
                    bk = 2 if q in (1, 2) else 3
                    at_ = {1: 0, 2: 256, 3: 0, 0: 256}[q]
                    n = 256 if q else P
                    w = mm(psum[bk][:, at_:at_ + n], qW[half, s, q * P:(q + 1) * P], kv((q + 1) * P - n, (q + 1) * P),
                           at_ == 0, True, last=True, after=[q_ready, *users(bk)] if at_ == 0 else [])
                sl = CON[:, bass.ds(hc + C_SLOPE, 1)]
                dist = CON[:, C_DIST:C_DIST + 256].unsqueeze(1).to_broadcast([P, 2, 256])
                m = stt(PW[:, 0:512].rearrange("p (a b) -> p a b", a=2), dist, sl,
                        psum[2][:, :].rearrange("p (a b) -> p a b", a=2), ALU.mult, ALU.add, after=[w, *users("pw")])
                prog.users[2] = [m]
                m = stt(PW[:, 640:896], CON[:, C_DIST:C_DIST + 256], sl, psum[3][:, 0:256], ALU.mult, ALU.add)
                m = stt(PW[:, 512:640], CON[:, C_DIST + P:C_DIST + 256], sl, psum[3][:, 256:384], ALU.mult, ALU.add)
                prog.users[3] = [m]
                mx, den, es = ST[:, 16:20], ST[:, 20:24], ST[:, 24:28]
                pw3 = [PW[:, 512:640], PW[:, 0:256], PW[:, 256:512], PW[:, 640:896]]
                for q in range(NT):
                    m = dve.run(V.tensor_reduce, mx[:, q:q + 1], pw3[q], AX, ALU.max, negate=True, after=[m])
                m = ts(mx, mx, LP[:, bass.ds(hc + L_SINK, 1)], ALU.min, 0.125, ALU.mult, after=[m, nsink])
                for q in range(NT):
                    e = actf(pw3[q], pw3[q], ACT.Exp, scale=0.125, bias=mx[:, q:q + 1], accum_out=den[:, q:q + 1], after=[m])
                e = actf(es, mx, ACT.Exp, bias=SINKB[:, bass.ds(hc, 1)], after=[m])
                m = tt(den, den, es, ALU.add, after=[e])
                m = dve.run(V.reciprocal, den, den, after=[m])
                for q in range(NT):
                    m = ts(pw3[q], pw3[q], den[:, q:q + 1], ALU.mult, after=[m])
                for b in range(NT):
                    bk, c = 4 + b // 2, (b % 2) * 256
                    cur = pw3[b][:, 128:256] if b else pw3[0]
                    w = transpose(psum[bk][:, c:c + P], cur, after=[m, *users(bk)] if c == 0 else [], last=b == 3)
                    if b < 3:
                        w = transpose(psum[bk][:, c + P:c + 256], pw3[b + 1][:, 0:P], last=b == 1)
                    if b == 1:
                        c0 = actf(PWT[:, 0:512], psum[4][:, :], after=[w, *users("pwt")])
                c1 = vcopy(PWT[:, 512:896], psum[5][:, 0:384], after=[w, *users("pwt")])
                prog.users[4], prog.users[5] = [c0], [c1]
                prog.users["pw"] = [w]
                return [c0, c1]

            def window_values(s, hh, pt, bank):
                half = slice(64 * hh, 64 * hh + 64)
                o = psum[bank]
                for q in range(NT):
                    val = lambda b: vW[:, b, s * P + 64 * hh:s * P + 64 * hh + 64]
                    w = mm(o[half, q * P:(q + 1) * P], val(q), PWT[:, q * 256:q * 256 + P], q == 0, q == 0,
                           after=[*pt, *users(bank)] if q == 0 else [])
                    if q:
                        w = mm(o[half, q * P:(q + 1) * P], val(q - 1), PWT[:, (q - 1) * 256 + P:q * 256],
                               False, True, last=True)
                prog.users["pwt"] = [w]
                return w

            SINKB = RSTD[:, 0, 0:16]
            m = vcopy(SINKB, LP[:, L_SINK:L_SINK + 16])
            nsink = ts(LP[:, L_SINK:L_SINK + 16], LP[:, L_SINK:L_SINK + 16], -8.0, ALU.mult, after=[m])
            cum = con(C_TRIL, P)

            def chunk(c):
                ck = bass.ts(c, P)
                c16 = bass.ds(c * 16, 16)
                m = actf(xC[:, :, :], XS[:, :, ck], after=users("xc"))
                m = actf(bC[:, :, :], bF[:, :, ck])
                m = actf(acC[0:16, :], acF[0:16, ck])
                cp = actf(cC[:, :, :], cF[:, :, ck])
                for g in range(2):
                    w = mm(psum[2][:, g * P:(g + 1) * P], bC[:, g, :], cC[:, g, :], True, True,
                           after=[cp, *users(2)] if g == 0 else [])
                for g in range(2):
                    w = transpose(psum[2][:, (2 + g) * P:(3 + g) * P], bC[:, g, :], last=g == 1)
                cb = tt(CBT[:, :, :], psum[2][:, 0:256].rearrange("p (g l) -> p g l", g=2),
                        cum.unsqueeze(1).to_broadcast([P, 2, P]), ALU.mult, after=[w])
                bt = actf(bT[:, :, :].rearrange("p a b -> p (a b)"), psum[2][:, 256:512], after=[w, cb])
                prog.users[2] = [bt]
                for j in range(KD):
                    bk = 3 + j // 4
                    w = transpose(psum[bk][:, (j % 4) * P:(j % 4 + 1) * P], xC[:, j, :],
                                  after=users(bk) if j % 4 == 0 else [], last=j % 4 == 3)
                    if j % 4 == 3:
                        hs = slice((j // 4) * 8, (j // 4) * 8 + 8)
                        xd = tt(XDT[:, (j // 4) * T:(j // 4 + 1) * T].rearrange("p (h d) -> p h d", d=64),
                                psum[bk][:, :].rearrange("p (h d) -> p h d", d=64),
                                dtT[:, bass.ds(c * 16 + (j // 4) * 8, 8)].unsqueeze(2).to_broadcast([P, 8, 64]),
                                ALU.mult, after=[w])
                        prog.users[bk] = [xd]
                for j in range(KD):
                    bk = 5 + j // 4
                    w = mm(psum[bk][:, (j % 4) * P:(j % 4 + 1) * P], PV[:, j * P:(j + 1) * P], cC[:, j // 4, :], j % 4 == 0, True,
                           after=[*users(bk), *users("pv")] if j % 4 == 0 else [], last=j % 4 == 3)
                pv_read = w
                for j in range(KD):
                    bk = 3 + j // 4
                    for hh in range(2):
                        w = mm(psum[bk][64 * hh:64 * hh + 64, (j % 4) * P:(j % 4 + 1) * P],
                               IDENT[0:16, 2 * j + hh:2 * j + hh + 1].to_broadcast([16, 64]), acC[0:16, :], j % 4 == 0,
                               True, after=users(bk) if j % 4 == 0 and hh == 0 else [], last=j % 4 == 3 and hh == 1)
                    if j % 4 == 3:
                        y = Y1[:, (j // 4) * T:(j // 4 + 1) * T]
                        e = actf(y, psum[bk][:, :], ACT.Exp, after=[w])
                        prog.users[bk] = [e]
                        y1 = tt(y, psum[5 + j // 4][:, :], y, ALU.mult, after=[e, pv_read])
                        prog.users[5 + j // 4] = [y1]
                m = tt(PV[:, :].rearrange("p (h d) -> p h d", d=64), PV[:, :].rearrange("p (h d) -> p h d", d=64),
                       chT[:, c16].unsqueeze(2).to_broadcast([P, 16, 64]), ALU.mult, after=[pv_read])
                for g in range(2):
                    xdd = tt(XDD[:, :].rearrange("p (h d) -> p h d", d=64),
                             XDT[:, g * T:(g + 1) * T].rearrange("p (h d) -> p h d", d=64),
                             endT[:, bass.ds(c * 16 + g * 8, 8)].unsqueeze(2).to_broadcast([P, 8, 64]),
                             ALU.mult, after=[xd, *users("xdd")])
                    w = mm(psum[2][:, :], bT[:, g, :], XDD[:, :], True, True, last=True, after=[xdd, bt, *users(2)])
                    prog.users["xdd"] = [w]
                    m = tt(PV[:, g * T:(g + 1) * T], PV[:, g * T:(g + 1) * T], psum[2][:, :], ALU.add, after=[w, m])
                    prog.users[2] = [m]
                prog.users["pv"] = [m]
                for g in range(2):
                    for h4 in range(2):
                        bk = 3 + h4
                        for h in range(4):
                            hd = g * 8 + h4 * 4 + h
                            w = mm(psum[bk][:, h * P:(h + 1) * P], IDENT[0:16, hd:hd + 1].to_broadcast([16, P]), acC[0:16, :],
                                   h == 0, True, after=users(bk) if h == 0 else [], last=h == 3)
                        m = tt(MX[:, h4 * 4:h4 * 4 + 4, :], psum[bk][:, :].rearrange("p (h l) -> p h l", h=4),
                               acT[:, bass.ds(c * 16 + g * 8 + h4 * 4, 4)].unsqueeze(2).to_broadcast([P, 4, P]),
                               ALU.subtract, after=[w, *users("mx")])
                        prog.users[bk] = [m]
                    m = ts(MX[:, :, :], MX[:, :, :], 0.0, ALU.min, after=[m])
                    m = actf(MX[:, :, :], MX[:, :, :], ACT.Exp, after=[m])
                    m = tt(MX[:, :, :], MX[:, :, :], CBT[:, g:g + 1, :].to_broadcast([P, 8, P]), ALU.mult, after=[m, cb])
                    bk = 5 + g
                    for h in range(8):
                        hd = g * 8 + h
                        half = slice(64 * (h % 2), 64 * (h % 2) + 64)
                        w = mm(psum[bk][half, (h // 2) * P:(h // 2 + 1) * P], XDT[:, hd * 64:(hd + 1) * 64], MX[:, h, :],
                               h < 2, True, after=[m, xd, *users(bk)] if h == 0 else [], last=h == 7)
                    prog.users["mx"] = [w]
                    yg = Y1[:, g * T:(g + 1) * T]
                    m = tt(yg, yg, psum[bk][:, :], ALU.add, after=[w, y1])
                    prog.users[bk] = [m]
                    for j in range(4):
                        jj = g * 4 + j
                        m2 = stt(XS[:, jj, ck], xC[:, jj, :], lcol(L_SKIP, jj), yg[:, j * P:(j + 1) * P], ALU.mult, ALU.add,
                                 after=[m] if j == 0 else [])
                prog.users["xc"] = [m2]

            def pair_and_chunk(c):
                for s in range(2):
                    b, o, m = dense(A_hi, A_lo, KD)
                    q_ready = actf(qW[:, s, :], o, after=[m, *users(f"qw{s}")])
                    prog.users[b] = [q_ready]
                    pt = window_head(c, s, 0, q_ready)
                    b2, o2, m2 = dense(A_hi, A_lo, KD)
                    w0 = window_values(s, 0, pt, 6)
                    t_m = actf(SQ[:, 0, :], o2, ACT.Tanh, scale=0.5, after=[m2, *users("sq0")])
                    zs = stt(SQ[:, 1, :], SQ[:, 0, :], 1.0, o2, ALU.add, ALU.mult, after=[t_m, *users("sq1")])
                    prog.users[b2] = prog.users["sq0"] = [zs]
                    pt = window_head(c, s, 1, q_ready)
                    w1 = window_values(s, 1, pt, 6)
                    prog.users[f"qw{s}"] = [w1]
                    m = stt(row(ATT, c * 2 + s), psum[6][:, :], 0.5, SQ[:, 1, :], ALU.mult, ALU.mult,
                            after=[w0, w1, zs])
                    prog.users[6] = prog.users["sq1"] = [m]
                chunk(c)

            prog.loop(NT, pair_and_chunk)
            fence()

            def gate_group(g):
                for j in range(4):
                    b, o, m = dense(A_hi, A_lo, KD)
                    t_m = actf(ACV[:, j % 2, :], o, ACT.Tanh, scale=0.5, after=[m, *users(f"a{j % 2}")])
                    zs = stt(TCV[:, j % 2, :], ACV[:, j % 2, :], 1.0, o, ALU.add, ALU.mult, after=[t_m])
                    prog.users[b] = [zs]
                    y = row(XS, g * 4 + j)
                    m = stt(y, y, 0.5, TCV[:, j % 2, :], ALU.mult, ALU.mult, after=[zs])
                    prog.users[f"a{j % 2}"] = [m]
                    sq = square_sum(j, 4, y, [m])
                r = norm_scale(1, [sq], EPS2, scale=1.0 / 512)
                for j in range(4):
                    y = row(XS, g * 4 + j)
                    m = stt(y, y, LP[:, bass.ds(g * 4 + j + L_NORM, 1)], RSTD[:, 1, :], ALU.mult, ALU.mult, after=[r])
                prog.users["rstd1"] = [m]

            prog.loop(2, gate_group)
            fence()
            omark = []
            for k in range(2 * KD):
                src = ATT[:, k, :] if k < KD else XS[:, k - KD, :]
                omark.append([split(OH[:, k, :], OL[:, k, :], src, 1.0, [])])
            for j in range(KD):
                b, o, m = dense(lambda k: OH[:, k, :], lambda k: OL[:, k, :], 2 * KD, marks=omark if j == 0 else None)
                m = stt(X[:, j, :], X[:, j, :], ALPHA, o, ALU.mult, ALU.add, after=[m])
                prog.users[b] = [m]
                w = mm(psum[6][:, :], CON[:, C_ONE:C_ONE + P], X[:, j, :], j == 0, j == KD - 1, last=True,
                       after=[m, *(users(6) if j == 0 else [])])
            mean = RSTD[:, 0, :]
            mn = actf(mean, psum[6][:, :], scale=1.0 / D, after=[w])
            prog.users[6] = [mn]
            for j in range(KD):
                m = tt(X[:, j, :], X[:, j, :], mean, ALU.subtract, after=[mn])
                sq = square_sum(j, KD, X[:, j, :], [m])
            r = norm_scale(1, [sq], EPS2)
            for j in range(KD):
                m = tt(X[:, j, :], X[:, j, :], RSTD[:, 1, :], ALU.mult, after=[r])
                m = actf(X[:, j, :], X[:, j, :], ACT.Identity, scale=lcol(L_LNG, j), bias=lcol(L_LNB, j), after=[m])
                split(A_hi(j), A_lo(j), X[:, j, :], 1.0, [m])
            prog.users["rstd1"] = [m]
            for _ in range((units_before - prog.fixed["blocks"] // BLOCKS) % RING):
                now = prog.mark(UNC)
                pe.wait(now, Mark(s_split, now.value + 1, now.steps))
                UNC.value += 1
                if not prog.dry:
                    PE.sem_inc(UNC.sem, 1)
                prog.fixed["blocks"] += BLOCKS
            prog.fixed["tiles"] += prog.fixed["tiles"] % 2

        prog.loop(2 if stop is None else 1, layer)
        fence()
        store_out(Mark(DVC.sem, DVC.value))
        assert stop is not None or UNC.value - RING in range(n_units - RING, n_units + 1), (UNC.value, n_units)


def _tiles(w, group=P):
    k, n = w.shape
    return [[w[a:a + P, c:c + P] for a in range(0, k, P)] for c in range(0, n, P)]


def _units(blocks):
    res = []
    for a in range(0, len(blocks), BLOCKS):
        u = np.zeros((P, BLOCKS, P), np.float32)
        for j, b in enumerate(blocks[a:a + BLOCKS]):
            u[:b.shape[0], j, :b.shape[1]] = b
        res.append(u.reshape(P, BLOCKS * P))
    return res


PAIRS = [(8 * t + j, 8 * t + 4 + j) for j in range(4) for t in range(2)]
HEADS = [h for pair in PAIRS for h in pair]


def _stream(w):
    s = []
    win = w["w_in"]
    c = np.cumsum([0, 512, 1024, 128, 128, 256, 64, 4, 1024, 1024])
    cut = lambda m, a, b: m[:, a:b]
    pool, q, k, v, qi, kiw, gp, ga = (cut(win, c[0], c[1]), cut(win, c[1], c[2]), cut(win, c[2], c[3]),
                                     cut(win, c[3], c[4]), cut(win, c[4], c[5]), cut(win, c[5], c[7]),
                                     cut(win, c[7], c[8]), cut(win, c[8], c[9]))
    flat = lambda t: [b for col in t for b in col]
    add = lambda t: s.extend(_units(flat(t)))
    each = lambda t: [s.extend(_units(col)) for col in t]
    for part in (k, v, kiw, qi, pool):
        each(_tiles(part))
    s.extend(_units([w["pool_w"][g] for g in range(4)]))
    add(_tiles(w["w_proj_pool"]))
    tq, tg = _tiles(q), _tiles(gp)
    for i in range(4):
        each([tq[2 * i], tq[2 * i + 1], tg[2 * i], tg[2 * i + 1]])
    ta, tb = _tiles(ga), _tiles(w["w_proj_attn"])
    for i in range(8):
        each([ta[i], tb[i]])
    each(_tiles(w["w_out"]))
    kv = w["w_kv_mem"]
    each(_tiles(kv[:, :512]))
    vm = kv[:, 512:].reshape(4, 2, P, T)
    for u in range(4):
        s.append(np.ascontiguousarray(vm[u].transpose(1, 0, 2)).reshape(P, 2 * T))
    each(_tiles(w["w_q_mem"]))
    add(_tiles(w["w_o_mem"]))
    tg, tu = _tiles(w["w_gate_up"][:, :D_FF]), _tiles(w["w_gate_up"][:, D_FF:])
    for i in range(KF):
        each([tg[i], tu[i]])
    each(_tiles(w["w_down"]))
    first = len(s)
    for L in range(2):
        wi, wo = w["w_in_2"][L], w["w_out_2"][L]
        c = np.cumsum([0, 1024, 256, 256, 1024, 1024, 1536, 16])
        q, k, v, za, zs, xbc, dt = (wi[:, c[j]:c[j + 1]] for j in range(7))
        heads = lambda m: m.reshape(D, 16, 64)[:, HEADS, :].reshape(D, D)
        each(_tiles(xbc))
        each(_tiles(dt))
        each(_tiles(k))
        each(_tiles(v))
        tq, tz = _tiles(heads(q)), _tiles(heads(za))
        for i in range(8):
            each([tq[i], tz[i]])
        each(_tiles(zs))
        wa = wo[:D].reshape(16, 64, D)[HEADS].reshape(D, D)
        each(_tiles(np.concatenate([wa, wo[D:]], axis=0)))
        while (len(s) - first) % RING:
            s.append(np.zeros((P, BLOCKS * P), np.float32))
    while len(s) % RING:
        s.append(np.zeros((P, BLOCKS * P), np.float32))
    return np.stack(s)


def _constants():
    import math
    con = np.zeros((P, C_N), np.float32)
    i, j = np.arange(P)[:, None], np.arange(P)[None, :]
    con[:, C_ID:C_ID + P] = i == j
    con[:, C_ONE:C_ONE + P] = 1.0
    con[:, C_CAUS:C_CAUS + P] = np.where(j > i, NEG, 0.0)
    con[:, C_TRIL:C_TRIL + P] = i <= j
    d = i - np.arange(256)[None, :] + P
    con[:, C_DIST:C_DIST + 256] = np.where((d >= 0) & (d < P), d, 1e30)
    dist = 255 - np.arange(384)
    n = np.maximum(dist, 0)
    large = 16 + (np.log(np.maximum(n, 1).astype(np.float32) / np.float32(16)) / np.float32(math.log(8))
                  * np.float32(16)).astype(np.int32)
    bucket = np.where(n < 16, n, np.minimum(large, 31))
    hot = (np.arange(32)[:, None] == bucket[None, :]).astype(np.float32)
    hot[31] -= 1.0
    con[:32, C_HOT:C_HOT + 384] = hot
    for g, win in enumerate(POOL_WINDOWS):
        con[:, C_INV + 16 * g:C_INV + 16 * g + 16] = 1.0 / np.minimum(np.arange(1, 17), win)
    slope = np.exp2(-8.0 * (np.array(HEADS) + 1) / 16)
    con[:, C_SLOPE:C_SLOPE + 16] = -8.0 * slope
    return con


def _params(w):
    par = np.zeros((P, Q_N), np.float32)
    for c, name in ((Q_MIXPRE, "norm_mix_pre"), (Q_MIXPOST, "norm_mix_post"), (Q_MEMPRE, "norm_mem_pre"),
                    (Q_MEMKV, "norm_mem_kv"), (Q_MEMPOST, "norm_mem_post"), (Q_FFNPRE, "norm_ffn_pre"),
                    (Q_FFNPOST, "norm_ffn_post")):
        par[:, c:c + 8] = w[name].reshape(8, P).T
    par[:, Q_PSCALE:Q_PSCALE + 4] = w["pool_scale"].reshape(4, P).T
    par[:32, Q_TAB:Q_TAB + 8] = w["rel_bias_table"]
    lp = np.zeros((P, 2, L_N), np.float32)
    for L in range(2):
        lp[:, L, L_CW:L_CW + 48] = w["conv_w_2"][L].T.reshape(12, P, 4).transpose(1, 0, 2).reshape(P, 48)
        lp[:, L, L_CB:L_CB + 12] = w["conv_b_2"][L].reshape(12, P).T
        lp[:, L, L_SKIP:L_SKIP + 8] = np.repeat(w["d_skip_2"][L], 64).reshape(8, P).T
        lp[:, L, L_NORM:L_NORM + 8] = w["ssm_norm_w_2"][L].reshape(8, P).T
        lp[:, L, L_LNG:L_LNG + 8] = w["ln_g_2"][L].reshape(8, P).T
        lp[:, L, L_LNB:L_LNB + 8] = w["ln_b_2"][L].reshape(8, P).T
        lp[:, L, L_SINK:L_SINK + 16] = w["sinks_2"][L][HEADS][None, :]
        lp[:16, L, L_DTB] = w["dt_bias_2"][L]
        lp[:16, L, L_ALOG] = w["a_log_2"][L]
    return par, lp


STOP = None


def kernel(**inputs):
    import concourse.bacc as bacc
    from concourse.bass_utils import run_bass_kernel_spmd as run_spmd

    w = {k: np.asarray(v) for k, v in inputs.items()}
    feature_major = lambda a: np.ascontiguousarray(a[0].T.reshape(KD, P, a.shape[1]).transpose(1, 0, 2))
    par, lpar = _params(w)
    arrays = {"ws": _stream(w), "x": feature_major(w["x"]), "mem": feature_major(w["mem"]), "con": _constants(),
              "par": par, "lpar": lpar}
    nc = bacc.Bacc("TRN2", target_bir_lowering=False, num_devices=1)
    ins = {n: nc.dram_tensor(f"{n}_dram", a.shape, F32, kind="ExternalInput").ap() for n, a in arrays.items()}
    ins["scratch"] = nc.dram_tensor("bias_rows", (8, P, 384), F32, kind="Internal").ap()
    out = nc.dram_tensor("out_dram", (P, KD, T), F32, kind="ExternalOutput").ap()
    build(nc, ins, out, {None: arrays["ws"].shape[0], 1: 140, 2: 200}[STOP], STOP)
    r = run_spmd(nc, [{f"{n}_dram": a for n, a in arrays.items()}], core_ids=[0])
    y = np.asarray(r.results[0]["out_dram"])
    return np.ascontiguousarray(y.transpose(1, 0, 2).reshape(D, T).T)[None]
```

```python
from contextlib import ExitStack

import numpy as np

import concourse.bass as bass
from concourse import mybir

F32 = mybir.dt.float32
F32R = mybir.dt.float32r
I32 = mybir.dt.int32
ALU = mybir.AluOpType
ACT = mybir.ActivationFunctionType
AX = mybir.AxisListType.X
ENG = mybir.EngineType

P = 128
T = 512
NT = T // P
D = 1024
KD = D // P
BLOCKS = 8
RING = 4
KB = 1024
EPS1 = 1e-6
EPS2 = 1e-5
NEG = -1e30
TAKEN = -3e38
TOPK = 128
ALPHA = 4.0 ** 0.25
POOL_WINDOWS = (2, 4, 8, 16)
D_FF = 2816
KF = D_FF // P

C_ID, C_ONE, C_CAUS, C_TRIL, C_DIST, C_HOT, C_INV, C_SLOPE = 0, 128, 256, 384, 512, 896, 1280, 1344
C_N = 1360
(Q_MIXPRE, Q_MIXPOST, Q_MEMPRE, Q_MEMKV, Q_MEMPOST, Q_FFNPRE, Q_FFNPOST, Q_PSCALE, Q_TAB) = \
    (0, 8, 16, 24, 32, 40, 48, 56, 60)
Q_N = 68
L_CW, L_CB, L_SKIP, L_NORM, L_LNG, L_LNB, L_SINK, L_DTB, L_ALOG, L_N = 0, 48, 60, 68, 76, 84, 92, 108, 109, 110


class Mark:

    def __init__(self, sem, value, steps=()):
        self.sem, self.value, self.steps = sem, value, steps


class Counter:
    def __init__(self, sem, value):
        self.sem, self.value = sem, value


class Program:

    def __init__(self, nc):
        self.nc = nc
        self.dry = False
        self.loops = []
        self.counters = {}
        self.users = {}
        self.fixed = {"blocks": 0, "tiles": 0}

    def counter(self, name, sem, value):
        self.counters[name] = Counter(sem, value)
        return self.counters[name]

    def mark(self, c):
        return Mark(c.sem, c.value, tuple((l, l.steps[c.sem.name]) for l in self.loops))

    def row(self, t, j):
        return t[:, bass.ds(j, 1), :].rearrange("p a t -> p (a t)")

    def loop(self, n, body):
        first = {k: c.value for k, c in self.counters.items()}
        held = {k: list(v) for k, v in self.users.items()}
        was = self.dry
        self.dry = True
        fixed = dict(self.fixed)
        body(0)
        self.dry = was
        loop = Loop(n)
        for k, c in self.counters.items():
            loop.steps[c.sem.name] = c.value - first[k]
        start = {c.sem.name: first[k] for k, c in self.counters.items()}
        last = self.users
        if not self.dry:
            for k, c in self.counters.items():
                c.value = first[k]
            self.users = {}
            for k, marks in last.items():
                back = [Mark(m.sem, m.value - loop.steps[m.sem.name],
                             m.steps + ((loop, loop.steps[m.sem.name]),))
                        for m in marks if m.value > start[m.sem.name]]
                self.users[k] = held.get(k, []) + back
            with self.nc.Fori(0, n, engines=(ENG.PE, ENG.Activation, ENG.DVE)) as i:
                loop.i = i
                self.loops.append(loop)
                self.fixed = fixed
                body(i)
                self.loops.pop()
        for k, marks in self.users.items():
            self.users[k] = [self.ended(m, loop, start, n) for m in marks]
        for k, c in self.counters.items():
            c.value = first[k] + n * loop.steps[c.sem.name]

    def ended(self, m, loop, start, n):
        steps = tuple(s for s in m.steps if s[0] is not loop)
        if m.value <= start[m.sem.name] and len(steps) == len(m.steps):
            return m
        return Mark(m.sem, m.value + (n - 1) * loop.steps[m.sem.name], steps)


class Loop:
    def __init__(self, n):
        self.n, self.i, self.steps = n, None, {}


class Queue:

    def __init__(self, prog, engine, counter, gate):
        self.p, self.e, self.c, self.gate_sem = prog, engine, counter, gate

    def wait(self, *marks):
        if self.p.dry:
            return
        latest = {}
        for m in marks:
            key = (m.sem.name, tuple((id(l), n) for l, n in m.steps if n))
            if key not in latest or latest[key].value < m.value:
                latest[key] = m
        for m in latest.values():
            value = m.value
            for loop, step in m.steps:
                if step:
                    value = loop.i * step + value
            self.e.wait_ge(m.sem, value)

    def gate(self):
        if not self.p.dry and self.p.loops:
            self.e.sem_inc(self.gate_sem, 1)

    def run(self, f, *args, after=(), count=None, quiet=False, gate=False, **kw):
        self.wait(*after)
        if gate and after:
            self.gate()
        c = count or self.c
        if not quiet:
            c.value += 1
        if self.p.dry:
            return self.p.mark(c)
        ins = f(*args, **kw)
        if not quiet:
            ins.then_inc(c.sem, 1)
            return self.p.mark(c)
        return None

    def done(self):
        return self.p.mark(self.c)


def build(nc, ins, out, n_units, stop=None):
    ctx = ExitStack()
    with ctx:
        sem = lambda n: ctx.enter_context(nc.semaphore(n))
        prog = Program(nc)
        users = lambda name: prog.users.get(name, [])

        base = (nc.sbuf_base + 63) // 64 * 64

        def at(name, kb, shape, dt=F32):
            size = 4 * int(np.prod(shape[1:]))
            assert base + kb * KB + size <= nc.sbuf_top, (name, kb, size)
            return nc.alloc_sbuf_tensor_at(name, shape, dt, offset=base + int(kb * KB))

        X = at("X", 0, [P, KD, T])
        RAW = at("RAW", 16, [P, RING, BLOCKS * P])
        WH = at("WH", 32, [P, RING, BLOCKS * P], F32R)
        WL = at("WL", 48, [P, RING, BLOCKS * P], F32R)
        AH = at("AH", 64, [P, KD, T], F32R)
        AL = at("AL", 80, [P, KD, T], F32R)
        SQ = at("SQ", 96, [P, 2, T])
        RSTD = at("RSTD", 100, [P, 2, T])
        CON = at("CON", 104, [P, C_N])
        PAR = at("PAR", 109.375, [P, Q_N])
        LPARS = at("LPARS", 109.75, [P, 2, L_N])
        LP = at("LP", 110.6875, [P, L_N])
        ST = at("ST", 111.125, [P, 64])
        ONES = at("ONES", 111.375, [P, 8])
        Z = 111.5
        con = lambda c, n: CON[:, c:c + n]
        IDENT = con(C_ID, P)

        psum = [ctx.enter_context(nc.psum_tensor(f"bank{b}", [P, T], F32)) for b in range(8)]

        PEC = prog.counter("pe", sem("s_pe"), 64)
        ACC = prog.counter("act", sem("s_act"), 64)
        DVC = prog.counter("dve", sem("s_dve"), 64)
        UNC = prog.counter("unit", sem("s_unit_read"), RING)
        s_split = sem("s_unit_split")
        s_hi = sem("s_unit_hi")
        s_raw = [sem(f"s_unit_loaded{j}") for j in range(RING)]
        s_ones = sem("s_ones")
        s_in = {n: sem(f"s_in_{n}") for n in ("x", "con", "par", "lp", "mem", "row0", "row1", "strip")}
        s_out = sem("s_out")
        pe = Queue(prog, nc.tensor, PEC, sem("s_pe_gate"))
        act = Queue(prog, nc.scalar, ACC, sem("s_act_gate"))
        dve = Queue(prog, nc.vector, DVC, sem("s_dve_gate"))
        for q in (pe, act, dve):
            q.e.sem_inc(q.c.sem, 64)
        pe.e.sem_inc(UNC.sem, RING)
        loaded = lambda n, v=16: Mark(s_in[n], v)

        nc.scalar.dma_start(X[:, :, :], ins["x"]).then_inc(s_in["x"], 16)
        nc.scalar.dma_start(CON[:, :], ins["con"]).then_inc(s_in["con"], 16)
        nc.scalar.dma_start(PAR[:, :], ins["par"]).then_inc(s_in["par"], 16)
        nc.scalar.dma_start(LPARS[:, :, :], ins["lpar"]).then_inc(s_in["lp"], 16)
        for q in (pe, act, dve):
            q.wait(loaded("x"), loaded("con"), loaded("par"), loaded("lp"))

        WS = ins["ws"]
        nc.gpsimd.memset(ONES[:, :], 1.0).then_inc(s_ones, 1)
        nc.gpsimd.wait_ge(s_ones, 1)
        nc.gpsimd.sem_inc(s_split, RING)
        with nc.sync.Fori(0, n_units // RING) as i:
            for j in range(RING):
                nc.sync.wait_ge(s_split, i * RING + (j + 1))
                nc.sync.dma_start(RAW[:, j, :], WS[i * RING + j]).then_inc(s_raw[j], 16)
        with nc.gpsimd.Fori(0, n_units // RING) as i:
            for j in range(RING):
                nc.gpsimd.wait_ge(s_raw[j], i * 16 + 16)
                nc.gpsimd.wait_ge(UNC.sem, i * RING + (j + 1))
                nc.gpsimd.tensor_tensor(WH[:, j, :], RAW[:, j, :], ONES[:, 0:1].to_broadcast([P, BLOCKS * P]),
                                        ALU.mult).then_inc(s_hi, 1)
                nc.gpsimd.wait_ge(s_hi, i * RING + (j + 1))
                nc.gpsimd.tensor_tensor(WL[:, j, :], RAW[:, j, :], WH[:, j, :].bitcast(F32),
                                        ALU.subtract).then_inc(s_split, 1)

        V, S, PE = nc.vector, nc.scalar, nc.tensor
        row = prog.row

        def tt(o, a, b, op, after=(), **k):
            return dve.run(V.tensor_tensor, o, a, b, op, after=after, **k)

        def ts(o, a, s1, op0, s2=None, op1=ALU.bypass, after=(), **k):
            return dve.run(V.tensor_scalar, o, a, s1, s2, op0, op1, after=after, **k)

        def stt(o, a, s, b, op0, op1, after=(), **k):
            return dve.run(V.scalar_tensor_tensor, after=after, out=o, in0=a, scalar=s, in1=b, op0=op0, op1=op1, **k)

        def vcopy(o, a, after=(), **k):
            return dve.run(V.tensor_copy, o, a, after=after, **k)

        def actf(o, a, f=ACT.Copy, after=(), **k):
            return act.run(S.activation, o, a, f, after=after, **k)

        def mm(o, l, r, start, stop, last=False, after=(), count=None, gate=False):
            return pe.run(PE.matmul, o, l, r, start=start, stop=stop, after=after, gate=gate, quiet=not last, count=count,
                          skip_group_check=True)

        def transpose(o, a, after=(), last=False):
            k = a.shape[0]
            return pe.run(PE.transpose, o, a, IDENT[0:k, 0:k], after=after, quiet=not last, gate=k < P)

        def split(hi, lo, src, scale, after):
            h = actf(hi, src, ACT.Copy, scale=scale, after=after)
            return stt(lo, src, scale, hi.bitcast(F32), ALU.mult, ALU.subtract, after=[h, *after])

        def fence():
            marks = [*(q.done() for q in (pe, act, dve)), prog.mark(UNC)]
            for q in (pe, act, dve):
                q.wait(*marks)
                q.gate()
            prog.users.clear()

        def product(o, hi, lo, nk, need=(), cols=P, more=False, marks=None, ks=None):
            pe.wait(*need)
            mark = None
            for k in ks or range(nk):
                pos = prog.fixed["blocks"]
                slot, b = pos // BLOCKS % RING, pos % BLOCKS
                if b == 0:
                    now = prog.mark(UNC)
                    pe.wait(Mark(s_split, now.value + 1, now.steps))
                if marks is not None:
                    pe.wait(*marks[k])
                w = slice(b * P, b * P + cols)
                end = b == BLOCKS - 1 or (k == nk - 1 and not more)
                mm(o, WH[:, slot, w], hi(k), k == 0, False)
                mm(o, WH[:, slot, w], lo(k), False, False)
                mark = mm(o, WL[:, slot, w], hi(k), False, k == nk - 1, last=end or k == nk - 1,
                          count=UNC if end else None)
                prog.fixed["blocks"] = (pos // BLOCKS + 1) * BLOCKS if end else pos + 1
            return mark

        def group(hi, lo, nk, n_tiles, marks, banks=(2, 3, 4, 5), n=T):
            outs = []
            for k in range(nk):
                for i in range(n_tiles):
                    o = psum[banks[i]][:, 0:n]
                    m = product(o, hi, lo, nk, need=[*(marks[k] if i == 0 else []), *(users(banks[i]) if k == 0 else [])],
                                more=True, ks=[k])
                    if k == nk - 1:
                        outs.append((banks[i], o, m))
            return outs

        def gbank():
            prog.fixed["tiles"] += 1
            return prog.fixed["tiles"] % 2

        def dense(hi, lo, nk, need=(), n=T, cols=P, more=False, marks=None):
            b = gbank()
            o = psum[b][0:cols, 0:n]
            m = product(o, hi, lo, nk, need=[*need, *users(b)], cols=cols, more=more, marks=marks)
            return b, o, m

        A_hi = lambda k: AH[:, k, :]
        A_lo = lambda k: AL[:, k, :]

        def square_sum(k, n, src, after, bank=7, nt=NT):
            s = k % 2
            m = actf(SQ[:, s, 0:nt * P], src, ACT.Square, after=[*after, *users(f"sq{s}")])

            def add():
                for q in range(nt):
                    r = mm(psum[bank][:, q:q + 1], SQ[:, s, q * P:(q + 1) * P], ONEC, k == 0 and q == 0,
                           k == n - 1, last=q == nt - 1, after=[m, *(users(bank) if k == 0 else [])] if q == 0 else [])
                prog.users[f"sq{s}"] = [r]
                return r
            return add

        ONEC = CON[:, C_ONE:C_ONE + 1]

        def inverse_root(v, r, n, after):
            t = ST[:, 40:40 + n]
            m = ts(r.bitcast(I32), v.bitcast(I32), 1, ALU.logical_shift_right, after=after)
            m = ts(r.bitcast(I32), r.bitcast(I32), -1.0, ALU.mult, 1597463007.0, ALU.add, after=[m])
            for _ in range(3):
                m = tt(t, r, r, ALU.mult, after=[m])
                m = stt(t, t, -0.5, v, ALU.mult, ALU.mult, after=[m])
                m = stt(r, t, 1.5, r, ALU.add, ALU.mult, after=[m])
            return m

        def spread(slot, rs, after, nt=NT, bank=6):
            d = RSTD[:, slot, 0:nt * P]
            for q in range(nt):
                m = ts(d[:, q * P:(q + 1) * P], IDENT, rs[:, q:q + 1], ALU.mult,
                       after=[*after, *users(f"rstd{slot}")] if q == 0 else [])

            def finish():
                w = mm(psum[bank][:, 0:nt * P], CON[:, C_ONE:C_ONE + P], d, True, True, last=True,
                       after=[m, *users(bank)])
                r = actf(d, psum[bank][:, 0:nt * P], ACT.Copy, after=[w])
                prog.users[bank] = [r]
                return r
            return finish

        def norm_scale(slot, after, eps, scale=1.0 / D, nt=NT, bank=7):
            v, r = ST[:, 32:32 + nt], ST[:, 36:36 + nt]
            m = ts(v, psum[bank][:, 0:nt], scale, ALU.mult, eps, ALU.add, after=after)
            prog.users[bank] = [m]
            m = inverse_root(v, r, nt, [m])
            return spread(slot, r, [m], nt)

        def store_out(after):
            nc.scalar.wait_ge(after.sem, after.value)
            nc.scalar.dma_start(out, X[:, :, :]).then_inc(s_out, 16)
            nc.scalar.wait_ge(s_out, 16)

        col = lambda base_, k: PAR[:, base_ + k:base_ + k + 1]
        kT = at("kT", Z + 0, [P, T])
        vTM = at("vTM", Z + 2, [P, NT, P])
        MSK = at("MSK", Z + 4, [P, 1280])
        STRIP = at("STRIP", Z + 9, [P, 8, 256])
        G = at("G", Z + 17, [P, KD, T])
        BH = at("BH", Z + 33, [P, KD, T], F32R)
        BL = at("BL", Z + 49, [P, KD, T], F32R)
        vF = at("vF", Z + 65, [P, T])
        qI = at("qI", Z + 67, [P, 2, T])
        kI = at("kI", Z + 71, [P, T])
        SC = at("SC", Z + 73, [P, T])
        RL = at("RL", Z + 75, [P, 2, T])
        wTM = at("wTM", Z + 79, [P, NT * 4])
        T8 = at("T8", Z + 79.25, [P, 8])
        UP = at("UP", Z + 80, [P, 3, T + 16])
        ROW = at("ROW", Z + 87, [P, 2, 384])
        qC = at("qC", Z + 65, [P, 2, T])
        PR = at("PR", Z + 69, [P, 2, 1280])
        PT = at("PT", Z + 79, [P, 2, 1280])
        mOFF = [0, 128, 384, 768]
        kOFF = [0, 512, 1024, 896]

        amark = []
        for k in range(KD):
            amark.append([split(A_hi(k), A_lo(k), X[:, k, :], col(Q_MIXPRE, k), [])])
        for k in range(KD):
            sq = square_sum(k, KD, X[:, k, :], [])()
        rstd = norm_scale(0, [sq], EPS1)()
        R0 = RSTD[:, 0, :]

        def scaled(dst, b, o, m, extra=()):
            r = tt(dst, o, R0[0:o.shape[0], :], ALU.mult, after=[m, rstd, *extra])
            prog.users[b] = [r]
            return r

        b, o, m = dense(A_hi, A_lo, KD, marks=amark)
        k_ready = scaled(kT[:, :], b, o, m)
        b, o, m = dense(A_hi, A_lo, KD)
        v_f = scaled(vF[:, :], b, o, m)
        b, o, m = dense(A_hi, A_lo, KD, cols=68)
        ki_w = scaled(kI[0:68, :], b, o, m)
        for q in range(NT):
            w = pe.run(PE.transpose, psum[2][:, q * 4:q * 4 + 4], kI[64:68, q * P:(q + 1) * P],
                       IDENT[64:68, 64:68], after=[ki_w], quiet=q < NT - 1)
        w_ready = ts(wTM[:, :], psum[2][:, 0:16], 1.0 / 16, ALU.mult, after=[w])
        ki_ready = vcopy(kI[64:128, :], kI[0:64, :], after=[w])
        prog.users[2] = [w_ready]
        for q in range(NT):
            w = transpose(psum[3][:, q * P:(q + 1) * P], vF[:, q * P:(q + 1) * P], after=[v_f], last=q == NT - 1)
        v_ready = actf(vTM[:, :, :].rearrange("p a b -> p (a b)"), psum[3][:, :], after=[w])
        prog.users[3] = [v_ready]
        for j in range(2):
            b, o, m = dense(A_hi, A_lo, KD)
            qi_ready = scaled(qI[:, j, :], b, o, m)

        table = PAR[0:32, Q_TAB:Q_TAB + 8]
        SCR = ins["scratch"]
        for h in range(8):
            s = h % 2
            w = mm(psum[4 + s][:, 0:384], table[:, h:h + 1].to_broadcast([32, P]), CON[0:32, C_HOT:C_HOT + 384],
                   True, True, last=True, after=users(4 + s))
            r = actf(ROW[:, s, :], psum[4 + s][:, 0:384], after=[w] + ([loaded(f"row{s}", 16 * (h // 2))] if h > 1 else []))
            prog.users[4 + s] = [r]
            act.wait(r)
            nc.scalar.dma_start(SCR[h], ROW[:, s, :]).then_inc(s_in[f"row{s}"], 16)
        act.wait(loaded("row0", 64), loaded("row1", 64))
        nc.scalar.dma_start(STRIP[:, :, :], SCR.rearrange("h p c -> h (p c)")[:, 127:127 + P * 383]
                            .rearrange("h (p c) -> p h c", c=383)[:, :, 0:256]).then_inc(s_in["strip"], 16)

        m0 = vcopy(MSK[:, 0:P], con(C_CAUS, P))

        def scores(q):
            keys = (q + 1) * P
            acc = None
            for h in range(4):
                half = slice(64 * (h % 2), 64 * (h % 2) + 64)
                bk = 2 + h % 2
                w = mm(psum[bk][:, 0:keys], qI[half, h // 2, q * P:(q + 1) * P], kI[half, 0:keys], True, True,
                       last=True, after=[qi_ready, ki_ready, *users(bk)])
                r = actf(RL[:, h % 2, 0:keys], psum[bk][:, 0:keys], ACT.Relu, after=[w, *users(f"rl{h % 2}")])
                prog.users[bk] = [r]
                wh = wTM[:, q * 4 + h:q * 4 + h + 1]
                if h == 0:
                    acc = ts(SC[:, 0:keys], RL[:, 0, 0:keys], wh, ALU.mult, after=[r, *users("sc")])
                else:
                    acc = stt(SC[:, 0:keys], RL[:, h % 2, 0:keys], wh, SC[:, 0:keys], ALU.mult, ALU.add, after=[r, acc])
                prog.users[f"rl{h % 2}"] = [acc]
            return tt(SC[:, keys - P:keys], SC[:, keys - P:keys], con(C_CAUS, P), ALU.add, after=[acc])

        def select(q, m):
            keys = (q + 1) * P
            for _ in range(TOPK // 8):
                m = dve.run(V.max, T8[:, :], SC[:, 0:keys], after=[m])
                m = dve.run(V.match_replace, SC[:, 0:keys], T8[:, :], SC[:, 0:keys], TAKEN, after=[m])
            m = ts(MSK[:, mOFF[q]:mOFF[q] + keys], SC[:, 0:keys], -2e38, ALU.is_gt, NEG, ALU.mult, after=[m])
            prog.users["sc"] = [m]
            return m

        s1 = scores(1)
        um = dve.run(V.memset, UP[:, :, 0:16], 0.0)
        U, S0, S1 = (UP[:, j, :] for j in range(3))
        N0, N1 = 16, T + 16
        pooled = []
        for g, win in enumerate(POOL_WINDOWS):
            b, o, m = dense(A_hi, A_lo, KD)
            m = scaled(U[:, N0:N1], b, o, m, [um])
            src, dst, step = U, S0, 1
            while step < win:
                m = tt(dst[:, N0:N1], src[:, N0:N1], src[:, N0 - step:N1 - step], ALU.add, after=[m])
                src, dst, step = dst, (S1 if dst is S0 else S0), step * 2
            inv = CON[:, C_INV + 16 * g:C_INV + 16 * g + 16]
            m1 = tt(dst[:, N0:N0 + 16], src[:, N0:N0 + 16], inv, ALU.mult, after=[m])
            m = stt(src[:, N0:N1], src[:, N0:N1], 1.0 / win, U[:, N0:N1], ALU.mult, ALU.subtract, after=[m1])
            m = tt(src[:, N0:N0 + 16], dst[:, N0:N0 + 16], U[:, N0:N0 + 16], ALU.subtract, after=[m])
            um = split(BH[:, g, :], BL[:, g, :], src[:, N0:N1], 1.0, [m])
            pooled.append([um])
            if g == 0:
                sel = select(1, s1)
                s1 = scores(2)
            if g == 2:
                sel = select(2, s1)
                s1 = scores(3)
        mixed = []
        for g in range(4):
            b, o, m = dense(lambda k: BH[:, g, :], lambda k: BL[:, g, :], 1, need=pooled[g], more=g < 3)
            r = split(BH[:, 4 + g, :], BL[:, 4 + g, :], o, col(Q_PSCALE, g), [m])
            prog.users[b] = [r]
            mixed.append([r])
        sel = select(3, s1)
        for j in range(KD):
            b, o, m = dense(lambda k: BH[:, 4 + k, :], lambda k: BL[:, 4 + k, :], 4, marks=mixed,
                            more=j % 2 == 0)
            r = actf(G[:, j, :], o, after=[m])
            prog.users[b] = [r]
        for q in (pe, act, dve):
            q.wait(loaded("strip"))
        fence()

        SCALE = 128.0 ** -0.5

        def query_tile(s):
            b, o, m = dense(A_hi, A_lo, KD)
            return scaled(qC[:, s, :], b, o, m, users(f"q{s}"))

        def head_logits(h, s, q_ready):
            where = [(2, 0), (3, 0), (2, 128), (4, 0)]
            mx, den = ST[:, 4 * s:4 * s + 4], ST[:, 8 + 4 * s:12 + 4 * s]
            wrote = {}
            for q in (0, 2, 1, 3):
                bk, c = where[q]
                keys = (q + 1) * P
                wrote[bk] = mm(psum[bk][:, c:c + keys], qC[:, s, q * P:(q + 1) * P], kT[:, 0:keys], c == 0, True,
                               last=True, after=[q_ready, *users(bk)] if c == 0 else [])
            for q in (0, 2, 1, 3):
                bk, c = where[q]
                keys = (q + 1) * P
                pr = PR[:, s, mOFF[q]:mOFF[q] + keys]
                m = stt(pr, psum[bk][:, c:c + keys], SCALE, MSK[:, mOFF[q]:mOFF[q] + keys], ALU.mult, ALU.add,
                        after=[wrote[bk], *users(f"pr{s}")])
                if q != 0:
                    near = slice(mOFF[q] + keys - 256, mOFF[q] + keys)
                    m = tt(PR[:, s, near], PR[:, s, near], row(STRIP, h), ALU.add, after=[m])
                else:
                    m = tt(PR[:, s, 0:P], PR[:, s, 0:P], row(STRIP, h)[:, P:256], ALU.add, after=[m])
                m = dve.run(V.tensor_reduce, mx[:, q:q + 1], pr, AX, ALU.max, negate=True, after=[m])
                if q:
                    prog.users[bk] = [m]
                e = actf(pr, pr, ACT.Exp, bias=mx[:, q:q + 1], accum_out=den[:, q:q + 1], after=[m])
            m = dve.run(V.reciprocal, den, den, after=[e])
            for q in range(NT):
                pr = PR[:, s, mOFF[q]:mOFF[q] + (q + 1) * P]
                m = ts(pr, pr, den[:, q:q + 1], ALU.mult, after=[m])
            prog.users[f"q{s}"] = [wrote[4]]
            return m

        def head_turn(s, p_ready):
            copies = []
            for bk, tiles in ((5, (0,)), (6, (1, 3)), (7, (2,))):
                c = 0
                for b in tiles:
                    for q in range(b, NT):
                        w = transpose(psum[bk][:, c:c + P], PR[:, s, mOFF[q] + b * P:mOFF[q] + (b + 1) * P],
                                      after=[p_ready, *users(bk)] if c == 0 else [], last=b == tiles[-1] and q == NT - 1)
                        c += P
                at_ = kOFF[tiles[0]]
                copy = vcopy if bk == 6 else actf
                copies.append(copy(PT[:, s, at_:at_ + c], psum[bk][:, 0:c], after=[w, *users(f"pt{s}")]))
                prog.users[bk] = [copies[-1]]
            prog.users[f"pr{s}"] = [w]
            return copies

        def head_values(h, s, pt):
            for b in range(NT):
                w = mm(psum[3][:, b * P:T], vTM[:, b, :], PT[:, s, kOFF[b]:kOFF[b] + T - b * P], b == 0, b == NT - 1,
                       last=b == NT - 1, after=[*pt, *users(3)] if b == 0 else [])
            prog.users[f"pt{s}"] = [w]
            r = split(row(BH, h), row(BL, h), psum[3][:, :], 1.0, [w])
            prog.users[3] = [r]
            prog.users["att_r"] = [r]

        def pool_gate(j):
            s = 0
            b, o, m = dense(A_hi, A_lo, KD)
            m = tt(SQ[:, s, :], o, R0, ALU.mult, after=[m, *users("sq0")])
            prog.users[b] = [m]
            m = actf(SQ[:, s, :], SQ[:, s, :], ACT.Tanh, scale=0.5, after=[m])
            g = row(G, j)
            m = stt(g, SQ[:, s, :], 1.0, g, ALU.add, ALU.mult, after=[m])
            prog.users["sq0"] = [m]

        def two_heads(i):
            h0, h1 = i * 2, i * 2 + 1
            q0 = query_tile(0)
            p0 = head_logits(h0, 0, q0)
            q1 = query_tile(1)
            t0 = head_turn(0, p0)
            p1 = head_logits(h1, 1, q1)
            pool_gate(h0)
            head_values(h0, 0, t0)
            t1 = head_turn(1, p1)
            pool_gate(h1)
            head_values(h1, 1, t1)

        prog.loop(4, two_heads)
        att_ready = users("att_r")
        B_hi = lambda k: BH[:, k, :]
        B_lo = lambda k: BL[:, k, :]

        def merge(j, after):
            b, o, m = dense(A_hi, A_lo, KD)
            m = tt(SQ[:, 0, :], o, R0, ALU.mult, after=[m, *users("sq0")])
            prog.users[b] = [m]
            t_m = actf(SQ[:, 0, :], SQ[:, 0, :], ACT.Tanh, scale=0.5, after=[m])
            b, o, m = dense(B_hi, B_lo, KD, need=after)
            m = stt(SQ[:, 0, :], SQ[:, 0, :], 1.0, o, ALU.add, ALU.mult, after=[m, t_m])
            prog.users[b] = [m]
            g = row(G, j)
            m = tt(g, g, SQ[:, 0, :], ALU.add, after=[m])
            prog.users["sq0"] = [m]
            prog.users["g"] = [m]

        def merge_two(i):
            merge(i * 2, att_ready)
            merge(i * 2 + 1, att_ready)

        prog.loop(4, merge_two)
        g_ready = users("g") + [prog.mark(UNC)]


        def project(hi, lo, nk, marks, Y, need=(), more=False):
            add = None
            for j in range(KD):
                b, o, m = dense(hi, lo, nk, marks=marks if j == 0 else None, need=need, more=more and j % 2 == 0)
                if add:
                    add()
                r = actf(Y[:, j, :], o, after=[m])
                prog.users[b] = [r]
                add = square_sum(j, KD, Y[:, j, :], [r])
            return add()

        def residual(Y, gain, next_gain, rs, a_free, nxt=True):
            marks = []
            xs = []
            for k in range(KD):
                m = stt(Y[:, k, :], Y[:, k, :], col(gain, k), RSTD[:, 1, :], ALU.mult, ALU.mult, after=[rs])
                m = tt(X[:, k, :], X[:, k, :], Y[:, k, :], ALU.add, after=[m])
                xs.append(m)
                if next_gain is not None:
                    marks.append([split(A_hi(k), A_lo(k), X[:, k, :], next_gain(k), [m, *a_free])])
            prog.users["rstd1"] = [xs[-1]]
            return marks, xs

        amark = [[split(A_hi(k), A_lo(k), G[:, k, :], 0.5, g_ready)] for k in range(KD)]
        memX = at("memX", Z + 65, [P, KD, 256])
        MH = at("MH", Z + 33, [P, KD, 256], F32R)
        ML = at("ML", Z + 41, [P, KD, 256], F32R)
        kM = at("kM", Z + 0, [P, 4, 256])
        vM = at("vM", Z + 4, [P, 2, T])
        qM = at("qM", Z + 8, [P, 2, T])
        PM = at("PM", Z + 57, [P, 2, 4 * 256])
        PMT = at("PMT", Z + 65, [P, 2, 2 * T])
        MAH = at("MAH", Z + 73, [P, 4, T], F32R)
        MAL = at("MAL", Z + 81, [P, 4, T], F32R)
        NM = 256
        act.wait(*att_ready, *users("pt0"), *users("pt1"))
        nc.scalar.dma_start(memX[:, :, :], ins["mem"]).then_inc(s_in["mem"], 16)
        act.wait(*g_ready)
        dve.wait(*g_ready)
        mm_marks = [[split(MH[:, k, :], ML[:, k, :], memX[:, k, :], col(Q_MEMKV, k), [loaded("mem")])] for k in range(KD)]
        for k in range(KD):
            sq = square_sum(k, KD, memX[:, k, :], [loaded("mem")], nt=2)()
        v2, r2 = ST[:, 32:34], ST[:, 36:38]
        m = ts(v2, psum[7][:, 0:2], 1.0 / D, ALU.mult, EPS1, ALU.add, after=[sq])
        prog.users[7] = [m]
        mem_r = inverse_root(v2, ST[:, 48:50], 2, [m])
        mem_rstd = spread(0, ST[:, 48:50], [mem_r], nt=2)()

        Y = G
        sq = project(A_hi, A_lo, KD, amark, Y, need=amark[-1])
        rs = norm_scale(1, [sq], EPS1)()

        amark, xmark = residual(Y, Q_MIXPOST, lambda k: col(Q_MEMPRE, k), rs, [prog.mark(UNC)])
        for j in range(4):
            b, o, m = dense(lambda k: MH[:, k, :], lambda k: ML[:, k, :], KD, n=NM, marks=mm_marks)
            r = tt(kM[:, j, :], o, RSTD[:, 0, 0:NM], ALU.mult, after=[m, mem_rstd])
            prog.users[b] = [r]
        km_ready = r
        prog.users["rstd0"] = [r]
        vb = [2, 3]
        for u in range(4):
            pos = prog.fixed["blocks"]
            slot = pos // BLOCKS % RING
            now = prog.mark(UNC)
            pe.wait(Mark(s_split, now.value + 1, now.steps))
            for kk in range(2):
                k = 2 * u + kk
                for t in range(2):
                    o = psum[vb[t]][:, :]
                    tk = slice(t * P, (t + 1) * P)
                    wsl = slice(kk * T, (kk + 1) * T)
                    mm(o, MH[:, k, tk], WH[:, slot, wsl], k == 0, False)
                    mm(o, MH[:, k, tk], WL[:, slot, wsl], False, False)
                    last = kk == 1 and t == 1
                    m = mm(o, ML[:, k, tk], WH[:, slot, wsl], False, k == KD - 1, last=last, count=UNC if last else None)
            prog.fixed["blocks"] += BLOCKS
        for t in range(2):
            vm_ready = ts(vM[:, t, :], psum[vb[t]][:, :], ST[:, 48 + t:49 + t], ALU.mult, after=[m, mem_r])
            prog.users[vb[t]] = [vm_ready]
        for k in range(KD):
            sq = square_sum(k, KD, X[:, k, :], [xmark[k]])()
        rstd = norm_scale(0, [sq], EPS1)()

        MSCALE = 128.0 ** -0.5

        def mem_logits(h, s, q_ready):
            mx, den = ST[:, 4 * s:4 * s + 4], ST[:, 8 + 4 * s:12 + 4 * s]
            for q in range(NT):
                bk = 2 + q // 2
                w = mm(psum[bk][:, (q % 2) * NM:(q % 2 + 1) * NM], qM[:, s, q * P:(q + 1) * P], kM[:, h, :],
                       q % 2 == 0, True, last=True, after=[q_ready, km_ready, *users(bk)] if q % 2 == 0 else [])
                if q % 2:
                    m = dve.run(V.tensor_reduce, mx[:, q - 1:q + 1],
                                psum[bk][:, :].rearrange("p (a b) -> p a b", a=2), AX, ALU.max, negate=True, after=[w])
            prog.users[f"qm{s}"] = [w]
            m = ts(mx, mx, MSCALE, ALU.mult, after=[m])
            for q in range(NT):
                bk = 2 + q // 2
                e = actf(PM[:, s, q * NM:(q + 1) * NM], psum[bk][:, (q % 2) * NM:(q % 2 + 1) * NM], ACT.Exp, scale=MSCALE,
                         bias=mx[:, q:q + 1], accum_out=den[:, q:q + 1], after=[m, *users(f"pm{s}")])
            prog.users[2] = prog.users[3] = [e]
            m = dve.run(V.reciprocal, den, den, after=[e])
            for q in range(NT):
                pr = PM[:, s, q * NM:(q + 1) * NM]
                m = ts(pr, pr, den[:, q:q + 1], ALU.mult, after=[m])
            return m

        def mem_values(h, s, p_ready):
            done = []
            for b in range(2):
                for q in range(NT):
                    w = transpose(psum[4 + b][:, q * P:(q + 1) * P], PM[:, s, q * NM + b * P:q * NM + (b + 1) * P],
                                  after=[p_ready, *users(4 + b)] if q == 0 else [], last=q == NT - 1)
                c = (actf, vcopy)[b](PMT[:, s, b * T:(b + 1) * T], psum[4 + b][:, :], after=[w, *users(f"pmt{s}")])
                prog.users[4 + b] = [c]
                done.append(c)
            prog.users[f"pm{s}"] = [w]
            for b in range(2):
                w = mm(psum[6][:, :], vM[:, b, h * P:(h + 1) * P], PMT[:, s, b * T:(b + 1) * T], b == 0, b == 1,
                       last=b == 1, after=[*done, vm_ready, *users(6)] if b == 0 else [])
            prog.users[f"pmt{s}"] = [w]
            r = split(MAH[:, h, :], MAL[:, h, :], psum[6][:, :], 1.0, [w])
            prog.users[6] = [r]
            return r

        held = None
        mark4 = []
        for h in range(4):
            s = h % 2
            b, o, m = dense(A_hi, A_lo, KD, marks=amark if h == 0 else None)
            q_ready = scaled(qM[:, s, :], b, o, m, users(f"qm{s}"))
            if held is not None:
                mark4.append([mem_values(h - 1, 1 - s, held)])
            held = mem_logits(h, s, q_ready)
        prog.users["rstd0"] = [q_ready]
        mark4.append([mem_values(3, 1, held)])
        Y = G
        sq = project(lambda k: MAH[:, k, :], lambda k: MAL[:, k, :], 4, mark4, Y, more=True)
        rs = norm_scale(1, [sq], EPS1)()
        amark, xmark = residual(Y, Q_MEMPOST, lambda k: col(Q_FFNPRE, k), rs, [])
        for k in range(KD):
            sq = square_sum(k, KD, X[:, k, :], [xmark[k]])()
        rstd = norm_scale(0, [sq], EPS1)()
        fence()

        DH = at("DH", Z + 0, [P, KF, T], F32R)
        DL = at("DL", Z + 44, [P, KF, T], F32R)
        HG = at("HG", Z + 88, [P, 2, T])
        HH = at("HH", Z + 92, [P, T])

        def gate_up(j, s):
            b, o, m = dense(A_hi, A_lo, KD)
            m = tt(HG[:, s, :], o, R0, ALU.mult, after=[m, *users(f"hg{s}")])
            prog.users[b] = [m]
            t_m = actf(SQ[:, s, :], HG[:, s, :], ACT.Tanh, scale=0.5, after=[m, *users(f"sq{s}")])
            m = stt(HG[:, s, :], SQ[:, s, :], 1.0, HG[:, s, :], ALU.add, ALU.mult, after=[t_m])
            prog.users[f"sq{s}"] = [m]
            m = tt(HG[:, s, :], HG[:, s, :], R0, ALU.mult, after=[m])
            b, o, m2 = dense(A_hi, A_lo, KD)
            m = tt(HH[:, :], o, HG[:, s, :], ALU.mult, after=[m, m2, *users("hh")])
            prog.users[b] = prog.users[f"hg{s}"] = [m]
            r = split(row(DH, j), row(DL, j), HH[:, :], 0.5, [m])
            prog.users["hh"] = prog.users["d"] = [r]

        def gate_up_two(i):
            gate_up(i * 2, 0)
            gate_up(i * 2 + 1, 1)

        prog.loop(KF // 2, gate_up_two)
        d_ready = users("d")
        YF = at("YF", 64, [P, KD, T])
        sq = project(lambda k: DH[:, k, :], lambda k: DL[:, k, :], KF, None, YF, need=d_ready)
        rs = norm_scale(1, [sq], EPS1)()
        amark, xmark = residual(YF, Q_FFNPOST, lambda k: 1.0, rs, [])
        for k in range(KD):
            prog.users[f"in{k}"] = amark[k]
        if stop == 1:
            fence()
            store_out(Mark(DVC.sem, DVC.value))
            return prog.fixed

        kW = at("kW", Z + 0, [P, 2, T])
        vW = at("vW", Z + 4, [P, NT, 256])
        ATT = at("ATT", Z + 8, [P, KD, T])
        XS = at("XS", Z + 24, [P, KD, T])
        OH = at("OH", 64, [P, 2 * KD, T], F32R)
        OL = at("OL", Z + 8, [P, 2 * KD, T], F32R)
        bF = at("bF", Z + 40, [P, 2, T])
        cF = at("cF", Z + 44, [P, 2, T])
        dtF = at("dtF", Z + 48, [P, T])
        acF = at("acF", Z + 50, [P, T])
        TM = at("TM", Z + 52, [P, 6, 64])
        dtT, acT, lastT, endT, chT = (TM[:, j, :] for j in range(5))
        PV = at("PV", Z + 53.5, [P, D])
        qW = at("qW", Z + 57.5, [P, 2, T])
        PWs = [at(f"PW{s}", Z + 61.5 + 3.5 * s, [P, 896]) for s in range(2)]
        PWTs = [at(f"PWT{s}", Z + (68.5, 91)[s], [P, 896]) for s in range(2)]
        XDD = at("XDD", Z + 48, [P, T])
        MX = at("MX", Z + 72, [P, 8, P])
        XDT = at("XDT", Z + 76, [P, D])
        CEX = at("CEX", Z + 80, [P, 8, P])
        xC = at("xC", Z + 84, [P, KD, P])
        bC = at("bC", Z + 88, [P, 2, P])
        CBT = at("CBT", Z + 89, [P, 2, P])
        bT = at("bT", Z + 90, [P, 2, P])
        ACV = at("ACV", Z + 57.5, [P, 2, T])
        TCV = at("TCV", Z + 61.5, [P, 2, T])
        vWF = at("vWF", Z + 65.5, [P, 2, T])
        DTW = at("DTW", Z + 72, [P, 4, T])
        lcol = lambda c, k=0: LP[:, c + k:c + k + 1]
        SINKB = at("SINKB", 111.4375, [P, 16])

        units_before = prog.fixed["blocks"] // BLOCKS

        def layer(L):
            m = vcopy(LP[:, :], row(LPARS, L), after=users("lp"))
            m = ts(LP[:, L_CW:L_CW + 60], LP[:, L_CW:L_CW + 60], 0.5, ALU.mult, after=[m])
            m = vcopy(SINKB[:, :], LP[:, L_SINK:L_SINK + 16], after=[m])
            m = ts(LP[:, L_SINK:L_SINK + 16], LP[:, L_SINK:L_SINK + 16], -8.0, ALU.mult, after=[m])
            lp_ready = m
            dve.run(V.memset, PV[:, :], 0.0)

            def conv(j, b, o, m):
                s = j % 2
                acc = ACV[:, s, :]
                m = actf(acc, o, ACT.Identity, scale=lcol(L_CW, 4 * j + 3), bias=lcol(L_CB, j),
                         after=[m, lp_ready, *users(f"acv{s}")])
                for tap in (2, 1, 0):
                    d = 3 - tap
                    m = stt(acc[:, d:T], o[:, 0:T - d], lcol(L_CW, 4 * j + tap), acc[:, d:T], ALU.mult, ALU.add, after=[m])
                prog.users[b] = [m]
                t_m = actf(TCV[:, s, :], acc, ACT.Tanh, after=[m])
                dst = XS[:, j, :] if j < 8 else (bF[:, j - 8, :] if j < 10 else cF[:, j - 10, :])
                m = stt(dst, TCV[:, s, :], 1.0, acc, ALU.add, ALU.mult, after=[t_m])
                prog.users[f"acv{s}"] = [m]

            first = group(A_hi, A_lo, KD, 4, [users(f"in{k}") for k in range(KD)])
            b, o, dt_m = dense(A_hi, A_lo, KD, cols=16)
            for j in range(4):
                conv(j, *first[j])

            a16 = ST[0:16, 56:57]
            v, e1, u, t1 = (DTW[0:16, j, :] for j in range(4))
            m = ts(v, o, LP[0:16, L_DTB:L_DTB + 1], ALU.add, after=[dt_m])
            prog.users[b] = [m]
            m = stt(e1, v, -1.0, v, ALU.mult, ALU.max, after=[m])
            e = actf(a16, LP[0:16, L_ALOG:L_ALOG + 1], ACT.Exp, after=[lp_ready])
            an = ts(a16, a16, -1.0, ALU.mult, after=[e])
            m = actf(e1, e1, ACT.Exp, scale=-1.0, after=[m])
            m = ts(u, e1, 1.0, ALU.add, after=[m])
            lg = actf(dtF[0:16, :], u, ACT.Ln, after=[m])
            m = ts(t1, u, -1.0, ALU.add, after=[m])
            m = tt(e1, e1, t1, ALU.subtract, after=[m])
            m = dve.run(V.reciprocal, u, u, after=[m, lg])
            m = tt(e1, e1, u, ALU.mult, after=[m])
            m = tt(e1, e1, dtF[0:16, :], ALU.add, after=[m])
            m = stt(dtF[0:16, :], v, 0.0, e1, ALU.max, ALU.add, after=[m])
            m = ts(v, dtF[0:16, :], a16, ALU.mult, after=[m, an])
            for c in range(NT):
                cs = slice(c * P, (c + 1) * P)
                m = dve.run(V.tensor_tensor_scan, acF[0:16, cs], ONES[0:16, 0:1].to_broadcast([16, P]), v[:, cs],
                            0.0, ALU.mult, ALU.add, after=[m])
            dt_ready = m
            for j in range(4, 12):
                conv(j, *dense(A_hi, A_lo, KD))

            for j in range(2):
                b, o, m = dense(A_hi, A_lo, KD)
                kw = actf(kW[:, j, :], o, after=[m])
                prog.users[b] = [kw]
            for c in range(NT):
                cs = slice(c * P, (c + 1) * P)
                c16 = slice(16 * c, 16 * c + 16)
                w = transpose(psum[2][:, c16], dtF[0:16, cs], after=[dt_ready, *users(2)] if c == 0 else [])
                w = transpose(psum[2][:, 64 + 16 * c:80 + 16 * c], acF[0:16, cs])
                w = mm(psum[2][:, 128 + 16 * c:144 + 16 * c], acF[0:16, (c + 1) * P - 1:(c + 1) * P].to_broadcast([16, P]),
                       IDENT[0:16, 0:16], True, True, last=c == 3)
            r = vcopy(TM[:, 0:3, :], psum[2][:, 0:192].rearrange("p (a b) -> p a b", a=3), after=[w])
            prog.users[2] = [r]
            m = tt(endT, lastT, acT, ALU.subtract, after=[r])
            m = actf(endT, endT, ACT.Exp, after=[m])
            actf(chT, lastT, ACT.Exp, after=[r])
            for j in range(2):
                b, o, m = dense(A_hi, A_lo, KD)
                r = actf(vWF[:, j, :], o, after=[m])
                prog.users[b] = [r]
                for q in range(NT):
                    w = transpose(psum[3 + j][:, q * P:(q + 1) * P], vWF[:, j, q * P:(q + 1) * P],
                                  after=[r, *users(3 + j)] if q == 0 else [], last=q == NT - 1)
                vw = vcopy(vW[:, :, j * P:(j + 1) * P], psum[3 + j][:, :].rearrange("p (a b) -> p a b", a=NT), after=[w])
                prog.users[3 + j] = [vw]
            fence()

            oW = [768, 0, 256, 512]
            DIST = CON[:, C_DIST:C_DIST + 384]

            def window_head(c, s, hh, q_ready):
                half = slice(64 * hh, 64 * hh + 64)
                PW, PWT = PWs[hh], PWTs[hh]
                hc = (c * 2 + s) * 2 + hh
                wrote = {}
                for q in (1, 2, 3, 0):
                    bk, at_ = 2 + oW[q] // T, oW[q] % T
                    n = 256 if q else P
                    wrote[bk] = mm(psum[bk][:, at_:at_ + n], qW[half, s, q * P:(q + 1) * P],
                                   kW[half, s, (q + 1) * P - n:(q + 1) * P], at_ == 0, True, last=q in (2, 0),
                                   after=[q_ready, *users(bk)] if at_ == 0 else [])
                sl = CON[:, bass.ds(hc + C_SLOPE, 1)]
                m = stt(PW[:, 0:512].rearrange("p (a b) -> p a b", a=2), DIST[:, 0:256].unsqueeze(1).to_broadcast([P, 2, 256]),
                        sl, psum[2][:, :].rearrange("p (a b) -> p a b", a=2), ALU.mult, ALU.add,
                        after=[wrote[2], *users(f"pw{hh}")])
                prog.users[2] = [m]
                m = stt(PW[:, 512:896], DIST, sl, psum[3][:, 0:384], ALU.mult, ALU.add, after=[wrote[3]])
                prog.users[3] = [m]
                z = 12 * hh
                mx, den, es = ST[:, z:z + 4], ST[:, z + 4:z + 8], ST[:, z + 8:z + 12]
                pw = [PW[:, oW[q]:oW[q] + (256 if q else P)] for q in range(NT)]
                m = dve.run(V.tensor_reduce, mx[:, 1:4], PW[:, 0:768].rearrange("p (a b) -> p a b", a=3), AX, ALU.max,
                            negate=True, after=[m])
                m = dve.run(V.tensor_reduce, mx[:, 0:1], pw[0], AX, ALU.max, negate=True)
                m = ts(mx, mx, LP[:, bass.ds(hc + L_SINK, 1)], ALU.min, 0.125, ALU.mult, after=[m])
                for q in range(NT):
                    actf(pw[q], pw[q], ACT.Exp, scale=0.125, bias=mx[:, q:q + 1], accum_out=den[:, q:q + 1],
                         after=[m] if q == 0 else [])
                e = actf(es, mx, ACT.Exp, bias=SINKB[:, bass.ds(hc, 1)])
                yield
                m = tt(den, den, es, ALU.add, after=[e])
                m = dve.run(V.reciprocal, den, den, after=[m])
                for q in range(NT):
                    m = ts(pw[q], pw[q], den[:, q:q + 1], ALU.mult, after=[m] if q == 0 else [])
                for b in range(NT):
                    bk, c0 = 2 + b // 2, (b % 2) * 256
                    cur = pw[b][:, 128:256] if b else pw[0]
                    w = transpose(psum[bk][:, c0:c0 + P], cur, after=[m, *users(bk)] if c0 == 0 else [], last=b == 3)
                    if b < 3:
                        w = transpose(psum[bk][:, c0 + P:c0 + 256], pw[b + 1][:, 0:P], last=b == 1)
                    if b == 1:
                        t0 = actf(PWT[:, 0:512], psum[2][:, :], after=[w, *users(f"pwt{hh}")])
                t1 = vcopy(PWT[:, 512:896], psum[3][:, 0:384], after=[w, *users(f"pwt{hh}")])
                prog.users[2], prog.users[3] = [t0], [t1]
                prog.users[f"pw{hh}"] = [w]
                yield
                o = psum[4]
                val = lambda b: vW[:, b, s * P + 64 * hh:s * P + 64 * hh + 64]
                for q in range(NT):
                    w = mm(o[half, q * P:(q + 1) * P], val(q), PWT[:, q * 256:q * 256 + P], q == 0, q == 0,
                           after=[t0, t1, *users(4)] if q == 0 else [])
                    if q:
                        w = mm(o[half, q * P:(q + 1) * P], val(q - 1), PWT[:, (q - 1) * 256 + P:q * 256],
                               False, True, last=q == NT - 1)
                prog.users[f"pwt{hh}"] = [w]
                yield w

            cum = con(C_TRIL, P)

            def chunk(c):
                ck = bass.ts(c, P)
                by_head = lambda t: t.rearrange("p (h d) -> p h d", d=64)
                over = lambda t, n, w: t.unsqueeze(2).to_broadcast([P, n, w])
                b_m = actf(bC[:, :, :], bF[:, :, ck], after=users("bc"))
                x_m = actf(xC[:, :, :], XS[:, :, ck], after=users("xc"))
                yield
                for g in range(2):
                    w = mm(psum[7][:, g * P:(g + 1) * P], bC[:, g, :], cF[:, g, ck], g == 0, True,
                           after=[b_m, *users(7)] if g == 0 else [])
                for g in range(2):
                    w = transpose(psum[7][:, (2 + g) * P:(3 + g) * P], bC[:, g, :], last=g == 1)
                prog.users["bc"] = [w]
                cb = tt(CBT[:, :, :], psum[7][:, 0:256].rearrange("p (g l) -> p g l", g=2),
                        cum.unsqueeze(1).to_broadcast([P, 2, P]), ALU.mult, after=[w])
                bt = actf(bT[:, :, :].rearrange("p a b -> p (a b)"), psum[7][:, 256:512], after=[w, cb, *users("bt")])
                prog.users[7] = [bt]
                for g in range(2):
                    bk = 5 + g
                    for j in range(4):
                        w = transpose(psum[bk][:, j * P:(j + 1) * P], xC[:, g * 4 + j, :],
                                      after=[x_m, *users(bk)] if j == 0 else [], last=j == 3)
                    xd = tt(by_head(XDT[:, g * T:(g + 1) * T]), by_head(psum[bk][:, :]),
                            over(dtT[:, bass.ds(c * 16 + g * 8, 8)], 8, 64), ALU.mult, after=[w, *users("xdt")])
                    prog.users[bk] = [xd]
                for g in range(2):
                    yield
                    for h4 in range(2):
                        bk = 5 + h4
                        hs = slice(h4 * 4, h4 * 4 + 4)
                        for h in range(4):
                            hd = g * 8 + h4 * 4 + h
                            w = mm(psum[bk][:, h * P:(h + 1) * P], IDENT[0:16, hd:hd + 1].to_broadcast([16, P]),
                                   acF[0:16, ck], h == 0, True, after=users(bk) if h == 0 else [], last=h == 3,
                                   gate=True)
                        m = tt(MX[:, hs, :], psum[bk][:, :].rearrange("p (h l) -> p h l", h=4),
                               over(acT[:, bass.ds(c * 16 + g * 8 + h4 * 4, 4)], 4, P), ALU.subtract,
                               after=[w, *users("mx")])
                        ce = actf(CEX[:, hs, :], psum[bk][:, :].rearrange("p (h l) -> p h l", h=4), ACT.Exp,
                                  after=[m, *users("cex")])
                        prog.users[bk] = [ce]
                    m = ts(MX[:, :, :], MX[:, :, :], 0.0, ALU.min, after=[m])
                    e = actf(MX[:, :, :], MX[:, :, :], ACT.Exp, after=[m])
                    xdd = tt(by_head(XDD[:, :]), by_head(XDT[:, g * T:(g + 1) * T]),
                             over(endT[:, bass.ds(c * 16 + g * 8, 8)], 8, 64), ALU.mult, after=[xd, *users("xdd")])
                    cx = tt(CEX[:, :, :], CEX[:, :, :], cF[:, g:g + 1, ck].to_broadcast([P, 8, P]), ALU.mult, after=[ce])
                    m = tt(MX[:, :, :], MX[:, :, :], CBT[:, g:g + 1, :].to_broadcast([P, 8, P]), ALU.mult, after=[e, cb])
                    yield
                    ns = mm(psum[5][:, :], bT[:, g, :], XDD[:, :], True, True, last=True, after=[xdd, bt, *users(5)])
                    prog.users["xdd"] = [ns]
                    yield
                    for h in range(8):
                        hd = g * 8 + h
                        half = slice(64 * (h % 2), 64 * (h % 2) + 64)
                        o = psum[7][half, (h // 2) * P:(h // 2 + 1) * P]
                        mm(o, PV[:, hd * 64:(hd + 1) * 64], CEX[:, h, :], h < 2, False,
                           after=[cx, *users("pv"), *users(7)] if h == 0 else [])
                        w = mm(o, XDT[:, hd * 64:(hd + 1) * 64], MX[:, h, :], False, True,
                               after=[m] if h == 0 else [], last=h == 7)
                    prog.users["mx"] = prog.users["cex"] = [w]
                    pv = PV[:, g * T:(g + 1) * T]
                    m = tt(by_head(pv), by_head(pv), over(chT[:, bass.ds(c * 16 + g * 8, 8)], 8, 64), ALU.mult, after=[w])
                    m = tt(pv, pv, psum[5][:, :], ALU.add, after=[ns, m])
                    prog.users[5] = prog.users["pv"] = [m]
                    for j in range(4):
                        jj = g * 4 + j
                        m = stt(XS[:, jj, ck], xC[:, jj, :], lcol(L_SKIP, jj), psum[7][:, j * P:(j + 1) * P],
                                ALU.mult, ALU.add)
                    prog.users[7] = prog.users["xc"] = [m]
                prog.users["xdt"] = prog.users["bt"] = [w, ns]
                yield

            def pair_and_chunk(c):
                ssd = chunk(c)
                next(ssd)

                def queries(s):
                    b, o, m = dense(A_hi, A_lo, KD)
                    q = actf(qW[:, s, :], o, after=[m, *users(f"qw{s}")])
                    prog.users[b] = [q]
                    return q

                def gate_tile():
                    b = gbank()
                    o = psum[b][:, :]
                    product(o, A_hi, A_lo, KD, need=users(b), ks=range(0, 4), more=True)
                    yield
                    m = product(o, A_hi, A_lo, KD, ks=range(4, 8))
                    t_m = actf(SQ[:, 0, :], o, ACT.Tanh, scale=0.5, after=[m, *users("sq0")])
                    zs = stt(SQ[:, 1, :], SQ[:, 0, :], 1.0, o, ALU.add, ALU.mult, after=[t_m, *users("sq1")])
                    prog.users[b] = prog.users["sq0"] = [zs]
                    yield zs

                def gated(s, w, zs):
                    m = stt(row(ATT, c * 2 + s), psum[4][:, :], 0.5, SQ[:, 1, :], ALU.mult, ALU.mult, after=[w, zs])
                    prog.users[4] = prog.users["sq1"] = [m]
                    prog.users[f"qw{s}"] = [w]

                q0 = queries(0)
                next(ssd)
                h0 = window_head(c, 0, 0, q0)
                next(h0)
                q1 = queries(1)
                h1 = window_head(c, 0, 1, q0)
                next(h1)
                next(ssd)
                next(h0)
                z = gate_tile()
                next(z)
                w = next(h0)
                next(ssd)
                next(h1)
                zs = next(z)
                h2 = window_head(c, 1, 0, q1)
                next(h2)
                w = next(h1)
                gated(0, w, zs)
                next(ssd)
                next(ssd)
                h3 = window_head(c, 1, 1, q1)
                next(h2)
                next(h3)
                z = gate_tile()
                next(z)
                next(ssd)
                next(h2)
                zs = next(z)
                next(h3)
                next(ssd)
                gated(1, next(h3), zs)

            prog.loop(NT, pair_and_chunk)
            fence()

            add = None
            for j in range(KD):
                b, o, gate_m = dense(A_hi, A_lo, KD)
                if add:
                    sq = add()
                if j == 4:
                    spread0 = norm_scale(1, [sq], EPS2, scale=1.0 / 512)
                if j == 6:
                    r0 = spread0()
                t_m = actf(ACV[:, j % 2, :], o, ACT.Tanh, scale=0.5, after=[gate_m, *users(f"a{j % 2}")])
                zs = stt(TCV[:, j % 2, :], ACV[:, j % 2, :], 1.0, o, ALU.add, ALU.mult, after=[t_m])
                prog.users[b] = [zs]
                y = XS[:, j, :]
                y_m = stt(y, y, 0.5, TCV[:, j % 2, :], ALU.mult, ALU.mult, after=[zs])
                prog.users[f"a{j % 2}"] = [y_m]
                add = square_sum(j % 4, 4, y, [y_m])
            out_hi, out_lo = (lambda k: OH[:, k, :]), (lambda k: OL[:, k, :])
            omark = [[split(out_hi(k), out_lo(k), ATT[:, k, :], 1.0, [gate_m])] for k in range(KD)]

            def gain(k, slot, r):
                y = XS[:, k, :]
                m = stt(y, y, lcol(L_NORM, k), RSTD[:, slot, :], ALU.mult, ALU.mult, after=[r])
                omark.append([split(out_hi(KD + k), out_lo(KD + k), y, 1.0, [m])])
                return m

            banks = [gbank(), gbank()]
            o = [psum[b][:, :] for b in banks]
            product(o[0], out_hi, out_lo, 2 * KD, need=users(banks[0]), ks=range(KD), marks=omark)
            sq = add()
            spread1 = norm_scale(0, [sq], EPS2, scale=1.0 / 512)
            for k in range(4):
                m = gain(k, 1, r0)
            prog.users["rstd1"] = [m]
            product(o[1], out_hi, out_lo, 2 * KD, need=users(banks[1]), ks=range(KD))
            r1 = spread1()
            for k in range(4, KD):
                m = gain(k, 0, r1)
            prog.users["rstd0"] = [m]
            tail = [product(o[i], out_hi, out_lo, 2 * KD, ks=range(KD, 2 * KD), marks=omark) for i in range(2)]

            def add_mean(j, m):
                return mm(psum[6][:, :], CON[:, C_ONE:C_ONE + P], X[:, j, :], j == 0, j == KD - 1, last=True,
                          after=[m, *(users(6) if j == 0 else [])])

            zm = []
            for j in range(KD):
                b, oj, m = (banks[j], o[j], tail[j]) if j < 2 else dense(out_hi, out_lo, 2 * KD)
                if j > 2:
                    add_mean(j - 3, zm[j - 3])
                zm.append(stt(X[:, j, :], X[:, j, :], ALPHA, oj, ALU.mult, ALU.add, after=[m]))
                prog.users[b] = [zm[-1]]
            for _ in range((units_before - prog.fixed["blocks"] // BLOCKS) % RING):
                now = prog.mark(UNC)
                pe.wait(now, Mark(s_split, now.value + 1, now.steps))
                UNC.value += 1
                if not prog.dry:
                    PE.sem_inc(UNC.sem, 1)
                prog.fixed["blocks"] += BLOCKS
            for j in range(KD - 3, KD):
                w = add_mean(j, zm[j])
            mean = RSTD[:, 0, :]
            mn = actf(mean, psum[6][:, :], scale=1.0 / D, after=[w, *users("rstd0")])
            prog.users[6] = [mn]
            for j in range(KD):
                m = tt(X[:, j, :], X[:, j, :], mean, ALU.subtract, after=[mn])
                sq = square_sum(j, KD, X[:, j, :], [m])()
            prog.users["rstd0"] = [m]
            r = norm_scale(1, [sq], EPS2)()
            for j in range(KD):
                m = tt(X[:, j, :], X[:, j, :], RSTD[:, 1, :], ALU.mult, after=[r])
                x_m = actf(X[:, j, :], X[:, j, :], ACT.Identity, scale=lcol(L_LNG, j), bias=lcol(L_LNB, j), after=[m])
                prog.users[f"x{j}"] = [x_m]
                prog.users[f"in{j}"] = [split(A_hi(j), A_lo(j), X[:, j, :], 1.0, [x_m])]
            prog.users["rstd1"] = [m]
            prog.users["lp"] = [x_m]
            prog.fixed["tiles"] += prog.fixed["tiles"] % 2

        prog.loop(2 if stop is None else 1, layer)
        for j in range(KD):
            act.wait(*users(f"x{j}"))
            nc.scalar.dma_start(out[:, j, :], X[:, j, :]).then_inc(s_out, 16)
        nc.scalar.wait_ge(s_out, 16 * KD)
        assert stop is not None or UNC.value - RING in range(n_units - RING, n_units + 1), (UNC.value, n_units)


def _tiles(w, group=P):
    k, n = w.shape
    return [[w[a:a + P, c:c + P] for a in range(0, k, P)] for c in range(0, n, P)]


def _units(blocks):
    res = []
    for a in range(0, len(blocks), BLOCKS):
        u = np.zeros((P, BLOCKS, P), np.float32)
        for j, b in enumerate(blocks[a:a + BLOCKS]):
            u[:b.shape[0], j, :b.shape[1]] = b
        res.append(u.reshape(P, BLOCKS * P))
    return res


PAIRS = [(8 * t + j, 8 * t + 4 + j) for j in range(4) for t in range(2)]
HEADS = [h for pair in PAIRS for h in pair]


def _stream(w):
    s = []
    win = w["w_in"]
    c = np.cumsum([0, 512, 1024, 128, 128, 256, 64, 4, 1024, 1024])
    cut = lambda m, a, b: m[:, a:b]
    pool, q, k, v, qi, kiw, gp, ga = (cut(win, c[0], c[1]), cut(win, c[1], c[2]), cut(win, c[2], c[3]),
                                     cut(win, c[3], c[4]), cut(win, c[4], c[5]), cut(win, c[5], c[7]),
                                     cut(win, c[7], c[8]), cut(win, c[8], c[9]))
    flat = lambda t: [b for col in t for b in col]
    add = lambda t: s.extend(_units(flat(t)))
    each = lambda t: [s.extend(_units(col)) for col in t]
    add_group = lambda t: s.extend(_units([col[k] for k in range(KD) for col in t]))
    for part in (k, v, kiw, qi, pool):
        each(_tiles(part))
    s.extend(_units([w["pool_w"][g] for g in range(4)]))
    add(_tiles(w["w_proj_pool"]))
    tq, tg = _tiles(q), _tiles(gp)
    for i in range(4):
        each([tq[2 * i], tq[2 * i + 1], tg[2 * i], tg[2 * i + 1]])
    ta, tb = _tiles(ga), _tiles(w["w_proj_attn"])
    for i in range(8):
        each([ta[i], tb[i]])
    each(_tiles(w["w_out"]))
    kv = w["w_kv_mem"]
    each(_tiles(kv[:, :512]))
    vm = kv[:, 512:].reshape(4, 2, P, T)
    for u in range(4):
        s.append(np.ascontiguousarray(vm[u].transpose(1, 0, 2)).reshape(P, 2 * T))
    each(_tiles(w["w_q_mem"]))
    add(_tiles(w["w_o_mem"]))
    tg, tu = _tiles(w["w_gate_up"][:, :D_FF]), _tiles(w["w_gate_up"][:, D_FF:])
    for i in range(KF):
        each([tg[i], tu[i]])
    each(_tiles(w["w_down"]))
    first = len(s)
    for L in range(2):
        wi, wo = w["w_in_2"][L], w["w_out_2"][L]
        c = np.cumsum([0, 1024, 256, 256, 1024, 1024, 1536, 16])
        q, k, v, za, zs, xbc, dt = (wi[:, c[j]:c[j + 1]] for j in range(7))
        heads = lambda m: m.reshape(D, 16, 64)[:, HEADS, :].reshape(D, D)
        tx = _tiles(xbc)
        add_group(tx[:4])
        each(_tiles(dt))
        each(tx[4:])
        each(_tiles(k))
        each(_tiles(v))
        tq, tz = _tiles(heads(q)), _tiles(heads(za))
        for i in range(8):
            each([tq[i]])
            if i % 2:
                each([tz[i - 1], tz[i]])
        each(_tiles(zs))
        wa = wo[:D].reshape(16, 64, D)[HEADS].reshape(D, D)
        ta, ts = _tiles(wa), _tiles(wo[D:])
        each([ta[0], ta[1], ts[0], ts[1]])
        each([a + b for a, b in zip(ta[2:], ts[2:])])
        while (len(s) - first) % RING:
            s.append(np.zeros((P, BLOCKS * P), np.float32))
    while len(s) % RING:
        s.append(np.zeros((P, BLOCKS * P), np.float32))
    return np.stack(s)


def _constants():
    import math
    con = np.zeros((P, C_N), np.float32)
    i, j = np.arange(P)[:, None], np.arange(P)[None, :]
    con[:, C_ID:C_ID + P] = i == j
    con[:, C_ONE:C_ONE + P] = 1.0
    con[:, C_CAUS:C_CAUS + P] = np.where(j > i, NEG, 0.0)
    con[:, C_TRIL:C_TRIL + P] = i <= j
    d = i - np.arange(256)[None, :] + P
    con[:, C_DIST:C_DIST + 256] = np.where((d >= 0) & (d < P), d, 1e30)
    con[:, C_DIST + 256:C_DIST + 384] = con[:, C_DIST + 128:C_DIST + 256]
    dist = 255 - np.arange(384)
    n = np.maximum(dist, 0)
    large = 16 + (np.log(np.maximum(n, 1).astype(np.float32) / np.float32(16)) / np.float32(math.log(8))
                  * np.float32(16)).astype(np.int32)
    bucket = np.where(n < 16, n, np.minimum(large, 31))
    hot = (np.arange(32)[:, None] == bucket[None, :]).astype(np.float32)
    hot[31] -= 1.0
    con[:32, C_HOT:C_HOT + 384] = hot
    for g, win in enumerate(POOL_WINDOWS):
        con[:, C_INV + 16 * g:C_INV + 16 * g + 16] = 1.0 / np.minimum(np.arange(1, 17), win)
    slope = np.exp2(-8.0 * (np.array(HEADS) + 1) / 16)
    con[:, C_SLOPE:C_SLOPE + 16] = -8.0 * slope
    return con


def _params(w):
    par = np.zeros((P, Q_N), np.float32)
    for c, name in ((Q_MIXPRE, "norm_mix_pre"), (Q_MIXPOST, "norm_mix_post"), (Q_MEMPRE, "norm_mem_pre"),
                    (Q_MEMKV, "norm_mem_kv"), (Q_MEMPOST, "norm_mem_post"), (Q_FFNPRE, "norm_ffn_pre"),
                    (Q_FFNPOST, "norm_ffn_post")):
        par[:, c:c + 8] = w[name].reshape(8, P).T
    par[:, Q_PSCALE:Q_PSCALE + 4] = w["pool_scale"].reshape(4, P).T
    par[:32, Q_TAB:Q_TAB + 8] = w["rel_bias_table"]
    lp = np.zeros((P, 2, L_N), np.float32)
    for L in range(2):
        lp[:, L, L_CW:L_CW + 48] = w["conv_w_2"][L].T.reshape(12, P, 4).transpose(1, 0, 2).reshape(P, 48)
        lp[:, L, L_CB:L_CB + 12] = w["conv_b_2"][L].reshape(12, P).T
        lp[:, L, L_SKIP:L_SKIP + 8] = np.repeat(w["d_skip_2"][L], 64).reshape(8, P).T
        lp[:, L, L_NORM:L_NORM + 8] = w["ssm_norm_w_2"][L].reshape(8, P).T
        lp[:, L, L_LNG:L_LNG + 8] = w["ln_g_2"][L].reshape(8, P).T
        lp[:, L, L_LNB:L_LNB + 8] = w["ln_b_2"][L].reshape(8, P).T
        lp[:, L, L_SINK:L_SINK + 16] = w["sinks_2"][L][HEADS][None, :]
        lp[:16, L, L_DTB] = w["dt_bias_2"][L]
        lp[:16, L, L_ALOG] = w["a_log_2"][L]
    return par, lp


STOP = None


def kernel(**inputs):
    import concourse.bacc as bacc
    from concourse.bass_utils import run_bass_kernel_spmd as run_spmd

    w = {k: np.asarray(v) for k, v in inputs.items()}
    feature_major = lambda a: np.ascontiguousarray(a[0].T.reshape(KD, P, a.shape[1]).transpose(1, 0, 2))
    par, lpar = _params(w)
    arrays = {"ws": _stream(w), "x": feature_major(w["x"]), "mem": feature_major(w["mem"]), "con": _constants(),
              "par": par, "lpar": lpar}
    nc = bacc.Bacc("TRN2", target_bir_lowering=False, num_devices=1)
    ins = {n: nc.dram_tensor(f"{n}_dram", a.shape, F32, kind="ExternalInput").ap() for n, a in arrays.items()}
    ins["scratch"] = nc.dram_tensor("bias_rows", (8, P, 384), F32, kind="Internal").ap()
    out = nc.dram_tensor("out_dram", (P, KD, T), F32, kind="ExternalOutput").ap()
    build(nc, ins, out, {None: arrays["ws"].shape[0], 1: 140, 2: 200}[STOP], STOP)
    r = run_spmd(nc, [{f"{n}_dram": a for n, a in arrays.items()}], core_ids=[0])
    y = np.asarray(r.results[0]["out_dram"])
    return np.ascontiguousarray(y.transpose(1, 0, 2).reshape(D, T).T)[None]
```

```python
from contextlib import ExitStack

import numpy as np

import concourse.bass as bass
from concourse import mybir

F32 = mybir.dt.float32
F32R = mybir.dt.float32r
I32 = mybir.dt.int32
ALU = mybir.AluOpType
ACT = mybir.ActivationFunctionType
AX = mybir.AxisListType.X
ENG = mybir.EngineType

P = 128
T = 512
NT = T // P
D = 1024
KD = D // P
BLOCKS = 8
RING = 4
KB = 1024
EPS1 = 1e-6
EPS2 = 1e-5
NEG = -1e30
TAKEN = -3e38
TOPK = 128
ALPHA = 4.0 ** 0.25
POOL_WINDOWS = (2, 4, 8, 16)
D_FF = 2816
KF = D_FF // P

C_ID, C_ONE, C_CAUS, C_TRIL, C_DIST, C_HOT, C_INV, C_SLOPE = 0, 128, 256, 384, 512, 896, 1280, 1344
C_N = 1360
(Q_MIXPRE, Q_MIXPOST, Q_MEMPRE, Q_MEMKV, Q_MEMPOST, Q_FFNPRE, Q_FFNPOST, Q_PSCALE, Q_TAB) = \
    (0, 8, 16, 24, 32, 40, 48, 56, 60)
Q_N = 68
L_CW, L_CB, L_SKIP, L_NORM, L_LNG, L_LNB, L_SINK, L_DTB, L_ALOG, L_N = 0, 48, 60, 68, 76, 84, 92, 108, 109, 110


class Mark:

    def __init__(self, sem, value, steps=()):
        self.sem, self.value, self.steps = sem, value, steps


class Counter:
    def __init__(self, sem, value):
        self.sem, self.value = sem, value


class Program:

    def __init__(self, nc):
        self.nc = nc
        self.dry = False
        self.loops = []
        self.counters = {}
        self.users = {}
        self.fixed = {"blocks": 0, "tiles": 0}

    def counter(self, name, sem, value):
        self.counters[name] = Counter(sem, value)
        return self.counters[name]

    def mark(self, c):
        return Mark(c.sem, c.value, tuple((l, l.steps[c.sem.name]) for l in self.loops))

    def row(self, t, j):
        return t[:, bass.ds(j, 1), :].rearrange("p a t -> p (a t)")

    def loop(self, n, body):
        first = {k: c.value for k, c in self.counters.items()}
        held = {k: list(v) for k, v in self.users.items()}
        was = self.dry
        self.dry = True
        fixed = dict(self.fixed)
        body(0)
        self.dry = was
        loop = Loop(n)
        for k, c in self.counters.items():
            loop.steps[c.sem.name] = c.value - first[k]
        start = {c.sem.name: first[k] for k, c in self.counters.items()}
        last = self.users
        if not self.dry:
            for k, c in self.counters.items():
                c.value = first[k]
            self.users = {}
            for k, marks in last.items():
                back = [Mark(m.sem, m.value - loop.steps[m.sem.name],
                             m.steps + ((loop, loop.steps[m.sem.name]),))
                        for m in marks if m.value > start[m.sem.name]]
                self.users[k] = held.get(k, []) + back
            with self.nc.Fori(0, n, engines=(ENG.PE, ENG.Activation, ENG.DVE)) as i:
                loop.i = i
                self.loops.append(loop)
                self.fixed = fixed
                body(i)
                self.loops.pop()
        for k, marks in self.users.items():
            self.users[k] = [self.ended(m, loop, start, n) for m in marks]
        for k, c in self.counters.items():
            c.value = first[k] + n * loop.steps[c.sem.name]

    def ended(self, m, loop, start, n):
        steps = tuple(s for s in m.steps if s[0] is not loop)
        if m.value <= start[m.sem.name] and len(steps) == len(m.steps):
            return m
        return Mark(m.sem, m.value + (n - 1) * loop.steps[m.sem.name], steps)


class Loop:
    def __init__(self, n):
        self.n, self.i, self.steps = n, None, {}


class Queue:

    def __init__(self, prog, engine, counter, gate):
        self.p, self.e, self.c, self.gate_sem = prog, engine, counter, gate

    def wait(self, *marks):
        if self.p.dry:
            return
        latest = {}
        for m in marks:
            key = (m.sem.name, tuple((id(l), n) for l, n in m.steps if n))
            if key not in latest or latest[key].value < m.value:
                latest[key] = m
        for m in latest.values():
            value = m.value
            for loop, step in m.steps:
                if step:
                    value = loop.i * step + value
            self.e.wait_ge(m.sem, value)

    def gate(self):
        if not self.p.dry and self.p.loops:
            self.e.sem_inc(self.gate_sem, 1)

    def run(self, f, *args, after=(), count=None, quiet=False, gate=False, **kw):
        self.wait(*after)
        if gate and after:
            self.gate()
        c = count or self.c
        if not quiet:
            c.value += 1
        if self.p.dry:
            return self.p.mark(c)
        ins = f(*args, **kw)
        if not quiet:
            ins.then_inc(c.sem, 1)
            return self.p.mark(c)
        return None

    def done(self):
        return self.p.mark(self.c)


def build(nc, ins, out, n_units, stop=None):
    ctx = ExitStack()
    with ctx:
        sem = lambda n: ctx.enter_context(nc.semaphore(n))
        prog = Program(nc)
        users = lambda name: prog.users.get(name, [])

        base = (nc.sbuf_base + 63) // 64 * 64

        def at(name, kb, shape, dt=F32):
            size = 4 * int(np.prod(shape[1:]))
            assert base + kb * KB + size <= nc.sbuf_top, (name, kb, size)
            return nc.alloc_sbuf_tensor_at(name, shape, dt, offset=base + int(kb * KB))

        X = at("X", 0, [P, KD, T])
        RAW = at("RAW", 16, [P, RING, BLOCKS * P])
        WH = at("WH", 32, [P, RING, BLOCKS * P], F32R)
        WL = at("WL", 48, [P, RING, BLOCKS * P], F32R)
        AH = at("AH", 64, [P, KD, T], F32R)
        AL = at("AL", 80, [P, KD, T], F32R)
        SUMS = at("SUMS", 111.5 + 92.5, [P, T])
        SQ = at("SQ", 96, [P, 2, T])
        RSTD = at("RSTD", 100, [P, 2, T])
        CON = at("CON", 104, [P, C_N])
        PAR = at("PAR", 109.375, [P, Q_N])
        LPARS = at("LPARS", 109.75, [P, 2, L_N])
        LP = at("LP", 110.6875, [P, L_N])
        ST = at("ST", 111.125, [P, 64])
        ONES = at("ONES", 111.375, [P, 8])
        Z = 111.5
        con = lambda c, n: CON[:, c:c + n]
        IDENT = con(C_ID, P)

        psum = [ctx.enter_context(nc.psum_tensor(f"bank{b}", [P, T], F32)) for b in range(8)]

        PEC = prog.counter("pe", sem("s_pe"), 64)
        ACC = prog.counter("act", sem("s_act"), 64)
        DVC = prog.counter("dve", sem("s_dve"), 64)
        UNC = prog.counter("unit", sem("s_unit_read"), RING)
        s_split = sem("s_unit_split")
        s_hi = sem("s_unit_hi")
        s_raw = [sem(f"s_unit_loaded{j}") for j in range(RING)]
        s_ones = sem("s_ones")
        s_in = {n: sem(f"s_in_{n}") for n in ("con", "par", "lp", "mem", "row0", "row1", "strip")}
        s_x = [sem(f"s_in_x{k}") for k in range(KD)]
        s_out = sem("s_out")
        pe = Queue(prog, nc.tensor, PEC, sem("s_pe_gate"))
        act = Queue(prog, nc.scalar, ACC, sem("s_act_gate"))
        dve = Queue(prog, nc.vector, DVC, sem("s_dve_gate"))
        for q in (pe, act, dve):
            q.e.sem_inc(q.c.sem, 64)
        pe.e.sem_inc(UNC.sem, RING)
        loaded = lambda n, v=16: Mark(s_in[n], v)

        nc.scalar.dma_start(PAR[:, :], ins["par"]).then_inc(s_in["par"], 16)
        for k in range(KD):
            nc.scalar.dma_start(X[:, k, :], ins["x"][:, k, :]).then_inc(s_x[k], 16)
            if k == 0:
                nc.scalar.dma_start(CON[:, :], ins["con"]).then_inc(s_in["con"], 16)
        nc.scalar.dma_start(LPARS[:, :, :], ins["lpar"]).then_inc(s_in["lp"], 16)
        act.wait(loaded("par"))
        dve.wait(loaded("par"))
        pe.wait(loaded("con"))

        WS = ins["ws"]
        nc.gpsimd.memset(ONES[:, :], 1.0).then_inc(s_ones, 1)
        nc.gpsimd.wait_ge(s_ones, 1)
        nc.gpsimd.sem_inc(s_split, RING)
        with nc.sync.Fori(0, n_units // RING) as i:
            for j in range(RING):
                nc.sync.wait_ge(s_split, i * RING + (j + 1))
                nc.sync.dma_start(RAW[:, j, :], WS[i * RING + j]).then_inc(s_raw[j], 16)
        with nc.gpsimd.Fori(0, n_units // RING) as i:
            for j in range(RING):
                nc.gpsimd.wait_ge(s_raw[j], i * 16 + 16)
                nc.gpsimd.wait_ge(UNC.sem, i * RING + (j + 1))
                nc.gpsimd.tensor_tensor(WH[:, j, :], RAW[:, j, :], ONES[:, 0:1].to_broadcast([P, BLOCKS * P]),
                                        ALU.mult).then_inc(s_hi, 1)
                nc.gpsimd.wait_ge(s_hi, i * RING + (j + 1))
                nc.gpsimd.tensor_tensor(WL[:, j, :], RAW[:, j, :], WH[:, j, :].bitcast(F32),
                                        ALU.subtract).then_inc(s_split, 1)

        V, S, PE = nc.vector, nc.scalar, nc.tensor
        row = prog.row

        def tt(o, a, b, op, after=(), **k):
            return dve.run(V.tensor_tensor, o, a, b, op, after=after, **k)

        def ts(o, a, s1, op0, s2=None, op1=ALU.bypass, after=(), **k):
            return dve.run(V.tensor_scalar, o, a, s1, s2, op0, op1, after=after, **k)

        def stt(o, a, s, b, op0, op1, after=(), **k):
            return dve.run(V.scalar_tensor_tensor, after=after, out=o, in0=a, scalar=s, in1=b, op0=op0, op1=op1, **k)

        def vcopy(o, a, after=(), **k):
            return dve.run(V.tensor_copy, o, a, after=after, **k)

        def actf(o, a, f=ACT.Copy, after=(), **k):
            return act.run(S.activation, o, a, f, after=after, **k)

        def mm(o, l, r, start, stop, last=False, after=(), count=None, gate=False):
            return pe.run(PE.matmul, o, l, r, start=start, stop=stop, after=after, gate=gate, quiet=not last, count=count,
                          skip_group_check=True)

        def transpose(o, a, after=(), last=False):
            k = a.shape[0]
            return pe.run(PE.transpose, o, a, IDENT[0:k, 0:k], after=after, quiet=not last, gate=k < P)

        def split(hi, lo, src, scale, after):
            h = actf(hi, src, ACT.Copy, scale=scale, after=after)
            return stt(lo, src, scale, hi.bitcast(F32), ALU.mult, ALU.subtract, after=[h, *after])

        def fence():
            marks = [*(q.done() for q in (pe, act, dve)), prog.mark(UNC)]
            for q in (pe, act, dve):
                q.wait(*marks)
                q.gate()
            prog.users.clear()

        def product(o, hi, lo, nk, need=(), cols=P, more=False, marks=None, ks=None):
            pe.wait(*need)
            mark = None
            for k in ks or range(nk):
                pos = prog.fixed["blocks"]
                slot, b = pos // BLOCKS % RING, pos % BLOCKS
                if b == 0:
                    now = prog.mark(UNC)
                    pe.wait(Mark(s_split, now.value + 1, now.steps))
                if marks is not None:
                    pe.wait(*marks[k])
                w = slice(b * P, b * P + cols)
                end = b == BLOCKS - 1 or (k == nk - 1 and not more)
                mm(o, WH[:, slot, w], hi(k), k == 0, False)
                mm(o, WH[:, slot, w], lo(k), False, False)
                mark = mm(o, WL[:, slot, w], hi(k), False, k == nk - 1, last=end or k == nk - 1,
                          count=UNC if end else None)
                prog.fixed["blocks"] = (pos // BLOCKS + 1) * BLOCKS if end else pos + 1
            return mark

        def group(hi, lo, nk, n_tiles, ready, banks=(2, 3, 4, 5), between=None):
            outs = []
            for k in range(nk):
                marks = ready(k)
                for i in range(n_tiles):
                    o = psum[banks[i]][:, :]
                    m = product(o, hi, lo, nk, need=[*(marks if i == 0 else []), *(users(banks[i]) if k == 0 else [])],
                                more=True, ks=[k])
                    if between and i == 0:
                        between(k)
                    outs.append((banks[i], o, m))
            return outs[-n_tiles:]

        def gbank():
            prog.fixed["tiles"] += 1
            return prog.fixed["tiles"] % 2

        def dense(hi, lo, nk, need=(), n=T, cols=P, more=False, marks=None):
            b = gbank()
            o = psum[b][0:cols, 0:n]
            m = product(o, hi, lo, nk, need=[*need, *users(b)], cols=cols, more=more, marks=marks)
            return b, o, m

        A_hi = lambda k: AH[:, k, :]
        A_lo = lambda k: AL[:, k, :]

        def squares(n=KD, nt=NT, bank=7):
            w = nt * P
            made = {}

            def tile(k, src, after):
                if k > 1:
                    a = f"sq{(k - 1) % 2}"
                    made[0] = tt(SUMS[:, 0:w], SUMS[:, 0:w], SQ[:, (k - 1) % 2, 0:w], ALU.add, after=[made[0], made[k - 1]])
                    prog.users[a] = [made[0]]
                dst, a = (SQ[:, k % 2, 0:w], f"sq{k % 2}") if k else (SUMS[:, 0:w], "acc")
                made[k] = actf(dst, src, ACT.Square, after=[*after, *users(a)])

            def total():
                for part, (t, m) in enumerate(((SUMS, made[0]), (SQ[:, (n - 1) % 2, :], made[n - 1]))):
                    for q in range(nt):
                        r = mm(psum[bank][:, q:q + 1], t[:, q * P:(q + 1) * P], ONEC, part == 0 and q == 0, part == 1,
                               last=q == nt - 1, after=[m, *(users(bank) if part == 0 else [])] if q == 0 else [])
                prog.users["acc"] = prog.users[f"sq{(n - 1) % 2}"] = [r]
                return r
            return tile, total

        ONEC = CON[:, C_ONE:C_ONE + 1]

        def inverse_root(v, r, n, after):
            t = ST[:, 40:40 + n]
            m = ts(r.bitcast(I32), v.bitcast(I32), 1, ALU.logical_shift_right, after=after)
            m = ts(r.bitcast(I32), r.bitcast(I32), -1.0, ALU.mult, 1597463007.0, ALU.add, after=[m])
            for _ in range(3):
                m = tt(t, r, r, ALU.mult, after=[m])
                m = stt(t, t, -0.5, v, ALU.mult, ALU.mult, after=[m])
                m = stt(r, t, 1.5, r, ALU.add, ALU.mult, after=[m])
            return m

        def spread(slot, rs, after, nt=NT, bank=6):
            def finish():
                for q in range(nt):
                    w = mm(psum[bank][:, q * P:(q + 1) * P], rs[:, q:q + 1].to_broadcast([P, P]), IDENT, q == 0, True,
                           last=q == nt - 1, after=[*after, *users(bank)] if q == 0 else [])
                r = actf(RSTD[:, slot, 0:nt * P], psum[bank][:, 0:nt * P], ACT.Copy, after=[w, *users(f"rstd{slot}")])
                prog.users[bank] = [r]
                return r
            return finish

        def norm_scale(slot, after, eps, scale=1.0 / D, nt=NT, bank=7):
            v, r = ST[:, 32:32 + nt], ST[:, 36 + 8 * slot:36 + 8 * slot + nt]
            m = ts(v, psum[bank][:, 0:nt], scale, ALU.mult, eps, ALU.add, after=after)
            prog.users[bank] = [m]
            m = inverse_root(v, r, nt, [m])
            return spread(slot, r, [m], nt)

        def store_out(after):
            nc.scalar.wait_ge(after.sem, after.value)
            nc.scalar.dma_start(out, X[:, :, :]).then_inc(s_out, 16)
            nc.scalar.wait_ge(s_out, 16)

        col = lambda base_, k: PAR[:, base_ + k:base_ + k + 1]
        kT = at("kT", Z + 0, [P, T])
        vTM = at("vTM", Z + 2, [P, NT, P])
        MSK = at("MSK", Z + 4, [P, 1280])
        STRIP = at("STRIP", Z + 9, [P, 8, 256])
        G = at("G", Z + 17, [P, KD, T])
        BH = at("BH", Z + 33, [P, KD, T], F32R)
        BL = at("BL", Z + 49, [P, KD, T], F32R)
        vF = at("vF", Z + 65, [P, T])
        qI = at("qI", Z + 67, [P, 2, T])
        kI = at("kI", Z + 71, [P, T])
        SCs = {q: at(f"SC{q}", Z + a, [P, (q + 1) * P]) for q, a in ((1, 90), (2, 91), (3, 92.5))}
        RL = at("RL", Z + 75, [P, 2, T])
        wTM = at("wTM", Z + 79, [P, NT * 4])
        T8 = at("T8", Z + 79.25, [P, 8])
        UP = at("UP", Z + 80, [P, 3, T + 16])
        ROW = at("ROW", Z + 87, [P, 2, 384])
        qC = at("qC", Z + 65, [P, 2, T])
        PR = at("PR", Z + 69, [P, 2, 1536])
        PT = at("PT", Z + 81, [P, 2, 1280])
        mOFF = [256, 0, 384, 768]
        kOFF = [0, 512, 1024, 896]

        memX = at("memX", Z + 65, [P, KD, 256])
        MH = at("MH", Z + 33, [P, KD, 256], F32R)
        ML = at("ML", Z + 41, [P, KD, 256], F32R)
        kM = at("kM", Z + 0, [P, 4, 256])
        vM = at("vM", Z + 4, [P, 2, T])
        qM = at("qM", Z + 8, [P, 4, T])
        PM = at("PM", Z + 57, [P, 2, 4 * 256])
        PMT = at("PMT", Z + 65, [P, 2, 2 * T])
        MAH = at("MAH", Z + 73, [P, 4, T], F32R)
        MAL = at("MAL", Z + 81, [P, 4, T], F32R)
        NM = 256

        def x_group(update, gain):
            x = {0: update(0)}
            square, total = squares()

            def ready(k):
                h = actf(A_hi(k), X[:, k, :], ACT.Copy, scale=gain(k), after=x[k])
                if 0 < k < KD - 1:
                    x[k + 1] = update(k + 1)
                m = stt(A_lo(k), X[:, k, :], gain(k), A_hi(k).bitcast(F32), ALU.mult, ALU.subtract, after=[h, *x[k]])
                square(k, X[:, k, :], x[k])
                if k == 0:
                    x[1] = update(1)
                return [m]

            scale = {}

            def between(k):
                if k == KD - 1:
                    scale["finish"] = norm_scale(0, [total()], EPS1)

            tiles = group(A_hi, A_lo, KD, 4, ready, between=between)
            return tiles, scale["finish"]

        first, finish = x_group(lambda k: [Mark(s_x[k], 16)], lambda k: col(Q_MIXPRE, k))
        R0 = RSTD[:, 0, :]
        v_tile = dense(A_hi, A_lo, KD)
        rstd = finish()

        def scaled(dst, b, o, m, extra=()):
            r = tt(dst, o, R0[0:o.shape[0], :], ALU.mult, after=[m, rstd, *extra])
            prog.users[b] = [r]
            return r

        ki_w = scaled(kI[0:68, :], first[0][0], psum[first[0][0]][0:68, :], first[0][2])
        for j in range(2):
            qi_ready = scaled(qI[:, j, :], *first[1 + j])
        v_f = scaled(vF[:, :], *v_tile)
        scaled(kT[:, :], *first[3])
        for q in range(NT):
            w = pe.run(PE.transpose, psum[2][:, q * 4:q * 4 + 4], kI[64:68, q * P:(q + 1) * P],
                       IDENT[64:68, 64:68], after=[ki_w, *users(2)], quiet=q < NT - 1)
        w_ready = ts(wTM[:, :], psum[2][:, 0:16], 1.0 / 16, ALU.mult, after=[w])
        ki_ready = vcopy(kI[64:128, :], kI[0:64, :], after=[w])
        prog.users[2] = [w_ready]
        b, o, m = pool_tile = dense(A_hi, A_lo, KD)
        for q in range(NT):
            w = transpose(psum[5][:, q * P:(q + 1) * P], vF[:, q * P:(q + 1) * P], after=[v_f, *users(5)] if q == 0 else [],
                          last=q == NT - 1)
        v_ready = actf(vTM[:, :, :].rearrange("p a b -> p (a b)"), psum[5][:, :], after=[w])
        prog.users[5] = [v_ready]

        table = PAR[0:32, Q_TAB:Q_TAB + 8]
        SCR = ins["scratch"]

        def bias_rows(h0):
            for h in (h0, h0 + 1):
                s = h % 2
                w = mm(psum[4 + s][:, 0:384], table[:, h:h + 1].to_broadcast([32, P]), CON[0:32, C_HOT:C_HOT + 384],
                       True, True, last=True, after=users(4 + s))
                r = actf(ROW[:, s, :], psum[4 + s][:, 0:384], after=[w] + ([loaded(f"row{s}", 16 * (h // 2))] if h > 1 else []))
                prog.users[4 + s] = [r]
                act.wait(r)
                nc.scalar.dma_start(SCR[h], ROW[:, s, :]).then_inc(s_in[f"row{s}"], 16)

        vcopy(MSK[:, mOFF[0]:mOFF[0] + P], con(C_CAUS, P))

        def scores(q):
            keys = (q + 1) * P
            SC = SCs[q]
            acc = None
            for h in range(4):
                half = slice(64 * (h % 2), 64 * (h % 2) + 64)
                bk = 2 + h % 2
                w = mm(psum[bk][:, 0:keys], qI[half, h // 2, q * P:(q + 1) * P], kI[half, 0:keys], True, True,
                       last=True, after=[qi_ready, ki_ready, *users(bk)])
                r = actf(RL[:, h % 2, 0:keys], psum[bk][:, 0:keys], ACT.Relu, after=[w, *users(f"rl{h % 2}")])
                prog.users[bk] = [r]
                wh = wTM[:, q * 4 + h:q * 4 + h + 1]
                if h == 0:
                    acc = ts(SC[:, 0:keys], RL[:, 0, 0:keys], wh, ALU.mult, after=[r])
                else:
                    acc = stt(SC[:, 0:keys], RL[:, h % 2, 0:keys], wh, SC[:, 0:keys], ALU.mult, ALU.add, after=[r, acc])
                prog.users[f"rl{h % 2}"] = [acc]
            return tt(SC[:, keys - P:keys], SC[:, keys - P:keys], con(C_CAUS, P), ALU.add, after=[acc])

        def select(q, m):
            keys = (q + 1) * P
            SC = SCs[q]
            for _ in range(TOPK // 8):
                m = dve.run(V.max, T8[:, :], SC[:, 0:keys], after=[m])
                m = dve.run(V.match_replace, SC[:, 0:keys], T8[:, :], SC[:, 0:keys], TAKEN, after=[m])
                yield
            ts(MSK[:, mOFF[q]:mOFF[q] + keys], SC[:, 0:keys], -2e38, ALU.is_gt, NEG, ALU.mult, after=[m])

        sc1 = scores(1)
        um = dve.run(V.memset, UP[:, :, 0:16], 0.0)
        U, S0, S1 = (UP[:, j, :] for j in range(3))
        N0, N1 = 16, T + 16
        pooled = []
        for g, win in enumerate(POOL_WINDOWS):
            b, o, m = pool_tile
            m = scaled(U[:, N0:N1], b, o, m, [um])
            if g < 3:
                pool_tile = dense(A_hi, A_lo, KD)
            src, dst, step = U, S0, 1
            while step < win:
                m = tt(dst[:, N0:N1], src[:, N0:N1], src[:, N0 - step:N1 - step], ALU.add, after=[m])
                src, dst, step = dst, (S1 if dst is S0 else S0), step * 2
            inv = CON[:, C_INV + 16 * g:C_INV + 16 * g + 16]
            m1 = tt(dst[:, N0:N0 + 16], src[:, N0:N0 + 16], inv, ALU.mult, after=[m])
            m = stt(src[:, N0:N1], src[:, N0:N1], 1.0 / win, U[:, N0:N1], ALU.mult, ALU.subtract, after=[m1])
            m = tt(src[:, N0:N0 + 16], dst[:, N0:N0 + 16], U[:, N0:N0 + 16], ALU.subtract, after=[m])
            um = split(BH[:, g, :], BL[:, g, :], src[:, N0:N1], 1.0, [m])
            bias_rows(2 * g)
            pooled.append([um])
        act.wait(loaded("row0", 64), loaded("row1", 64))
        nc.scalar.dma_start(STRIP[:, :, :], SCR.rearrange("h p c -> h (p c)")[:, 127:127 + P * 383]
                            .rearrange("h (p c) -> p h c", c=383)[:, :, 0:256]).then_inc(s_in["strip"], 16)
        mixed = []
        for g in range(4):
            b, o, m = dense(lambda k: BH[:, g, :], lambda k: BL[:, g, :], 1, need=pooled[g], more=g < 3)
            r = split(BH[:, 4 + g, :], BL[:, 4 + g, :], o, col(Q_PSCALE, g), [m])
            prog.users[b] = [r]
            mixed.append([r])
        sc2, sc3 = scores(2), scores(3)
        g_made = []
        rounds = (r for q, m in ((1, sc1), (2, sc2), (3, sc3)) for r in select(q, m))

        def select_rounds(n):
            for _ in range(n):
                next(rounds, None)

        select_rounds(28)
        for j in range(KD):
            b, o, m = dense(lambda k: BH[:, 4 + k, :], lambda k: BL[:, 4 + k, :], 4, marks=mixed,
                            more=j % 2 == 0)
            g_made.append(actf(G[:, j, :], o, after=[m]))
            prog.users[b] = [g_made[-1]]
        def pool_gate(j):
            s = j % 2
            b, o, m = dense(A_hi, A_lo, KD)
            m = tt(SQ[:, s, :], o, R0, ALU.mult, after=[m, *users(f"sq{s}")])
            prog.users[b] = [m]
            m = actf(SQ[:, s, :], SQ[:, s, :], ACT.Tanh, scale=0.5, after=[m])
            m = stt(G[:, j, :], SQ[:, s, :], 1.0, G[:, j, :], ALU.add, ALU.mult, after=[m, g_made[j]])
            prog.users[f"sq{s}"] = [m]

        for j in range(KD):
            pool_gate(j)
            select_rounds(3)
        select_rounds(48)
        for q in (pe, act, dve):
            q.wait(loaded("strip"))
        fence()

        SCALE = 128.0 ** -0.5

        def query_tile(s):
            b, o, m = dense(A_hi, A_lo, KD)
            return scaled(qC[:, s, :], b, o, m, users(f"q{s}"))

        def head(h, s, q_ready):
            where = [(2, 0), (3, 0), (2, 128), (4, 0)]
            mx, den = ST[:, 4 * s:4 * s + 4], ST[:, 8 + 4 * s:12 + 4 * s]
            wrote = {}
            for q in (0, 2, 1, 3):
                bk, c = where[q]
                keys = (q + 1) * P
                wrote[bk] = mm(psum[bk][:, c:c + keys], qC[:, s, q * P:(q + 1) * P], kT[:, 0:keys], c == 0, True,
                               last=True, after=[q_ready, *users(bk)] if c == 0 else [])
            for bk, c, n in ((2, mOFF[0], T), (3, mOFF[1], 256), (4, mOFF[3], T)):
                m = stt(PR[:, s, c:c + n], psum[bk][:, 0:n], SCALE, MSK[:, c:c + n], ALU.mult, ALU.add,
                        after=[wrote[bk], *users(f"pr{s}")])
                prog.users[bk] = [m]
            near = PR[:, s, :].rearrange("p (a b) -> p a b", b=T)[:, :, 0:256]
            m = tt(near, near, STRIP[:, bass.ds(h, 1), :].to_broadcast([P, 3, 256]), ALU.add, after=[m])
            near = PR[:, s, mOFF[0]:mOFF[0] + P]
            m = tt(near, near, row(STRIP, h)[:, P:256], ALU.add)
            for q in (1, 2, 3, 0):
                pr = PR[:, s, mOFF[q]:mOFF[q] + (q + 1) * P]
                m = dve.run(V.tensor_reduce, mx[:, q:q + 1], pr, AX, ALU.max, negate=True, after=[m] if q == 1 else [])
                e = actf(pr, pr, ACT.Exp, bias=mx[:, q:q + 1], accum_out=den[:, q:q + 1], after=[m])
            prog.users[f"q{s}"] = [wrote[4]]
            yield
            m = dve.run(V.reciprocal, den, den, after=[e])
            for q in range(NT):
                pr = PR[:, s, mOFF[q]:mOFF[q] + (q + 1) * P]
                m = ts(pr, pr, den[:, q:q + 1], ALU.mult, after=[m] if q == 0 else [])
            p_ready = m
            yield
            copies = []
            for bk, tiles in ((5, (0,)), (6, (1, 3)), (7, (2,))):
                c = 0
                for b in tiles:
                    for q in range(b, NT):
                        w = transpose(psum[bk][:, c:c + P], PR[:, s, mOFF[q] + b * P:mOFF[q] + (b + 1) * P],
                                      after=[p_ready, *users(bk)] if c == 0 else [], last=b == tiles[-1] and q == NT - 1)
                        c += P
                at_ = kOFF[tiles[0]]
                copy = vcopy if bk == 6 else actf
                copies.append(copy(PT[:, s, at_:at_ + c], psum[bk][:, 0:c], after=[w, *users(f"pt{s}")]))
                prog.users[bk] = [copies[-1]]
            prog.users[f"pr{s}"] = [w]
            yield
            bk = gbank()
            for b in range(NT):
                w = mm(psum[bk][:, b * P:T], vTM[:, b, :], PT[:, s, kOFF[b]:kOFF[b] + T - b * P], b == 0, b == NT - 1,
                       last=b == NT - 1, after=[*copies, *users(bk)] if b == 0 else [])
            prog.users[f"pt{s}"] = [w]
            r = split(row(BH, h), row(BL, h), psum[bk][:, :], 1.0, [w])
            prog.users[bk] = [r]
            prog.users["att_r"] = [r]
            yield

        def four_heads(i):
            h0, h1, h2, h3 = (lambda j=j: head(i * 4 + j, j % 2, query_tile(j % 2)) for j in range(4))
            h0 = h0()
            next(h0)
            h1 = h1()
            next(h0)
            next(h1)
            next(h0)
            h2 = h2()
            next(h1)
            next(h0)
            next(h2)
            next(h1)
            h3 = h3()
            next(h2)
            next(h3)
            next(h1)
            next(h2)
            next(h3)
            next(h2)
            next(h3)
            next(h3)

        prog.loop(2, four_heads)
        att_ready = users("att_r")
        B_hi = lambda k: BH[:, k, :]
        B_lo = lambda k: BL[:, k, :]

        def merge(j, after):
            b, o, m = dense(A_hi, A_lo, KD)
            m = tt(SQ[:, 0, :], o, R0, ALU.mult, after=[m, *users("sq0")])
            prog.users[b] = [m]
            t_m = actf(SQ[:, 0, :], SQ[:, 0, :], ACT.Tanh, scale=0.5, after=[m])
            b, o, m = dense(B_hi, B_lo, KD, need=after)
            m = stt(SQ[:, 0, :], SQ[:, 0, :], 1.0, o, ALU.add, ALU.mult, after=[m, t_m])
            prog.users[b] = [m]
            g = row(G, j)
            m = tt(g, g, SQ[:, 0, :], ALU.add, after=[m])
            prog.users["sq0"] = [m]
            prog.users["g"] = [m]

        def merge_two(i):
            merge(i * 2, att_ready)
            merge(i * 2 + 1, att_ready)

        act.wait(*att_ready, *users("pt0"), *users("pt1"))
        nc.scalar.dma_start(memX[:, :, :], ins["mem"]).then_inc(s_in["mem"], 16)
        prog.loop(4, merge_two)
        g_ready = users("g") + [prog.mark(UNC)]


        def project(hi, lo, nk, Y, marks=None, ready=None, more=False, between=None, then=None):
            tiles = group(hi, lo, nk, 4, ready, between=between) if ready else []
            if then:
                then()
            square, total = squares()
            for j in range(KD):
                b, o, m = tiles[j] if j < len(tiles) else dense(hi, lo, nk, marks=marks, more=more and j % 2 == 0)
                r = actf(Y[:, j, :], o, after=[m])
                prog.users[b] = [r]
                square(j, Y[:, j, :], [r])
            return total()

        def residual(Y, gain, rs):
            def update(k):
                m = stt(Y[:, k, :], Y[:, k, :], col(gain, k), RSTD[:, 1, :], ALU.mult, ALU.mult, after=[rs])
                m = tt(X[:, k, :], X[:, k, :], Y[:, k, :], ALU.add, after=[m])
                prog.users["rstd1"] = [m]
                return [m]
            return update

        def merged(k):
            return [split(A_hi(k), A_lo(k), G[:, k, :], 0.5, g_ready)]

        mm_marks = []

        def memory_rows():
            for k in range(KD):
                mm_marks.append([split(MH[:, k, :], ML[:, k, :], memX[:, k, :], col(Q_MEMKV, k), [loaded("mem"), *g_ready])])
            square, total = squares(nt=2)
            for k in range(KD):
                square(k, memX[:, k, :], [loaded("mem")])
            sq = total()
            v2 = ST[:, 32:34]
            m = ts(v2, psum[7][:, 0:2], 1.0 / D, ALU.mult, EPS1, ALU.add, after=[sq])
            prog.users[7] = [m]
            return inverse_root(v2, ST[:, 48:50], 2, [m])

        Y = G
        held = []
        sq = project(A_hi, A_lo, KD, Y, ready=merged, then=lambda: held.append(memory_rows()))
        mem_r = held[0]
        mem_finish = spread(0, ST[:, 48:50], [mem_r], nt=2)
        rs_finish = norm_scale(1, [sq], EPS1)
        mem_rstd = mem_finish()
        for j in range(4):
            b, o, m = dense(lambda k: MH[:, k, :], lambda k: ML[:, k, :], KD, n=NM, marks=mm_marks)
            if j == 1:
                rs = rs_finish()
            r = tt(kM[:, j, :], o, RSTD[:, 0, 0:NM], ALU.mult, after=[m, mem_rstd])
            prog.users[b] = [r]
        km_ready = r
        prog.users["rstd0"] = [r]
        first, finish = x_group(residual(Y, Q_MIXPOST, rs), lambda k: col(Q_MEMPRE, k))

        vb = [gbank(), gbank()]

        def value_unit(u):
            pos = prog.fixed["blocks"]
            slot = pos // BLOCKS % RING
            now = prog.mark(UNC)
            pe.wait(Mark(s_split, now.value + 1, now.steps))
            for kk in range(2):
                k = 2 * u + kk
                for t in range(2):
                    o = psum[vb[t]][:, :]
                    tk = slice(t * P, (t + 1) * P)
                    wsl = slice(kk * T, (kk + 1) * T)
                    if k == 0:
                        pe.wait(*users(vb[t]))
                    mm(o, MH[:, k, tk], WH[:, slot, wsl], k == 0, False)
                    mm(o, MH[:, k, tk], WL[:, slot, wsl], False, False)
                    last = kk == 1 and t == 1
                    m = mm(o, ML[:, k, tk], WH[:, slot, wsl], False, k == KD - 1, last=last, count=UNC if last else None)
            prog.fixed["blocks"] += BLOCKS
            return m

        MSCALE = 128.0 ** -0.5

        def mem_logits(h):
            s = h % 2
            mx, den = ST[:, 4 * s:4 * s + 4], ST[:, 8 + 4 * s:12 + 4 * s]
            for q in range(NT):
                bk = 2 + 2 * s + q // 2
                w = mm(psum[bk][:, (q % 2) * NM:(q % 2 + 1) * NM], qM[:, h, q * P:(q + 1) * P], kM[:, h, :],
                       q % 2 == 0, True, last=True, after=[*q_ready, km_ready, *users(bk)] if q % 2 == 0 else [])
                if q % 2:
                    m = dve.run(V.tensor_reduce, mx[:, q - 1:q + 1],
                                psum[bk][:, :].rearrange("p (a b) -> p a b", a=2), AX, ALU.max, negate=True, after=[w])
            m = ts(mx, mx, MSCALE, ALU.mult, after=[m])
            for q in range(NT):
                bk = 2 + 2 * s + q // 2
                e = actf(PM[:, s, q * NM:(q + 1) * NM], psum[bk][:, (q % 2) * NM:(q % 2 + 1) * NM], ACT.Exp, scale=MSCALE,
                         bias=mx[:, q:q + 1], accum_out=den[:, q:q + 1], after=[m, *users(f"pm{s}")])
            prog.users[2 + 2 * s] = prog.users[3 + 2 * s] = [e]
            return e

        def mem_values(h, e):
            s = h % 2
            den = ST[:, 8 + 4 * s:12 + 4 * s]
            m = dve.run(V.reciprocal, den, den, after=[e])
            for q in range(NT):
                pr = PM[:, s, q * NM:(q + 1) * NM]
                m = ts(pr, pr, den[:, q:q + 1], ALU.mult, after=[m])
            yield
            done = []
            for b in range(2):
                for q in range(NT):
                    w = transpose(psum[b][:, q * P:(q + 1) * P], PM[:, s, q * NM + b * P:q * NM + (b + 1) * P],
                                  after=[m, *users(b)] if q == 0 else [], last=q == NT - 1)
                c = (actf, vcopy)[b](PMT[:, s, b * T:(b + 1) * T], psum[b][:, :], after=[w, *users(f"pmt{s}")])
                prog.users[b] = [c]
                done.append(c)
            prog.users[f"pm{s}"] = [w]
            yield
            for b in range(2):
                w = mm(psum[6][:, :], vM[:, b, h * P:(h + 1) * P], PMT[:, s, b * T:(b + 1) * T], b == 0, b == 1,
                       last=b == 1, after=[*done, vm_ready, *users(6)] if b == 0 else [])
            prog.users[f"pmt{s}"] = [w]
            r = split(MAH[:, h, :], MAL[:, h, :], psum[6][:, :], 1.0, [w])
            prog.users[6] = [r]
            yield [r]

        value_unit(0)
        rstd = finish()
        q_ready = [scaled(qM[:, h, :], *first[h], users("qm")) for h in range(4)]
        prog.users["rstd0"] = [q_ready[-1]]
        value_unit(1)
        probs = [mem_logits(0)]
        value_unit(2)
        probs.append(mem_logits(1))
        m = value_unit(3)
        for t in range(2):
            vm_ready = ts(vM[:, t, :], psum[vb[t]][:, :], ST[:, 48 + t:49 + t], ALU.mult, after=[m, mem_r])
            prog.users[vb[t]] = [vm_ready]
        heads = [mem_values(h, probs[h]) for h in range(2)]
        mem_marks = {}

        def step(h):
            mem_marks[h] = next(heads[h])

        step(0)
        step(0)
        probs.append(mem_logits(2))
        step(1)
        step(0)
        step(1)
        probs.append(mem_logits(3))
        heads += [mem_values(h, probs[h]) for h in (2, 3)]
        step(2)
        step(1)
        step(2)

        def mem_head(k):
            for h in {0: (3,), 1: (2,), 2: (3,), 3: (3,)}[k]:
                step(h)
            return mem_marks[k]

        sq = project(lambda k: MAH[:, k, :], lambda k: MAL[:, k, :], 4, Y, ready=mem_head, more=True)
        rs = norm_scale(1, [sq], EPS1)()

        DH = at("DH", Z + 0, [P, KF, T], F32R)
        DL = at("DL", Z + 44, [P, KF, T], F32R)
        HG = at("HG", Z + 88, [P, 2, T])

        def gate_up(j, s, gate, up):
            b, o, m = gate()
            m = tt(HG[:, s, :], o, R0, ALU.mult, after=[m, rstd, *users(f"hg{s}")])
            prog.users[b] = [m]
            prog.users[f"earlier{s}"] = [m]
            t_m = actf(SQ[:, s, :], HG[:, s, :], ACT.Tanh, scale=0.5, after=[m, *users(f"sq{s}")])
            yield
            m = stt(HG[:, s, :], SQ[:, s, :], 1.0, HG[:, s, :], ALU.add, ALU.mult, after=[t_m])
            prog.users[f"sq{s}"] = [m]
            m = tt(HG[:, s, :], HG[:, s, :], R0, ALU.mult, after=[m])
            b, o, m2 = up()
            m = tt(HG[:, s, :], o, HG[:, s, :], ALU.mult, after=[m, m2])
            prog.users[b] = [m]
            r = split(row(DH, j), row(DL, j), HG[:, s, :], 0.5, [m])
            prog.users[f"hg{s}"] = prog.users["d"] = [r]
            yield

        tile = lambda: dense(A_hi, A_lo, KD)

        def gate_up_two(i):
            for s in range(2):
                for _ in gate_up(i * 2 + 2 + s, s, tile, tile):
                    pass

        first, finish = x_group(residual(Y, Q_MEMPOST, rs), lambda k: col(Q_FFNPRE, k))
        rstd = finish()
        pair = [gate_up(s, s, lambda s=s: first[2 * s], lambda s=s: first[2 * s + 1]) for s in range(2)]
        for _ in range(2):
            for half in pair:
                next(half)
        prog.loop(KF // 2 - 1, gate_up_two)
        d_ready = users("d")
        YF = at("YF", 64, [P, KD, T])
        sq = project(lambda k: DH[:, k, :], lambda k: DL[:, k, :], KF, YF,
                     marks=[users("earlier0")] * (KF - 2) + [d_ready] * 2)
        rs = norm_scale(1, [sq], EPS1)()
        update = residual(YF, Q_FFNPOST, rs)
        for k in range(KD):
            prog.users[f"in{k}"] = [split(A_hi(k), A_lo(k), X[:, k, :], 1.0, update(k))]
        if stop == 1:
            fence()
            store_out(Mark(DVC.sem, DVC.value))
            return prog.fixed

        kW = at("kW", Z + 0, [P, 2, T])
        vW = at("vW", Z + 4, [P, NT, 256])
        ATT = at("ATT", Z + 8, [P, KD, T])
        XS = at("XS", Z + 24, [P, KD, T])
        OH = at("OH", 64, [P, 2 * KD, T], F32R)
        OL = at("OL", Z + 8, [P, 2 * KD, T], F32R)
        bF = at("bF", Z + 40, [P, 2, T])
        cF = at("cF", Z + 44, [P, 2, T])
        dtF = at("dtF", Z + 48, [P, T])
        acF = at("acF", Z + 50, [P, T])
        TM = at("TM", Z + 52, [P, 6, 64])
        dtT, acT, lastT, endT, chT = (TM[:, j, :] for j in range(5))
        PV = at("PV", Z + 53.5, [P, D])
        qW = at("qW", Z + 57.5, [P, 2, T])
        PWs = [at(f"PW{s}", Z + 61.5 + 3.5 * s, [P, 896]) for s in range(2)]
        PWTs = [at(f"PWT{s}", Z + (68.5, 91)[s], [P, 896]) for s in range(2)]
        ACH = at("ACH", 100, [16, T], F32R)
        ACL = at("ACL", 102, [16, T], F32R)
        ONEHOT = at("ONEHOT", 109.3125, [16, 16], F32R)
        XDD = at("XDD", Z + 48, [P, T])
        MX = at("MX", Z + 72, [P, 8, P])
        XDT = at("XDT", Z + 76, [P, D])
        CEX = at("CEX", Z + 80, [P, 8, P])
        xC = at("xC", Z + 84, [P, KD, P])
        bC = at("bC", Z + 88, [P, 2, P])
        CBT = at("CBT", Z + 89, [P, 2, P])
        bT = at("bT", Z + 90, [P, 2, P])
        ACV = at("ACV", Z + 57.5, [P, 2, T])
        TCV = at("TCV", Z + 61.5, [P, 2, T])
        vWF = at("vWF", Z + 65.5, [P, 2, T])
        DTW = at("DTW", Z + 72, [P, 4, T])
        lcol = lambda c, k=0: LP[:, c + k:c + k + 1]
        SINKB = at("SINKB", 111.4375, [P, 16])

        units_before = prog.fixed["blocks"] // BLOCKS

        def layer(L):
            m = vcopy(LP[:, :], row(LPARS, L), after=users("lp"))
            m = ts(LP[:, L_CW:L_CW + 60], LP[:, L_CW:L_CW + 60], 0.5, ALU.mult, after=[m])
            m = vcopy(SINKB[:, :], LP[:, L_SINK:L_SINK + 16], after=[m])
            m = ts(LP[:, L_SINK:L_SINK + 16], LP[:, L_SINK:L_SINK + 16], -8.0, ALU.mult, after=[m])
            lp_ready = m
            dve.run(V.memset, PV[:, :], 0.0)

            def conv(j, b, o, m):
                s = j % 2
                acc = ACV[:, s, :]
                m = actf(acc, o, ACT.Identity, scale=lcol(L_CW, 4 * j + 3), bias=lcol(L_CB, j),
                         after=[m, lp_ready, *users(f"acv{s}")])
                yield
                for tap in (2, 1, 0):
                    d = 3 - tap
                    m = stt(acc[:, d:T], o[:, 0:T - d], lcol(L_CW, 4 * j + tap), acc[:, d:T], ALU.mult, ALU.add, after=[m])
                prog.users[b] = [m]
                yield
                t_m = actf(TCV[:, s, :], acc, ACT.Tanh, after=[m])
                dst = XS[:, j, :] if j < 8 else (bF[:, j - 8, :] if j < 10 else cF[:, j - 10, :])
                prog.users[f"acv{s}"] = [stt(dst, TCV[:, s, :], 1.0, acc, ALU.add, ALU.mult, after=[t_m])]
                yield

            def decays(v, e1, u, t1, v_m):
                a16 = ST[0:16, 56:57]
                m = stt(e1, v, -1.0, v, ALU.mult, ALU.max, after=[v_m])
                e = actf(a16, LP[0:16, L_ALOG:L_ALOG + 1], ACT.Exp, after=[lp_ready])
                an = ts(a16, a16, -1.0, ALU.mult, after=[e])
                m = actf(e1, e1, ACT.Exp, scale=-1.0, after=[m])
                yield
                m = ts(u, e1, 1.0, ALU.add, after=[m])
                lg = actf(dtF[0:16, :], u, ACT.Ln, after=[m])
                yield
                m = ts(t1, u, -1.0, ALU.add, after=[m])
                m = tt(e1, e1, t1, ALU.subtract, after=[m])
                m = dve.run(V.reciprocal, u, u, after=[m, lg])
                m = tt(e1, e1, u, ALU.mult, after=[m])
                yield
                m = tt(e1, e1, dtF[0:16, :], ALU.add, after=[m])
                m = stt(dtF[0:16, :], v, 0.0, e1, ALU.max, ALU.add, after=[m])
                m = ts(v, dtF[0:16, :], a16, ALU.mult, after=[m, an])
                yield
                for c in range(NT):
                    cs = slice(c * P, (c + 1) * P)
                    m = dve.run(V.tensor_tensor_scan, acF[0:16, cs], ONES[0:16, 0:1].to_broadcast([16, P]), v[:, cs],
                                0.0, ALU.mult, ALU.add, after=[m])
                yield m

            first = group(A_hi, A_lo, KD, 4, lambda k: users(f"in{k}"))
            b, o, dt_m = dense(A_hi, A_lo, KD, cols=16)
            now = conv(0, *first[0])
            next(now)
            next(now)
            v, e1, u, t1 = (DTW[0:16, j, :] for j in range(4))
            v_m = ts(v, o, LP[0:16, L_DTB:L_DTB + 1], ALU.add, after=[dt_m])
            prog.users[b] = [v_m]
            for j in range(1, 12):
                if j == 4:
                    for i in range(2):
                        b, o, m = dense(A_hi, A_lo, KD)
                        prog.users[b] = [actf(kW[:, i, :], o, after=[m])]
                last, now = now, conv(j, *(first[j] if j < 4 else dense(A_hi, A_lo, KD)))
                next(now)
                next(now)
                next(last)
                if j == 4:
                    steps = decays(v, e1, u, t1, v_m)
                if 6 <= j < 11:
                    dt_ready = next(steps)
            next(now)

            for c in range(NT):
                cs = slice(c * P, (c + 1) * P)
                c16 = slice(16 * c, 16 * c + 16)
                w = transpose(psum[2][:, c16], dtF[0:16, cs], after=[dt_ready, *users(2)] if c == 0 else [])
                w = transpose(psum[2][:, 64 + 16 * c:80 + 16 * c], acF[0:16, cs])
                w = mm(psum[2][:, 128 + 16 * c:144 + 16 * c], acF[0:16, (c + 1) * P - 1:(c + 1) * P].to_broadcast([16, P]),
                       IDENT[0:16, 0:16], True, True, last=c == 3)
            r = vcopy(TM[:, 0:3, :], psum[2][:, 0:192].rearrange("p (a b) -> p a b", a=3), after=[w])
            prog.users[2] = [r]
            m = tt(endT, lastT, acT, ALU.subtract, after=[r])
            m = actf(endT, endT, ACT.Exp, after=[m])
            actf(chT, lastT, ACT.Exp, after=[r])
            split(ACH[:, :], ACL[:, :], acF[0:16, :], 1.0, [dt_ready])
            for j in range(2):
                b, o, m = dense(A_hi, A_lo, KD)
                r = actf(vWF[:, j, :], o, after=[m])
                prog.users[b] = [r]
                for q in range(NT):
                    w = transpose(psum[3 + j][:, q * P:(q + 1) * P], vWF[:, j, q * P:(q + 1) * P],
                                  after=[r, *users(3 + j)] if q == 0 else [], last=q == NT - 1)
                vw = vcopy(vW[:, :, j * P:(j + 1) * P], psum[3 + j][:, :].rearrange("p (a b) -> p a b", a=NT), after=[w])
                prog.users[3 + j] = [vw]
            fence()

            oW = [768, 0, 256, 512]
            DIST = CON[:, C_DIST:C_DIST + 384]

            def window_head(c, s, hh, q_ready):
                half = slice(64 * hh, 64 * hh + 64)
                PW, PWT = PWs[hh], PWTs[hh]
                hc = (c * 2 + s) * 2 + hh
                wrote = {}
                for q in (1, 2, 3, 0):
                    bk, at_ = 2 + oW[q] // T, oW[q] % T
                    n = 256 if q else P
                    wrote[bk] = mm(psum[bk][:, at_:at_ + n], qW[half, s, q * P:(q + 1) * P],
                                   kW[half, s, (q + 1) * P - n:(q + 1) * P], at_ == 0, True, last=q in (2, 0),
                                   after=[q_ready, *users(bk)] if at_ == 0 else [])
                sl = CON[:, bass.ds(hc + C_SLOPE, 1)]
                m = stt(PW[:, 0:512].rearrange("p (a b) -> p a b", a=2), DIST[:, 0:256].unsqueeze(1).to_broadcast([P, 2, 256]),
                        sl, psum[2][:, :].rearrange("p (a b) -> p a b", a=2), ALU.mult, ALU.add,
                        after=[wrote[2], *users(f"pw{hh}")])
                prog.users[2] = [m]
                m = stt(PW[:, 512:896], DIST, sl, psum[3][:, 0:384], ALU.mult, ALU.add, after=[wrote[3]])
                prog.users[3] = [m]
                z = 12 * hh
                mx, den, es = ST[:, z:z + 4], ST[:, z + 4:z + 8], ST[:, z + 8:z + 12]
                pw = [PW[:, oW[q]:oW[q] + (256 if q else P)] for q in range(NT)]
                m = dve.run(V.tensor_reduce, mx[:, 1:4], PW[:, 0:768].rearrange("p (a b) -> p a b", a=3), AX, ALU.max,
                            negate=True, after=[m])
                m = dve.run(V.tensor_reduce, mx[:, 0:1], pw[0], AX, ALU.max, negate=True)
                m = ts(mx, mx, LP[:, bass.ds(hc + L_SINK, 1)], ALU.min, 0.125, ALU.mult, after=[m])
                for q in range(NT):
                    actf(pw[q], pw[q], ACT.Exp, scale=0.125, bias=mx[:, q:q + 1], accum_out=den[:, q:q + 1],
                         after=[m] if q == 0 else [])
                e = actf(es, mx, ACT.Exp, bias=SINKB[:, bass.ds(hc, 1)])
                yield
                m = tt(den, den, es, ALU.add, after=[e])
                m = dve.run(V.reciprocal, den, den, after=[m])
                for q in range(NT):
                    m = ts(pw[q], pw[q], den[:, q:q + 1], ALU.mult, after=[m] if q == 0 else [])
                yield
                for b in range(NT):
                    bk, c0 = 2 + b // 2, (b % 2) * 256
                    cur = pw[b][:, 128:256] if b else pw[0]
                    w = transpose(psum[bk][:, c0:c0 + P], cur, after=[m, *users(bk)] if c0 == 0 else [], last=b == 3)
                    if b < 3:
                        w = transpose(psum[bk][:, c0 + P:c0 + 256], pw[b + 1][:, 0:P], last=b == 1)
                    if b == 1:
                        t0 = actf(PWT[:, 0:512], psum[2][:, :], after=[w, *users(f"pwt{hh}")])
                t1 = actf(PWT[:, 512:896], psum[3][:, 0:384], after=[w, *users(f"pwt{hh}")])
                prog.users[2], prog.users[3] = [t0], [t1]
                prog.users[f"pw{hh}"] = [w]
                yield
                o = psum[4]
                val = lambda b: vW[:, b, s * P + 64 * hh:s * P + 64 * hh + 64]
                for q in range(NT):
                    w = mm(o[half, q * P:(q + 1) * P], val(q), PWT[:, q * 256:q * 256 + P], q == 0, q == 0,
                           after=[t0, t1, *users(4)] if q == 0 else [])
                    if q:
                        w = mm(o[half, q * P:(q + 1) * P], val(q - 1), PWT[:, (q - 1) * 256 + P:q * 256],
                               False, True, last=q == NT - 1)
                prog.users[f"pwt{hh}"] = [w]
                yield w

            cum = con(C_TRIL, P)

            def chunk(c):
                ck = bass.ts(c, P)
                by_head = lambda t: t.rearrange("p (h d) -> p h d", d=64)
                over = lambda t, n, w: t.unsqueeze(2).to_broadcast([P, n, w])
                b_m = actf(bC[:, :, :], bF[:, :, ck], after=users("bc"))
                x_m = actf(xC[:, :, :], XS[:, :, ck], after=users("xc"))
                yield
                for g in range(2):
                    w = mm(psum[7][:, g * P:(g + 1) * P], bC[:, g, :], cF[:, g, ck], g == 0, True,
                           after=[b_m, *users(7)] if g == 0 else [])
                for g in range(2):
                    w = transpose(psum[7][:, (2 + g) * P:(3 + g) * P], bC[:, g, :], last=g == 1)
                prog.users["bc"] = [w]
                cb = tt(CBT[:, :, :], psum[7][:, 0:256].rearrange("p (g l) -> p g l", g=2),
                        cum.unsqueeze(1).to_broadcast([P, 2, P]), ALU.mult, after=[w])
                bt = actf(bT[:, :, :].rearrange("p a b -> p (a b)"), psum[7][:, 256:512], after=[w, cb, *users("bt")])
                prog.users[7] = [bt]
                for g in range(2):
                    bk = 5 + g
                    for j in range(4):
                        w = transpose(psum[bk][:, j * P:(j + 1) * P], xC[:, g * 4 + j, :],
                                      after=[x_m, *users(bk)] if j == 0 else [], last=j == 3)
                    xd = tt(by_head(XDT[:, g * T:(g + 1) * T]), by_head(psum[bk][:, :]),
                            over(dtT[:, bass.ds(c * 16 + g * 8, 8)], 8, 64), ALU.mult, after=[w, *users("xdt")])
                    prog.users[bk] = [xd]
                for g in range(2):
                    yield
                    xdd = tt(by_head(XDD[:, :]), by_head(XDT[:, g * T:(g + 1) * T]),
                             over(endT[:, bass.ds(c * 16 + g * 8, 8)], 8, 64), ALU.mult, after=[xd, *users("xdd")])
                    for h4 in range(2):
                        bk = 5 + h4
                        hs = slice(h4 * 4, h4 * 4 + 4)
                        for h in range(4):
                            hd = g * 8 + h4 * 4 + h
                            pick = ONEHOT[:, hd:hd + 1].to_broadcast([16, P])
                            mm(psum[bk][:, h * P:(h + 1) * P], pick, ACH[:, ck], h == 0, False,
                               after=users(bk) if h == 0 else [], gate=True)
                            w = mm(psum[bk][:, h * P:(h + 1) * P], pick, ACL[:, ck], False, True, last=h == 3)
                        m = tt(MX[:, hs, :], psum[bk][:, :].rearrange("p (h l) -> p h l", h=4),
                               over(acT[:, bass.ds(c * 16 + g * 8 + h4 * 4, 4)], 4, P), ALU.subtract,
                               after=[w, *users("mx")])
                        ce = actf(CEX[:, hs, :], psum[bk][:, :].rearrange("p (h l) -> p h l", h=4), ACT.Exp,
                                  after=[m, *users("cex")])
                        prog.users[bk] = [ce]
                    m = ts(MX[:, :, :], MX[:, :, :], 0.0, ALU.min, after=[m])
                    e = actf(MX[:, :, :], MX[:, :, :], ACT.Exp, after=[m])
                    cx = tt(CEX[:, :, :], CEX[:, :, :], cF[:, g:g + 1, ck].to_broadcast([P, 8, P]), ALU.mult, after=[ce])
                    m = tt(MX[:, :, :], MX[:, :, :], CBT[:, g:g + 1, :].to_broadcast([P, 8, P]), ALU.mult, after=[e, cb])
                    yield
                    ns = mm(psum[5][:, :], bT[:, g, :], XDD[:, :], True, True, last=True, after=[xdd, bt, *users(5)])
                    prog.users["xdd"] = [ns]
                    yield
                    for h in range(8):
                        hd = g * 8 + h
                        half = slice(64 * (h % 2), 64 * (h % 2) + 64)
                        o = psum[7][half, (h // 2) * P:(h // 2 + 1) * P]
                        mm(o, PV[:, hd * 64:(hd + 1) * 64], CEX[:, h, :], h < 2, False,
                           after=[cx, *users("pv"), *users(7)] if h == 0 else [])
                        w = mm(o, XDT[:, hd * 64:(hd + 1) * 64], MX[:, h, :], False, True,
                               after=[m] if h == 0 else [], last=h == 7)
                    prog.users["mx"] = prog.users["cex"] = [w]
                    pv = PV[:, g * T:(g + 1) * T]
                    m = tt(by_head(pv), by_head(pv), over(chT[:, bass.ds(c * 16 + g * 8, 8)], 8, 64), ALU.mult, after=[w])
                    m = tt(pv, pv, psum[5][:, :], ALU.add, after=[ns, m])
                    prog.users[5] = prog.users["pv"] = [m]
                    for j in range(4):
                        jj = g * 4 + j
                        m = stt(XS[:, jj, ck], xC[:, jj, :], lcol(L_SKIP, jj), psum[7][:, j * P:(j + 1) * P],
                                ALU.mult, ALU.add)
                    prog.users[7] = prog.users["xc"] = [m]
                prog.users["xdt"] = prog.users["bt"] = [w, ns]
                yield

            def pair_and_chunk(c):
                ssd = chunk(c)
                next(ssd)

                def queries(s):
                    b, o, m = dense(A_hi, A_lo, KD)
                    q = actf(qW[:, s, :], o, after=[m, *users(f"qw{s}")])
                    prog.users[b] = [q]
                    return q

                def gate_tile():
                    b = gbank()
                    o = psum[b][:, :]
                    product(o, A_hi, A_lo, KD, need=users(b), ks=range(0, 4), more=True)
                    yield
                    m = product(o, A_hi, A_lo, KD, ks=range(4, 8))
                    t_m = actf(SQ[:, 0, :], o, ACT.Tanh, scale=0.5, after=[m, *users("sq0")])
                    zs = stt(SQ[:, 1, :], SQ[:, 0, :], 1.0, o, ALU.add, ALU.mult, after=[t_m, *users("sq1")])
                    prog.users[b] = prog.users["sq0"] = [zs]
                    yield zs

                def gated(s, w, zs):
                    m = stt(row(ATT, c * 2 + s), psum[4][:, :], 0.5, SQ[:, 1, :], ALU.mult, ALU.mult, after=[w, zs])
                    prog.users[4] = prog.users["sq1"] = [m]
                    prog.users[f"qw{s}"] = [w]

                q0 = queries(0)
                next(ssd)
                h0 = window_head(c, 0, 0, q0)
                next(h0)
                q1 = queries(1)
                h1 = window_head(c, 0, 1, q0)
                next(h1)
                next(h0)
                next(ssd)
                z = gate_tile()
                next(z)
                next(h1)
                next(h0)
                next(ssd)
                zs = next(z)
                next(h0)
                next(h1)
                h2 = window_head(c, 1, 0, q1)
                next(h2)
                next(ssd)
                gated(0, next(h1), zs)
                h3 = window_head(c, 1, 1, q1)
                next(h3)
                next(h2)
                next(ssd)
                z = gate_tile()
                next(z)
                next(h3)
                next(h2)
                next(ssd)
                zs = next(z)
                next(h2)
                next(h3)
                next(ssd)
                gated(1, next(h3), zs)

            prog.loop(NT, pair_and_chunk)
            fence()

            out_hi, out_lo = (lambda k: OH[:, k, :]), (lambda k: OL[:, k, :])

            def gain(k, slot, r):
                y = XS[:, k, :]
                return stt(y, y, lcol(L_NORM, k), RSTD[:, slot, :], ALU.mult, ALU.mult, after=[r])

            def split_out(k):
                return [split(out_hi(k), out_lo(k), ATT[:, k, :], 1.0, [gate_m])]

            square, total = squares(4)
            for j in range(KD):
                b, o, gate_m = dense(A_hi, A_lo, KD)
                if j == 4:
                    spread0 = norm_scale(1, [total()], EPS2, scale=1.0 / 512)
                    square, total = squares(4)
                if j == 6:
                    r0 = spread0()
                if j == KD - 1:
                    omark = [split_out(k) for k in range(2)]
                t_m = actf(ACV[:, j % 2, :], o, ACT.Tanh, scale=0.5, after=[gate_m, *users(f"a{j % 2}")])
                zs = stt(TCV[:, j % 2, :], ACV[:, j % 2, :], 1.0, o, ALU.add, ALU.mult, after=[t_m])
                prog.users[b] = [zs]
                y = XS[:, j, :]
                y_m = stt(y, y, 0.5, TCV[:, j % 2, :], ALU.mult, ALU.mult, after=[zs])
                prog.users[f"a{j % 2}"] = [y_m]
                square(j % 4, y, [y_m])
                if j == 6:
                    gain_m = [gain(k, 1, r0) for k in range(4)]
                    prog.users["rstd1"] = [gain_m[-1]]
            omark += [split_out(k) for k in range(2, KD)]

            def split_ssm(k, m):
                omark.append([split(out_hi(KD + k), out_lo(KD + k), XS[:, k, :], 1.0, [m, gate_m])])

            banks = [gbank(), gbank()]
            o = [psum[b][:, :] for b in banks]

            def two_tiles(ks):
                for k in ks:
                    for i in range(2):
                        m = product(o[i], out_hi, out_lo, 2 * KD, need=users(banks[i]) if k == 0 else (), ks=[k],
                                    marks=omark, more=True)
                        if k == 2 * KD - 1:
                            tail.append(m)

            tail = []
            two_tiles(range(3))
            spread1 = norm_scale(0, [total()], EPS2, scale=1.0 / 512)
            for k in range(4):
                split_ssm(k, gain_m[k])
            two_tiles(range(3, KD))
            r1 = spread1()
            for k in range(4, KD):
                m = gain(k, 0, r1)
                split_ssm(k, m)
            prog.users["rstd0"] = [m]
            two_tiles(range(KD, 2 * KD))

            for j in range(KD):
                b, oj, m = (banks[j], o[j], tail[j]) if j < 2 else dense(out_hi, out_lo, 2 * KD)
                z_m = stt(X[:, j, :], X[:, j, :], ALPHA, oj, ALU.mult, ALU.add, after=[m])
                prog.users[b] = [z_m]
                if 0 < j < KD - 1:
                    sum_m = tt(SUMS[:, :], X[:, 0, :] if j == 1 else SUMS[:, :], X[:, j, :], ALU.add,
                               after=[z_m, *users("acc")])
                    prog.users["acc"] = [sum_m]
            for _ in range((units_before - prog.fixed["blocks"] // BLOCKS) % RING):
                now = prog.mark(UNC)
                pe.wait(now, Mark(s_split, now.value + 1, now.steps))
                UNC.value += 1
                if not prog.dry:
                    PE.sem_inc(UNC.sem, 1)
                prog.fixed["blocks"] += BLOCKS
            mm(psum[6][:, :], CON[:, C_ONE:C_ONE + P], SUMS[:, :], True, False, after=[sum_m, *users(6)])
            w = mm(psum[6][:, :], CON[:, C_ONE:C_ONE + P], X[:, KD - 1, :], False, True, last=True, after=[z_m])
            prog.users["acc"] = [w]
            mean = RSTD[:, 0, :]
            mn = actf(mean, psum[6][:, :], scale=1.0 / D, after=[w, *users("rstd0")])
            prog.users[6] = [mn]
            square, total = squares()
            for j in range(KD):
                m = tt(X[:, j, :], X[:, j, :], mean, ALU.subtract, after=[mn])
                square(j, X[:, j, :], [m])
            prog.users["rstd0"] = [m]
            r = norm_scale(1, [total()], EPS2)()
            for j in range(KD):
                m = tt(X[:, j, :], X[:, j, :], RSTD[:, 1, :], ALU.mult, after=[r])
                x_m = ts(X[:, j, :], X[:, j, :], lcol(L_LNG, j), ALU.mult, lcol(L_LNB, j), ALU.add, after=[m])
                prog.users[f"x{j}"] = [x_m]
                prog.users[f"in{j}"] = [split(A_hi(j), A_lo(j), X[:, j, :], 1.0, [x_m])]
            prog.users["rstd1"] = [m]
            prog.users["lp"] = [x_m]
            prog.fixed["tiles"] += prog.fixed["tiles"] % 2

        dve.wait(loaded("lp"))
        vcopy(ONEHOT[:, :], IDENT[0:16, 0:16])
        prog.loop(2 if stop is None else 1, layer)
        for j in range(KD):
            act.wait(*users(f"x{j}"))
            nc.scalar.dma_start(out[:, j, :], X[:, j, :]).then_inc(s_out, 16)
        nc.scalar.wait_ge(s_out, 16 * KD)
        assert stop is not None or UNC.value - RING in range(n_units - RING, n_units + 1), (UNC.value, n_units)


def _tiles(w, group=P):
    k, n = w.shape
    return [[w[a:a + P, c:c + P] for a in range(0, k, P)] for c in range(0, n, P)]


def _units(blocks):
    res = []
    for a in range(0, len(blocks), BLOCKS):
        u = np.zeros((P, BLOCKS, P), np.float32)
        for j, b in enumerate(blocks[a:a + BLOCKS]):
            u[:b.shape[0], j, :b.shape[1]] = b
        res.append(u.reshape(P, BLOCKS * P))
    return res


PAIRS = [(8 * t + j, 8 * t + 4 + j) for j in range(4) for t in range(2)]
HEADS = [h for pair in PAIRS for h in pair]


def _stream(w):
    s = []
    win = w["w_in"]
    c = np.cumsum([0, 512, 1024, 128, 128, 256, 64, 4, 1024, 1024])
    cut = lambda m, a, b: m[:, a:b]
    pool, q, k, v, qi, kiw, gp, ga = (cut(win, c[0], c[1]), cut(win, c[1], c[2]), cut(win, c[2], c[3]),
                                     cut(win, c[3], c[4]), cut(win, c[4], c[5]), cut(win, c[5], c[7]),
                                     cut(win, c[7], c[8]), cut(win, c[8], c[9]))
    flat = lambda t: [b for col in t for b in col]
    add = lambda t: s.extend(_units(flat(t)))
    each = lambda t: [s.extend(_units(col)) for col in t]
    add_group = lambda t: s.extend(_units([col[k] for k in range(len(t[0])) for col in t]))
    add_group(_tiles(np.concatenate([kiw, np.zeros((D, P - 68), np.float32), qi, k], axis=1)))
    each(_tiles(v))
    each(_tiles(pool))
    s.extend(_units([w["pool_w"][g] for g in range(4)]))
    add(_tiles(w["w_proj_pool"]))
    each(_tiles(gp))
    each(_tiles(q))
    ta, tb = _tiles(ga), _tiles(w["w_proj_attn"])
    for i in range(8):
        each([ta[i], tb[i]])
    to = _tiles(w["w_out"])
    add_group(to[:4])
    each(to[4:])
    kv = w["w_kv_mem"]
    each(_tiles(kv[:, :512]))
    add_group(_tiles(w["w_q_mem"]))
    vm = kv[:, 512:].reshape(4, 2, P, T)
    for u in range(4):
        s.append(np.ascontiguousarray(vm[u].transpose(1, 0, 2)).reshape(P, 2 * T))
    to = _tiles(w["w_o_mem"])
    add_group(to[:4])
    add(to[4:])
    tg, tu = _tiles(w["w_gate_up"][:, :D_FF]), _tiles(w["w_gate_up"][:, D_FF:])
    add_group([tg[0], tu[0], tg[1], tu[1]])
    for i in range(2, KF):
        each([tg[i], tu[i]])
    each(_tiles(w["w_down"]))
    first = len(s)
    for L in range(2):
        wi, wo = w["w_in_2"][L], w["w_out_2"][L]
        c = np.cumsum([0, 1024, 256, 256, 1024, 1024, 1536, 16])
        q, k, v, za, zs, xbc, dt = (wi[:, c[j]:c[j + 1]] for j in range(7))
        heads = lambda m: m.reshape(D, 16, 64)[:, HEADS, :].reshape(D, D)
        tx = _tiles(xbc)
        add_group(tx[:4])
        each(_tiles(dt))
        each(_tiles(k))
        each(tx[4:])
        each(_tiles(v))
        tq, tz = _tiles(heads(q)), _tiles(heads(za))
        for i in range(8):
            each([tq[i]])
            if i % 2:
                each([tz[i - 1], tz[i]])
        each(_tiles(zs))
        wa = wo[:D].reshape(16, 64, D)[HEADS].reshape(D, D)
        ta, ts = _tiles(wa), _tiles(wo[D:])
        add_group([ta[0], ta[1]])
        add_group([ts[0], ts[1]])
        each([a + b for a, b in zip(ta[2:], ts[2:])])
        while (len(s) - first) % RING:
            s.append(np.zeros((P, BLOCKS * P), np.float32))
    while len(s) % RING:
        s.append(np.zeros((P, BLOCKS * P), np.float32))
    return np.stack(s)


def _constants():
    import math
    con = np.zeros((P, C_N), np.float32)
    i, j = np.arange(P)[:, None], np.arange(P)[None, :]
    con[:, C_ID:C_ID + P] = i == j
    con[:, C_ONE:C_ONE + P] = 1.0
    con[:, C_CAUS:C_CAUS + P] = np.where(j > i, NEG, 0.0)
    con[:, C_TRIL:C_TRIL + P] = i <= j
    d = i - np.arange(256)[None, :] + P
    con[:, C_DIST:C_DIST + 256] = np.where((d >= 0) & (d < P), d, 1e30)
    con[:, C_DIST + 256:C_DIST + 384] = con[:, C_DIST + 128:C_DIST + 256]
    dist = 255 - np.arange(384)
    n = np.maximum(dist, 0)
    large = 16 + (np.log(np.maximum(n, 1).astype(np.float32) / np.float32(16)) / np.float32(math.log(8))
                  * np.float32(16)).astype(np.int32)
    bucket = np.where(n < 16, n, np.minimum(large, 31))
    hot = (np.arange(32)[:, None] == bucket[None, :]).astype(np.float32)
    hot[31] -= 1.0
    con[:32, C_HOT:C_HOT + 384] = hot
    for g, win in enumerate(POOL_WINDOWS):
        con[:, C_INV + 16 * g:C_INV + 16 * g + 16] = 1.0 / np.minimum(np.arange(1, 17), win)
    slope = np.exp2(-8.0 * (np.array(HEADS) + 1) / 16)
    con[:, C_SLOPE:C_SLOPE + 16] = -8.0 * slope
    return con


def _params(w):
    par = np.zeros((P, Q_N), np.float32)
    for c, name in ((Q_MIXPRE, "norm_mix_pre"), (Q_MIXPOST, "norm_mix_post"), (Q_MEMPRE, "norm_mem_pre"),
                    (Q_MEMKV, "norm_mem_kv"), (Q_MEMPOST, "norm_mem_post"), (Q_FFNPRE, "norm_ffn_pre"),
                    (Q_FFNPOST, "norm_ffn_post")):
        par[:, c:c + 8] = w[name].reshape(8, P).T
    par[:, Q_PSCALE:Q_PSCALE + 4] = w["pool_scale"].reshape(4, P).T
    par[:32, Q_TAB:Q_TAB + 8] = w["rel_bias_table"]
    lp = np.zeros((P, 2, L_N), np.float32)
    for L in range(2):
        lp[:, L, L_CW:L_CW + 48] = w["conv_w_2"][L].T.reshape(12, P, 4).transpose(1, 0, 2).reshape(P, 48)
        lp[:, L, L_CB:L_CB + 12] = w["conv_b_2"][L].reshape(12, P).T
        lp[:, L, L_SKIP:L_SKIP + 8] = np.repeat(w["d_skip_2"][L], 64).reshape(8, P).T
        lp[:, L, L_NORM:L_NORM + 8] = w["ssm_norm_w_2"][L].reshape(8, P).T
        lp[:, L, L_LNG:L_LNG + 8] = w["ln_g_2"][L].reshape(8, P).T
        lp[:, L, L_LNB:L_LNB + 8] = w["ln_b_2"][L].reshape(8, P).T
        lp[:, L, L_SINK:L_SINK + 16] = w["sinks_2"][L][HEADS][None, :]
        lp[:16, L, L_DTB] = w["dt_bias_2"][L]
        lp[:16, L, L_ALOG] = w["a_log_2"][L]
    return par, lp


STOP = None


def kernel(**inputs):
    import concourse.bacc as bacc
    from concourse.bass_utils import run_bass_kernel_spmd as run_spmd

    w = {k: np.asarray(v) for k, v in inputs.items()}
    feature_major = lambda a: np.ascontiguousarray(a[0].T.reshape(KD, P, a.shape[1]).transpose(1, 0, 2))
    par, lpar = _params(w)
    arrays = {"ws": _stream(w), "x": feature_major(w["x"]), "mem": feature_major(w["mem"]), "con": _constants(),
              "par": par, "lpar": lpar}
    nc = bacc.Bacc("TRN2", target_bir_lowering=False, num_devices=1)
    ins = {n: nc.dram_tensor(f"{n}_dram", a.shape, F32, kind="ExternalInput").ap() for n, a in arrays.items()}
    ins["scratch"] = nc.dram_tensor("bias_rows", (8, P, 384), F32, kind="Internal").ap()
    out = nc.dram_tensor("out_dram", (P, KD, T), F32, kind="ExternalOutput").ap()
    build(nc, ins, out, {None: arrays["ws"].shape[0], 1: 140, 2: 200}[STOP], STOP)
    r = run_spmd(nc, [{f"{n}_dram": a for n, a in arrays.items()}], core_ids=[0])
    y = np.asarray(r.results[0]["out_dram"])
    return np.ascontiguousarray(y.transpose(1, 0, 2).reshape(D, T).T)[None]
```
